# Optimizing a Trainium2 kernel written in Bass

```python
import jax, jax.numpy as jnp
from jax import lax
import numpy as np

D_MODEL = 1024
BATCH = 1
SEQ = 256
DEPTH = 2

N_META = 16
EPS = 1e-6
SSD_D_INNER = 2 * D_MODEL
SSD_HEAD_DIM = 64
SSD_HEADS = SSD_D_INNER // SSD_HEAD_DIM
SSD_GROUPS = 8
SSD_HPG = SSD_HEADS // SSD_GROUPS
SSD_STATE = 128
SSD_CONV = 4
SSD_CHUNK = 128
SSD_CONV_DIM = SSD_D_INNER + 2 * SSD_GROUPS * SSD_STATE
SSD_IN_DIM = SSD_D_INNER + SSD_CONV_DIM + SSD_HEADS
MLA_HEADS = 16
MLA_NOPE = 64
MLA_ROPE = 32
MLA_V = 64
MLA_QK = MLA_NOPE + MLA_ROPE
MLA_Q_RANK = 384
MLA_KV_RANK = 256
MLA_IN_DIM = MLA_Q_RANK + MLA_KV_RANK + MLA_ROPE
ROPE_THETA = 10000.0
ATTN_BLOCK = 128
D_FF = 4 * D_MODEL
N_SSD_LAYERS = (DEPTH + 1) // 2
N_MLA_LAYERS = DEPTH // 2


def rms_norm(x, gain):
    xf = x.astype(jnp.float32)
    y = xf * lax.rsqrt(jnp.mean(xf * xf, axis=-1, keepdims=True) + EPS)
    return (y * gain.astype(jnp.float32)).astype(x.dtype)

def causal_depthwise_conv(u, w, b):
    out = lax.conv_general_dilated(
        u, w[:, None, :].astype(u.dtype), window_strides=(1,),
        padding=[(SSD_CONV - 1, 0)], dimension_numbers=('NWC', 'WIO', 'NWC'),
        feature_group_count=u.shape[-1])
    return out + b.astype(u.dtype)

def ssd_mixer(h, w_in, conv_w, conv_b, dt_bias, a_log, d_skip, norm_g, w_out):
    f32 = jnp.float32
    bsz, L, _ = h.shape
    zxbcdt = h @ w_in
    z, xbc, dt = jnp.split(zxbcdt, [SSD_D_INNER, SSD_D_INNER + SSD_CONV_DIM], axis=-1)
    xbc = jax.nn.silu(causal_depthwise_conv(xbc, conv_w, conv_b))
    xs, b_in, c_in = jnp.split(xbc, [SSD_D_INNER, SSD_D_INNER + SSD_GROUPS * SSD_STATE], axis=-1)
    dt = jax.nn.softplus(dt.astype(f32) + dt_bias.astype(f32))
    a = -jnp.exp(a_log.astype(f32))

    pad = (-L) % SSD_CHUNK
    n_chunks = (L + pad) // SSD_CHUNK

    def front_pad(t):
        return jnp.pad(t.astype(f32), [(0, 0), (pad, 0)] + [(0, 0)] * (t.ndim - 2))

    x_c = front_pad(xs).reshape(bsz, n_chunks, SSD_CHUNK, SSD_GROUPS, SSD_HPG, SSD_HEAD_DIM)
    b_c = front_pad(b_in).reshape(bsz, n_chunks, SSD_CHUNK, SSD_GROUPS, SSD_STATE)
    c_c = front_pad(c_in).reshape(bsz, n_chunks, SSD_CHUNK, SSD_GROUPS, SSD_STATE)
    dt_c = front_pad(dt).reshape(bsz, n_chunks, SSD_CHUNK, SSD_GROUPS, SSD_HPG)
    xdt = x_c * dt_c[..., None]
    a_dt = (dt_c * a.reshape(SSD_GROUPS, SSD_HPG)).transpose(0, 1, 3, 4, 2)
    a_cs = jnp.cumsum(a_dt, axis=-1)

    idx = jnp.arange(SSD_CHUNK)
    causal = idx[:, None] >= idx[None, :]
    decay = jnp.exp(jnp.where(causal, a_cs[..., :, None] - a_cs[..., None, :], -jnp.inf))
    cb = jnp.einsum('bclgn,bcsgn->bcgls', c_c, b_c)
    y_diag = jnp.einsum('bcgjls,bcsgjp->bclgjp', cb[:, :, :, None] * decay, xdt)

    decay_to_end = jnp.exp(a_cs[..., -1:] - a_cs).transpose(0, 1, 4, 2, 3)
    states = jnp.einsum('bclgn,bclgjp->bcgjpn', b_c, xdt * decay_to_end[..., None])
    chunk_decay = jnp.exp(a_cs[..., -1])

    def step(carry, inp):
        st, dec = inp
        return carry * dec[..., None, None] + st, carry

    init = jnp.zeros((bsz, SSD_GROUPS, SSD_HPG, SSD_HEAD_DIM, SSD_STATE), f32)
    _, prev = lax.scan(step, init, (jnp.moveaxis(states, 1, 0), jnp.moveaxis(chunk_decay, 1, 0)))
    prev = jnp.moveaxis(prev, 0, 1)
    decay_from_start = jnp.exp(a_cs).transpose(0, 1, 4, 2, 3)
    y_off = jnp.einsum('bclgn,bcgjpn->bclgjp', c_c, prev) * decay_from_start[..., None]

    y = (y_diag + y_off).reshape(bsz, n_chunks * SSD_CHUNK, SSD_D_INNER)[:, pad:]
    y = y + xs.astype(f32) * jnp.repeat(d_skip.astype(f32), SSD_HEAD_DIM)
    g = (y * jax.nn.silu(z.astype(f32))).reshape(bsz, L, SSD_GROUPS, SSD_D_INNER // SSD_GROUPS)
    g = g * lax.rsqrt(jnp.mean(g * g, axis=-1, keepdims=True) + EPS)
    g = g.reshape(bsz, L, SSD_D_INNER) * norm_g.astype(f32)
    return g.astype(h.dtype) @ w_out

def rope_tables(L):
    inv = 1.0 / (ROPE_THETA ** (jnp.arange(0, MLA_ROPE, 2, dtype=jnp.float32) / MLA_ROPE))
    ang = jnp.arange(L, dtype=jnp.float32)[:, None] * inv[None, :]
    return jnp.cos(ang)[None, :, None, :], jnp.sin(ang)[None, :, None, :]

def apply_rope(t, cos, sin):
    t1, t2 = jnp.split(t, 2, axis=-1)
    cos = cos.astype(t.dtype)
    sin = sin.astype(t.dtype)
    return jnp.concatenate([t1 * cos - t2 * sin, t1 * sin + t2 * cos], axis=-1)

def mla_mixer(h, w_in, q_a_g, w_q_b, kv_a_g, w_kv_b, q_norm_g, k_norm_g, w_out):
    bsz, L, _ = h.shape
    q_lat, kv_lat, k_pe = jnp.split(h @ w_in, [MLA_Q_RANK, MLA_Q_RANK + MLA_KV_RANK], axis=-1)
    q = (rms_norm(q_lat, q_a_g) @ w_q_b).reshape(bsz, L, MLA_HEADS, MLA_QK)
    kv = (rms_norm(kv_lat, kv_a_g) @ w_kv_b).reshape(bsz, L, MLA_HEADS, MLA_NOPE + MLA_V)
    k_nope, v = jnp.split(kv, [MLA_NOPE], axis=-1)
    k = jnp.concatenate(
        [k_nope, jnp.broadcast_to(k_pe[:, :, None, :], (bsz, L, MLA_HEADS, MLA_ROPE))], axis=-1)
    q = rms_norm(q, q_norm_g)
    k = rms_norm(k, k_norm_g)
    cos, sin = rope_tables(L)
    q = jnp.concatenate([q[..., :MLA_NOPE], apply_rope(q[..., MLA_NOPE:], cos, sin)], axis=-1)
    k = jnp.concatenate([k[..., :MLA_NOPE], apply_rope(k[..., MLA_NOPE:], cos, sin)], axis=-1)
    scale = MLA_QK ** -0.5

    blocks = [(0, N_META)] + [(s, min(s + ATTN_BLOCK, L)) for s in range(N_META, L, ATTN_BLOCK)]
    outs = []
    for s, e in blocks:
        sc = jnp.einsum('bqhd,bkhd->bhqk', q[:, s:e], k[:, :e]).astype(jnp.float32) * scale
        mask = jnp.arange(e)[None, :] <= jnp.arange(s, e)[:, None]
        p = jax.nn.softmax(jnp.where(mask, sc, -jnp.inf), axis=-1).astype(v.dtype)
        outs.append(jnp.einsum('bhqk,bkhd->bqhd', p, v[:, :e]))
    o = jnp.concatenate(outs, axis=1).reshape(bsz, L, MLA_HEADS * MLA_V)
    return o @ w_out

def sqrelu_mlp(h, w_up, w_down):
    return jnp.square(jax.nn.relu(h @ w_up)) @ w_down

def first_inputs(seed: int = 0) -> dict:
    key = jax.random.key(seed)
    ks = jax.random.split(key, 24)
    f32 = jnp.float32

    def nrm(k, shape, fan_in):
        return jax.random.normal(k, shape, f32) * (fan_in ** -0.5)

    def gain(k, shape):
        return 1.0 + 0.02 * jax.random.normal(k, shape, f32)

    ns, nm = N_SSD_LAYERS, N_MLA_LAYERS
    dt0 = jnp.exp(jax.random.uniform(ks[7], (ns, SSD_HEADS), f32, np.log(1e-3), np.log(1e-1)))
    return {
        "x": jax.random.normal(ks[0], (BATCH, SEQ, D_MODEL), f32),
        "meta_tokens": jax.random.normal(ks[1], (N_META, D_MODEL), f32),
        "ln_mix": gain(ks[2], (DEPTH, D_MODEL)),
        "ln_mlp": gain(ks[3], (DEPTH, D_MODEL)),
        "ssd_w_in": nrm(ks[4], (ns, D_MODEL, SSD_IN_DIM), D_MODEL),
        "ssd_conv_w": nrm(ks[5], (ns, SSD_CONV, SSD_CONV_DIM), SSD_CONV),
        "ssd_conv_b": 0.02 * jax.random.normal(ks[6], (ns, SSD_CONV_DIM), f32),
        "ssd_dt_bias": dt0 + jnp.log(-jnp.expm1(-dt0)),
        "ssd_a_log": jnp.log(jax.random.uniform(ks[8], (ns, SSD_HEADS), f32, 1.0, 16.0)),
        "ssd_d": 1.0 + 0.1 * jax.random.normal(ks[9], (ns, SSD_HEADS), f32),
        "ssd_norm": gain(ks[10], (ns, SSD_D_INNER)),
        "ssd_w_out": nrm(ks[11], (ns, SSD_D_INNER, D_MODEL), SSD_D_INNER),
        "mla_w_in": nrm(ks[12], (nm, D_MODEL, MLA_IN_DIM), D_MODEL),
        "mla_q_a_norm": gain(ks[13], (nm, MLA_Q_RANK)),
        "mla_w_q_b": nrm(ks[14], (nm, MLA_Q_RANK, MLA_HEADS * MLA_QK), MLA_Q_RANK),
        "mla_kv_a_norm": gain(ks[15], (nm, MLA_KV_RANK)),
        "mla_w_kv_b": nrm(ks[16], (nm, MLA_KV_RANK, MLA_HEADS * (MLA_NOPE + MLA_V)), MLA_KV_RANK),
        "mla_q_norm": gain(ks[17], (nm, MLA_QK)),
        "mla_k_norm": gain(ks[18], (nm, MLA_QK)),
        "mla_w_out": nrm(ks[19], (nm, MLA_HEADS * MLA_V, D_MODEL), MLA_HEADS * MLA_V),
        "mlp_w_up": nrm(ks[20], (DEPTH, D_MODEL, D_FF), D_MODEL),
        "mlp_w_down": nrm(ks[21], (DEPTH, D_FF, D_MODEL), D_FF),
    }

def first_block(x, meta_tokens, ln_mix, ln_mlp, ssd_w_in, ssd_conv_w, ssd_conv_b, ssd_dt_bias,
              ssd_a_log, ssd_d, ssd_norm, ssd_w_out, mla_w_in, mla_q_a_norm, mla_w_q_b,
              mla_kv_a_norm, mla_w_kv_b, mla_q_norm, mla_k_norm, mla_w_out, mlp_w_up, mlp_w_down):
    bsz = x.shape[0]
    meta = jnp.broadcast_to(meta_tokens[None].astype(x.dtype), (bsz, N_META, D_MODEL))
    h = jnp.concatenate([meta, x], axis=1)
    for i in range(DEPTH):
        j = i // 2
        hn = rms_norm(h, ln_mix[i])
        if i % 2 == 0:
            h = h + ssd_mixer(hn, ssd_w_in[j], ssd_conv_w[j], ssd_conv_b[j], ssd_dt_bias[j],
                              ssd_a_log[j], ssd_d[j], ssd_norm[j], ssd_w_out[j])
        else:
            h = h + mla_mixer(hn, mla_w_in[j], mla_q_a_norm[j], mla_w_q_b[j], mla_kv_a_norm[j],
                              mla_w_kv_b[j], mla_q_norm[j], mla_k_norm[j], mla_w_out[j])
        h = h + sqrelu_mlp(rms_norm(h, ln_mlp[i]), mlp_w_up[i], mlp_w_down[i])
    return h[:, N_META:]


DEPTH_2 = 1

GRID_W = 64
N_HEADS = 8
HEAD_DIM = 64
ATTN_WIDTH = N_HEADS * HEAD_DIM
CONV_WIDTH = D_MODEL // 2
CONV_K = 3
WIN_ROWS_MAX = 8
WIN_COLS = 16
Q_COL_BLOCK = 16
KEY_COL_SPAN = 32
D_FF_2 = 4 * D_MODEL
NEG_INF = -1e30
PROJ_SPLITS = [ATTN_WIDTH, ATTN_WIDTH, ATTN_WIDTH, CONV_WIDTH, CONV_WIDTH, CONV_WIDTH, D_MODEL]
PROJ_WIDTH = 3 * ATTN_WIDTH + 3 * CONV_WIDTH + 2 * D_MODEL


def rms_norm_2(x, g):
    xf = x.astype(jnp.float32)
    xf = xf * lax.rsqrt(jnp.mean(xf * xf, axis=-1, keepdims=True) + EPS)
    return xf.astype(x.dtype) * g

def _na_indices(rows):
    kr = min(WIN_ROWS_MAX, rows)
    r = np.arange(rows)
    row_start = np.clip(r - kr // 2, 0, rows - kr)
    key_rows = row_start[:, None] + np.arange(kr)[None, :]
    rel_r = key_rows - r[:, None] + WIN_ROWS_MAX - 1
    ncb = GRID_W // Q_COL_BLOCK
    j = np.arange(ncb)
    cb_start = np.clip(j * Q_COL_BLOCK - WIN_COLS // 2, 0, GRID_W - KEY_COL_SPAN)
    key_cols = cb_start[:, None] + np.arange(KEY_COL_SPAN)[None, :]
    q_cols = j[:, None] * Q_COL_BLOCK + np.arange(Q_COL_BLOCK)[None, :]
    win_start = np.clip(q_cols - WIN_COLS // 2, 0, GRID_W - WIN_COLS)
    kc = key_cols[:, None, :]
    col_mask = (kc >= win_start[..., None]) & (kc < win_start[..., None] + WIN_COLS)
    rel_c = np.clip(kc - q_cols[..., None] + WIN_COLS - 1, 0, 2 * WIN_COLS - 2)
    key_tok = key_rows[:, None, :, None] * GRID_W + key_cols[None, :, None, :]
    key_tok = key_tok.reshape(rows, ncb, kr * KEY_COL_SPAN).astype(np.int32)
    mask = np.broadcast_to(col_mask[:, :, None, :], (ncb, Q_COL_BLOCK, kr, KEY_COL_SPAN))
    mask = mask.reshape(ncb, Q_COL_BLOCK, kr * KEY_COL_SPAN)
    return kr, key_tok, rel_r.astype(np.int32), rel_c.astype(np.int32), mask

def neighbourhood_attention(q, k, v, rpb):
    B, S, H, dh = q.shape
    rows = S // GRID_W
    kr, key_tok, rel_r, rel_c, mask = _na_indices(rows)
    ncb = GRID_W // Q_COL_BLOCK
    qb = q.reshape(B, rows, ncb, Q_COL_BLOCK, H, dh)
    kb = k[:, key_tok]
    vb = v[:, key_tok]
    s = jnp.einsum('brjqhd,brjkhd->bhrjqk', qb, kb).astype(jnp.float32) * (dh ** -0.5)
    bias = rpb[:, rel_r[:, None, None, :, None], rel_c[None, :, :, None, :]]
    bias = bias.reshape(H, rows, ncb, Q_COL_BLOCK, kr * KEY_COL_SPAN).astype(jnp.float32)
    s = jnp.where(jnp.asarray(mask), s + bias[None], NEG_INF)
    p = jax.nn.softmax(s, axis=-1).astype(v.dtype)
    o = jnp.einsum('bhrjqk,brjkhd->brjqhd', p, vb)
    return o.reshape(B, S, H * dh)

def short_gated_conv(cb, cc, ch, w):
    z = cc * ch
    zp = jnp.pad(z, ((0, 0), (1, 1), (0, 0)))
    conv = zp[:, :-2] * w[0] + zp[:, 1:-1] * w[1] + zp[:, 2:] * w[2]
    return cb * conv

def second_inputs(seed: int = 0) -> dict:
    key = jax.random.key(seed)
    ks = jax.random.split(key, 16)
    f32 = jnp.float32

    def nrm(k, shape, scale):
        return jax.random.normal(k, shape, f32) * scale

    return {
        "x": nrm(ks[0], (BATCH, SEQ, D_MODEL), 1.0),
        "norm1_g": 1.0 + nrm(ks[1], (DEPTH_2, D_MODEL), 0.02),
        "w_in": nrm(ks[2], (DEPTH_2, D_MODEL, PROJ_WIDTH), D_MODEL ** -0.5),
        "q_norm_g": 1.0 + nrm(ks[3], (DEPTH_2, HEAD_DIM), 0.02),
        "k_norm_g": 1.0 + nrm(ks[4], (DEPTH_2, HEAD_DIM), 0.02),
        "rpb": nrm(ks[5], (DEPTH_2, N_HEADS, 2 * WIN_ROWS_MAX - 1, 2 * WIN_COLS - 1), 0.5),
        "conv_w": nrm(ks[6], (DEPTH_2, CONV_K, CONV_WIDTH), CONV_K ** -0.5),
        "w_attn_branch": nrm(ks[7], (DEPTH_2, ATTN_WIDTH, D_MODEL), ATTN_WIDTH ** -0.5),
        "w_conv_branch": nrm(ks[8], (DEPTH_2, CONV_WIDTH, D_MODEL), CONV_WIDTH ** -0.5),
        "w_o": nrm(ks[9], (DEPTH_2, D_MODEL, D_MODEL), D_MODEL ** -0.5),
        "norm2_g": 1.0 + nrm(ks[10], (DEPTH_2, D_MODEL), 0.02),
        "w_mlp_in": nrm(ks[11], (DEPTH_2, D_MODEL, D_FF_2), D_MODEL ** -0.5),
        "w_mlp_out": nrm(ks[12], (DEPTH_2, D_FF_2, D_MODEL), D_FF_2 ** -0.5),
    }

def second_block(x, norm1_g, w_in, q_norm_g, k_norm_g, rpb, conv_w, w_attn_branch,
              w_conv_branch, w_o, norm2_g, w_mlp_in, w_mlp_out):
    B, S, _ = x.shape
    split_pts = [int(p) for p in np.cumsum(PROJ_SPLITS)]
    for l in range(DEPTH_2):
        u = rms_norm_2(x, norm1_g[l])
        proj = u @ w_in[l]
        q, k, v, cb, cc, ch, ga, gb = jnp.split(proj, split_pts, axis=-1)
        q = rms_norm_2(q.reshape(B, S, N_HEADS, HEAD_DIM), q_norm_g[l])
        k = rms_norm_2(k.reshape(B, S, N_HEADS, HEAD_DIM), k_norm_g[l])
        v = v.reshape(B, S, N_HEADS, HEAD_DIM)
        y_a = neighbourhood_attention(q, k, v, rpb[l]) @ w_attn_branch[l]
        y_b = short_gated_conv(cb, cc, ch, conv_w[l]) @ w_conv_branch[l]
        merged = jax.nn.sigmoid(ga) * y_a + jax.nn.sigmoid(gb) * y_b
        x = x + merged @ w_o[l]
        h = rms_norm_2(x, norm2_g[l]) @ w_mlp_in[l]
        x = x + jnp.square(jax.nn.relu(h)) @ w_mlp_out[l]
    return x


def setup_inputs(seed=0):
    out = dict(first_inputs(seed))
    for name, value in second_inputs(seed + 1).items():
        if name != "x":
            out[name + "_2"] = value
    return out


def reference(
    x, meta_tokens, ln_mix, ln_mlp, ssd_w_in, ssd_conv_w, ssd_conv_b, ssd_dt_bias, ssd_a_log,
    ssd_d, ssd_norm, ssd_w_out, mla_w_in, mla_q_a_norm, mla_w_q_b, mla_kv_a_norm, mla_w_kv_b,
    mla_q_norm, mla_k_norm, mla_w_out, mlp_w_up, mlp_w_down, norm1_g_2, w_in_2, q_norm_g_2,
    k_norm_g_2, rpb_2, conv_w_2, w_attn_branch_2, w_conv_branch_2, w_o_2, norm2_g_2, w_mlp_in_2,
    w_mlp_out_2,
):
    x = first_block(
        x, meta_tokens, ln_mix, ln_mlp, ssd_w_in, ssd_conv_w, ssd_conv_b, ssd_dt_bias,
        ssd_a_log, ssd_d, ssd_norm, ssd_w_out, mla_w_in, mla_q_a_norm, mla_w_q_b, mla_kv_a_norm,
        mla_w_kv_b, mla_q_norm, mla_k_norm, mla_w_out, mlp_w_up, mlp_w_down,
    )
    return second_block(
        x, norm1_g_2, w_in_2, q_norm_g_2, k_norm_g_2, rpb_2, conv_w_2, w_attn_branch_2,
        w_conv_branch_2, w_o_2, norm2_g_2, w_mlp_in_2, w_mlp_out_2,
    )


_drawn_inputs = setup_inputs


def setup_inputs(seed=0):
    import zlib

    import numpy as np

    out = dict(_drawn_inputs(seed))
    spreads = {}
    factors = {'ln_mlp': 2.688,
     'ssd_norm': 3.32,
     'mla_q_a_norm': 8.0,
     'mla_kv_a_norm': 8.0,
     'mla_q_norm': 8.0,
     'mla_k_norm': 8.0,
     'norm1_g_2': 6.42,
     'q_norm_g_2': 64.0,
     'k_norm_g_2': 64.0,
     'rpb_2': 22.368,
     'norm2_g_2': 42.64}
    for name, (base, spread) in spreads.items():
        noise = np.random.default_rng([zlib.crc32(name.encode()), seed]).standard_normal(out[name].shape)
        drawn = base * np.exp(spread * noise) if base else spread * noise
        out[name] = __import__('jax').numpy.asarray(drawn.astype(out[name].dtype))
    for name, factor in factors.items():
        out[name] = (out[name] * factor).astype(out[name].dtype)
    return out
```

```python
import numpy as np
from contextlib import ExitStack
import concourse.bass as bass
from concourse import mybir
from concourse.alu_op_type import AluOpType as ALU

F32 = mybir.dt.float32
F32R = mybir.dt.float32r
ACT = mybir.ActivationFunctionType

P = 128
D = 1024
KD = D // P
META = 16
SEQ = 256
T = META + SEQ
T2 = SEQ
EPS = 1e-6
GROUPS = 8
HPG = 4
HD = 64
FF_TILES = 32
CHUNK = 2048
MLA_HEADS = 16
QK = 96
NA_HEADS = 8
NEG = -1e30
CLAMP = -44.0

C_DT = 0
C_GRP = C_DT + 1
C_SOUT = C_GRP + 3 * GROUPS
C_UP0 = C_SOUT + 8
C_DN0 = C_UP0 + 16
C_MIN = C_DN0 + 16
C_HEAD = C_MIN + 3
C_MOUT = C_HEAD + 8
C_UP1 = C_MOUT + 4
C_DN1 = C_UP1 + 16
C_IN2 = C_DN1 + 16
C_BR = C_IN2 + 20
C_WO = C_BR + 4
C_UP2 = C_WO + 4
C_DN2 = C_UP2 + 16
N_CHUNKS = C_DN2 + 16

K_DT = 0
K_GRP = 1
K_SOUT = K_GRP + 3 * GROUPS
K_UP0 = K_SOUT + 8
K_DN0 = K_UP0 + 16
K_MIN = K_DN0 + 8
K_HEAD = K_MIN + 3
K_MOUT = K_HEAD + 16
K_UP1 = K_MOUT + 4
K_DN1 = K_UP1 + 16
K_IN2 = K_DN1 + 8
K_BR = K_IN2 + 20
K_WO = K_BR + 8
K_UP2 = K_WO + 4
K_DN2 = K_UP2 + 16

N_IDENT, N_ONES, N_BLK = 0, 128, 256
N_SSD = 384
SSD_W = T + (T - 128) + (T - 256)
N_MLA = N_SSD + SSD_W
MLA_W = 144 + T
N_ROPE = N_MLA + MLA_W
N_NA = N_ROPE + T
N_CONST = N_NA + 64

V_GAIN = 0
V_CONV = V_GAIN + 6 * KD
V_DSKIP = V_CONV + GROUPS * 4 * 5
V_SNORM = V_DSKIP + 16
V_QA = V_SNORM + 16
V_KVA = V_QA + 3
V_QG = V_KVA + 2
V_KG = V_QG + 1
V_CONV2 = V_KG + 1
V_QN2 = V_CONV2 + 12
V_KN2 = V_QN2 + 1
V_DTB = V_KN2 + 1
V_ALOG = V_DTB + 1
N_VEC = V_ALOG + 1


class At:

    def __init__(self, base, step=0, turn=0):
        assert step % 2 == 0
        self.base, self.step, self.turn = base, step, turn

    def __add__(self, n):
        return At(self.base + n, self.step, self.turn)

    def times(self, n, plus=0):
        return At(self.base * n + plus, self.step * n, self.turn)

    @property
    def value(self):
        return self.turn * self.step + self.base if self.step else self.base

    @property
    def half(self):
        return self.turn * (self.step // 2) + self.base // 2 if self.step else self.base // 2

    @property
    def parity(self):
        return self.base % 2


def build(nc, w, h0, vec, const, rpb, out, acs_dram):
    ctx = ExitStack()
    with ctx:
        def sb(name, shape, dt=F32, where=ctx):
            return where.enter_context(nc.sbuf_tensor(name, shape, dt))

        def sem(name):
            return ctx.enter_context(nc.semaphore(name))

        w_raw = [sb(f"w_raw{i}", [P, CHUNK]) for i in range(2)]
        w_hi = [sb(f"w_hi{i}", [P, CHUNK], F32R) for i in range(2)]
        w_lo = [sb(f"w_lo{i}", [P, CHUNK], F32R) for i in range(2)]
        h = sb("h", [P, KD, T])
        x_hi = sb("x_hi", [P, KD, T], F32R)
        x_lo = sb("x_lo", [P, KD, T], F32R)
        h_sq = sb("h_sq", [P, KD, T])
        r_ln = sb("r_ln", [P, T])
        r_inv = sb("r_inv", [P, T])
        vecs = sb("vecs", [P, N_VEC])
        cst = sb("cst", [P, N_CONST])
        bias_mask = sb("bias_mask", [P, NA_HEADS, 2, 256])
        eps_t = sb("eps_t", [P, 3])

        ssd = ExitStack()
        g_hi = sb("g_hi", [P, 16, T], F32R, ssd)
        g_lo = sb("g_lo", [P, 16, T], F32R, ssd)
        a_exp = sb("a_exp", [32, 1], F32, ssd)
        cols = sb("cols", [P, 6, 32], F32, ssd)
        acs_bc = [sb(f"acs_bc{i}", [P, HPG, T], F32, ssd) for i in range(2)]
        u = sb("u", [P, 4, T + 3], F32, ssd)
        cv = sb("cv", [P, 4, T], F32, ssd)
        sg = sb("sg", [P, 4, T], F32, ssd)
        z_raw = sb("z_raw", [P, 2, T], F32, ssd)
        z_sg = sb("z_sg", [P, 2, T], F32, ssd)
        xs_s = [sb(f"xs_s{i}", [P, 2, T], F32, ssd) for i in range(2)]
        bc_s = sb("bc_s", [P, 2, T], F32, ssd)
        z_s = [sb(f"z_s{i}", [P, 2, T], F32, ssd) for i in range(2)]
        x_tok = sb("x_tok", [P, 3, 256], F32, ssd)
        cbm = sb("cbm", [P, SSD_W], F32, ssd)
        dd = sb("dd", [P, HPG, SSD_W], F32, ssd)
        mm = sb("mm", [P, HPG, SSD_W], F32, ssd)
        y1 = sb("y1", [P, 2, T], F32, ssd)
        y2 = sb("y2", [P, 2, T], F32, ssd)
        dtx, dtb, dta, dt_t = [mm[0:32, i, 0:T] for i in range(4)]
        acs = y1[0:32, 0, :]
        y_sum = sb("y_sum", [P, T], F32, ssd)
        g_ln = sb("g_ln", [P, T], F32, ssd)
        g_inv = sb("g_inv", [P, T], F32, ssd)
        ssd.close()

        mlp_mem = ExitStack()
        hid_hi = sb("hid_hi", [P, FF_TILES, T], F32R, mlp_mem)
        hid_lo = sb("hid_lo", [P, FF_TILES, T], F32R, mlp_mem)
        relu = [sb(f"relu{i}", [P, 2, T], F32, mlp_mem) for i in range(2)]
        relu_sq = [sb(f"relu_sq{i}", [P, 2, T], F32, mlp_mem) for i in range(2)]
        down_r = [sb(f"down_r{i}", [P, T], F32, mlp_mem) for i in range(2)]
        mlp_mem.close()

        mla = ExitStack()
        lat = sb("lat", [P, 6, T], F32, mla)
        lat_sq = h_sq[:, 0:6, :]
        lat_n = lat[:, 0:5, :]
        l_hi = sb("l_hi", [P, 5, T], F32R, mla)
        l_lo = sb("l_lo", [P, 5, T], F32R, mla)
        l_ln = sb("l_ln", [P, 2, T], F32, mla)
        l_inv = sb("l_inv", [P, 2, T], F32, mla)
        rope_q = sb("rope_q", [P, T], F32, mla)
        rope_k = sb("rope_k", [P, T], F32, mla)
        rot_a = sb("rot_a", [P, 2, T], F32, mla)
        rot_b = sb("rot_b", [P, 2, T], F32, mla)
        q_pre = sb("q_pre", [QK, 4, T2], F32, mla)
        k_pre = sb("k_pre", [QK, 4, T], F32, mla)
        q_sq = sb("q_sq", [QK, 2, T2], F32, mla)
        k_sq = sb("k_sq", [QK, 4, T], F32, mla)
        v_t = sb("v_t", [P, 4, T], F32, mla)
        n_ln = sb("n_ln", [QK, 2, T], F32, mla)
        n_inv = sb("n_inv", [QK, 2, T], F32, mla)
        q_fin = [sb(f"q_fin{i}", [QK, 4, T2], F32, mla) for i in range(2)]
        k_fin = [sb(f"k_fin{i}", [QK, 4, T], F32, mla) for i in range(2)]
        v_tok = [sb(f"v_tok{i}", [P, 4, 3, HD], F32, mla) for i in range(2)]
        o_hi = sb("o_hi", [P, 8, T2], F32R, mla)
        o_lo = sb("o_lo", [P, 8, T2], F32R, mla)
        s_m = [sb(f"s_m{i}", [P, MLA_W], F32, mla) for i in range(2)]
        pr = [sb(f"pr{i}", [P, MLA_W], F32, mla) for i in range(2)]
        p_t = sb("p_t", [P, 384], F32, mla)
        p_t0 = sb("p_t0", [META, T2], F32, mla)
        mx = [sb(f"mx{i}", [P, 2], F32, mla) for i in range(2)]
        nmx = [sb(f"nmx{i}", [P, 2], F32, mla) for i in range(2)]
        rsum = [sb(f"rsum{i}", [P, 2], F32, mla) for i in range(2)]
        rinv = [sb(f"rinv{i}", [P, 2], F32, mla) for i in range(2)]
        mla.close()

        na = ExitStack()
        qk_r = sb("qk_r", [P, 8, T2], F32, na)
        qk_f = sb("qk_f", [P, 8, T2], F32, na)
        qk_sq = [sb(f"qk_sq{i}", [P, 2, T2], F32, na) for i in range(2)]
        qk_ln = sb("qk_ln", [P, 2, T2], F32, na)
        qk_inv = [sb(f"qk_inv{i}", [P, 2, T2], F32, na) for i in range(2)]
        v_r = sb("v_r", [P, 4, T2], F32, na)
        v2 = sb("v2", [P, 2, 512], F32, na)
        cc_ch = h_sq[:, 0:2, 0:T2]
        zc = sb("zc", [P, 4, T2 + 2], F32, na)
        cv2 = sb("cv2", [P, 4, T2], F32, na)
        cb_r = sb("cb_r", [P, 4, T2], F32, na)
        yb = cv2
        yb_hi = sb("yb_hi", [P, 4, T2], F32R, na)
        yb_lo = sb("yb_lo", [P, 4, T2], F32R, na)
        ya_hi = sb("ya_hi", [P, 4, T2], F32R, na)
        ya_lo = sb("ya_lo", [P, 4, T2], F32R, na)
        gate = sb("gate", [P, 16, T2], F32, na)
        s_m2 = [sb(f"s_m2{i}", [P, 512], F32, na) for i in range(2)]
        pr2 = [sb(f"pr2{i}", [P, 512], F32, na) for i in range(2)]
        p_t2 = sb("p_t2", [P, 512], F32, na)
        mx2 = [sb(f"mx2{i}", [P, 2], F32, na) for i in range(2)]
        nmx2 = [sb(f"nmx2{i}", [P, 2], F32, na) for i in range(2)]
        rsum2 = [sb(f"rsum2{i}", [P, 2], F32, na) for i in range(2)]
        rinv2 = [sb(f"rinv2{i}", [P, 2], F32, na) for i in range(2)]
        m_a, m_b = h_sq[:, 2:4, 0:T2], h_sq[:, 4:6, 0:T2]
        na.close()

        lin = ctx.enter_context(nc.psum_tensor("lin", [P, 4, 512], F32))
        ps4, ps5, ps6, ps7 = [ctx.enter_context(nc.psum_tensor(f"ps{i}", [P, 512], F32)) for i in range(4, 8)]

        def linp(k, n, rows=slice(0, P)):
            return lin[rows, 2 * k.parity:2 * k.parity + 2, n]

        ident = cst[:, N_IDENT:N_IDENT + P]
        ones = cst[:, N_ONES:N_ONES + P]
        blk = cst[:, N_BLK:N_BLK + P]

        def v(col, n=1, rows=slice(0, P)):
            return vecs[rows, bass.ds(col, n)]

        def gain(norm, kt):
            return v(V_GAIN + norm * KD + kt)

        def over(ap, n):
            return ap.unsqueeze(1).broadcast_to([ap.shape[0], n, ap.shape[1]])

        w_arrived = [sem(f"w_arrived{i}") for i in range(2)]
        w_hi_done, w_lo_done, w_used = sem("w_hi_done"), sem("w_lo_done"), sem("w_used")
        drained = [sem(f"drained{i}") for i in range(2)]
        half_done = sem("half_done")
        small_in, h_in, rpb_in, out_done = sem("small_in"), sem("h_in"), sem("rpb_in"), sem("out_done")
        xh_done, xl_done = sem("xh_done"), sem("xl_done")
        hsq_done, hsum_done, stat_done = sem("hsq_done"), sem("hsum_done"), sem("stat_done")
        rln_done, r_done = sem("rln_done"), sem("r_done")
        h_mlp = sem("h_mlp")
        memset_done, bias_done, pool_memset = sem("memset_done"), sem("bias_done"), sem("pool_memset")
        dt_dve, dt_act, dtT_done, cols_done = sem("dt_dve"), sem("dt_act"), sem("dtT_done"), sem("cols_done")
        acs_out = sem("acs_out")
        acs_in = [sem(f"acs_in{i}") for i in range(2)]
        cv0_done, cv_step, clamped, sg_step, silu_done = (sem("cv0_done"), sem("cv_step"), sem("clamped"),
                                                          sem("sg_step"), sem("silu_done"))
        xT_done, xtok_done, cb_done, cbm_done = sem("xT_done"), sem("xtok_done"), sem("cb_done"), sem("cbm_done")
        dd_done, ee_done, mm_done, y_done, y_read = (sem("dd_done"), sem("ee_done"), sem("mm_done"),
                                                     sem("y_done"), sem("y_read"))
        y2_done, ysq_done, ysum_done, gstat_done = sem("y2_done"), sem("ysq_done"), sem("ysum_done"), sem("gstat_done")
        gln_done, ginv_done, y3_done, gh_done, gl_done = (sem("gln_done"), sem("ginv_done"), sem("y3_done"),
                                                          sem("gh_done"), sem("gl_done"))
        relu_done, rsq_done, hh_done, hl_done = sem("relu_done"), sem("rsq_done"), sem("hh_done"), sem("hl_done")
        latsq_done, lstat_done, l_act, latn_done = sem("latsq_done"), sem("lstat_done"), sem("l_act"), sem("latn_done")
        lh_done, ll_done, rope_done, krope = sem("lh_done"), sem("ll_done"), sem("rope_done"), sem("krope")
        raw_read, rot_done, rot_sum, nsum_done = sem("raw_read"), sem("rot_done"), sem("rot_sum"), sem("nsum_done")
        nln_done, ninv_done, fin_done = sem("nln_done"), sem("ninv_done"), sem("fin_done")
        s_done, sm_done, nm_done, ex_done = sem("s_done"), sem("sm_done"), sem("nm_done"), sem("ex_done")
        ri_done, p_done, pT_done, pt_done, pt0_done = (sem("ri_done"), sem("p_done"), sem("pT_done"),
                                                       sem("pt_done"), sem("pt0_done"))
        pv_done, oh_done, ol_done = sem("pv_done"), sem("oh_done"), sem("ol_done")
        qksq_done, qkstat_done, qkln_done, qkinv_done, qkf_done = (sem("qksq_done"), sem("qkstat_done"),
                                                                   sem("qkln_done"), sem("qkinv_done"), sem("qkf_done"))
        vT_done, v2_done = sem("vT_done"), sem("v2_done")
        z_done, cv2_0, cv2_step, yb_done, ybh_done, ybl_done = (sem("z_done"), sem("cv2_0"), sem("cv2_step"),
                                                                sem("yb_done"), sem("ybh_done"), sem("ybl_done"))
        gclamp, gate_step = sem("gclamp"), sem("gate_step")
        s2_done, sm2_done, nm2_done, ex2_done = sem("s2_done"), sem("sm2_done"), sem("nm2_done"), sem("ex2_done")
        ri2_done, p2_done, pT2_done, pt2_done = sem("ri2_done"), sem("p2_done"), sem("pT2_done"), sem("pt2_done")
        pv2_done, yah_done, yal_done = sem("pv2_done"), sem("yah_done"), sem("yal_done")
        m_done, mh_done, ml_done = sem("m_done"), sem("mh_done"), sem("ml_done")

        block = ctx.enter_context(nc.Block())

        SLOT_TURNS = 3
        LAST = N_CHUNKS - 2

        def h_ready(norm, kt):
            if norm == 0:
                return (h_in, 16)
            if norm == 1:
                k = At(K_SOUT + kt)
            elif norm == 3:
                k = At(K_MOUT + kt // 2)
            elif norm == 5:
                k = At(K_WO + kt // 2)
            else:
                return (h_mlp, 8 * (norm // 2 - 1) + kt + 1)
            return (drained[k.parity], k.half + 1)

        def tokens(norm):
            return slice(0, T) if norm < 3 else slice(META, T)

        def width(norm):
            return T if norm < 3 else T2

        @block.sync
        def _(sp):
            sp.dma_start(cst[:, :], const).then_inc(small_in, 16)
            sp.dma_start(vecs[:, :], vec).then_inc(small_in, 16)
            sp.dma_start(h[:, :, :], h0).then_inc(h_in, 16)
            for i in range(2):
                sp.dma_start(w_raw[i][:, :], w[i]).then_inc(w_arrived[i], 16)
            with sp.Fori(1, N_CHUNKS // 2) as turn:
                for i in range(2):
                    sp.wait_ge(w_lo_done, turn * 2 + (i - 1))
                    sp.dma_start(w_raw[i][:, :], w[turn * 2 + i]).then_inc(w_arrived[i], 16)
            for kt in range(KD):
                sp.wait_ge(h_mlp, 16 + kt + 1)
                sp.dma_start(out[:, kt, :], h[:, kt, META:T]).then_inc(out_done, 16)
            sp.wait_ge(out_done, 16 * KD)

        @block.tensor
        def _(pe):
            mm3 = nc.tensor.matmul

            def free(k):
                if k.base >= 2:
                    pe.wait_ge(drained[k.parity], k.half)

            def weights(c):
                pe.wait_ge(w_lo_done, (c + 1).value)

            def tile(o, c, at, step, kts, hi, lo, n, first=True, last=True, kt0=0, before=None):
                for i in range(kts):
                    if before:
                        before(i)
                    wh = w_hi[c.parity][:, at + i * step:at + i * step + P]
                    wl = w_lo[c.parity][:, at + i * step:at + i * step + P]
                    xh, xl = hi[:, kt0 + i, 0:n], lo[:, kt0 + i, 0:n]
                    mm3(o, wh, xh, start=first and i == 0, stop=False)
                    mm3(o, wh, xl, start=False, stop=False)
                    ins = mm3(o, wl, xh, start=False, stop=last and i == kts - 1)
                return ins

            def lin_chunk(c, k, n, norm=None):
                weights(c)
                free(k)
                for j in range(2):
                    before = None
                    if norm is not None and j == 0:
                        before = lambda i: pe.wait_ge(xl_done, KD * norm + i + 1)
                    ins = tile(lin[:, 2 * k.parity + j, 0:n], c, j * P, 256, KD, x_hi, x_lo, n, before=before)
                ins.then_inc(w_used, 1)

            def norm_stat(norm):
                n = width(norm)
                pe.wait_ge(hsum_done, norm + 1)
                nc.tensor.matmul(ps7[:, 0:n], ones, h_sq[:, 0, 0:n], start=True, stop=True).then_inc(stat_done, 1)

            pe.wait_ge(small_in, 32)
            c, k = At(C_DT), At(K_DT)
            weights(c)
            tile(lin[:, 0, 0:T], c, 0, 256, KD, x_hi, x_lo, T,
                 before=lambda i: pe.wait_ge(xl_done, i + 1)).then_inc(w_used, 1)
            norm_stat(0)

            def dt_transposes():
                pe.wait_ge(dt_dve, 6)
                for i, src in enumerate((dt_t, acs)):
                    for s in range(3):
                        n = min(P, T - s * P)
                        ins = nc.tensor.transpose(ps4[0:n, (3 * i + s) * 32:(3 * i + s + 1) * 32],
                                                  src[:, s * P:s * P + n], ident[0:32, 0:32])
                ins.then_inc(dtT_done, 1)

            def x_transposes(g):
                pe.wait_ge(silu_done, g.times(3, 1).value)
                if g.base >= 1:
                    pe.wait_ge(y_read, g.times(2, -1).value)
                else:
                    pe.wait_ge(cols_done, 2)
                for q in range(2):
                    nc.tensor.transpose(ps4[:, q * P:(q + 1) * P], xs_s[g.parity][:, q, 0:128], ident)
                    nc.tensor.transpose(ps6[:, q * P:(q + 1) * P], xs_s[g.parity][:, q, 128:256], ident)
                    ins = nc.tensor.transpose(ps4[0:META, 256 + q * P:256 + (q + 1) * P],
                                              xs_s[g.parity][:, q, 256:T], ident)
                ins.then_inc(xT_done, 1)

            def cb_products(g):
                pe.wait_ge(silu_done, g.times(3, 2).value)
                if g.base >= 2:
                    pe.wait_ge(gln_done, (g + (-1)).value)
                b, cc = bc_s[:, 0, :], bc_s[:, 1, :]
                nc.tensor.matmul(ps5[:, 0:T], b[:, 0:128], cc, start=True, stop=True)
                nc.tensor.matmul(ps5[:, T:T + 144], b[:, 128:256], cc[:, 128:T], start=True, stop=True)
                nc.tensor.matmul(ps5[0:META, 416:432], b[:, 256:T], cc[:, 256:T],
                                 start=True, stop=True).then_inc(cb_done, 1)

            def group_stat(g):
                pe.wait_ge(ysum_done, (g + 1).value)
                pe.wait_ge(cbm_done, (g + 2).value) if g.base < 7 else None
                nc.tensor.matmul(ps5[:, 0:T], ones, y_sum[:, :], start=True, stop=True).then_inc(gstat_done, 1)

            def y_products(g):
                pe.wait_ge(xtok_done, (g + 1).value)
                for q in range(2):
                    o = (ps6, ps7)[q]
                    if q == 1 and g.base >= 1:
                        pe.wait_ge(y_read, g.times(2).value)
                    if q == 1 and g.base == 0:
                        pe.wait_ge(rln_done, 1)
                    for e in range(2):
                        j = 2 * q + e
                        pe.wait_ge(mm_done, g.times(4, j + 1).value)
                        rows = slice(e * HD, (e + 1) * HD)
                        cs = slice(j * HD, (j + 1) * HD)
                        nc.tensor.matmul(o[rows, 0:T], x_tok[:, 0, cs], mm[:, j, 0:T], start=True, stop=False)
                        nc.tensor.matmul(o[rows, 128:T], x_tok[:, 1, cs], mm[:, j, T:416], start=False, stop=False)
                        ins = nc.tensor.matmul(o[rows, 256:T], x_tok[0:META, 2, cs], mm[0:META, j, 416:432],
                                               start=False, stop=True)
                    ins.then_inc(y_done, 1)

            def slot(s, has_lin=True, has_scan=True, has_stat=True, first=False):
                c, k = s.times(3, C_GRP), s.times(3, K_GRP)
                if has_lin:
                    lin_chunk(c, k, T)
                if first:
                    dt_transposes()
                if has_scan:
                    x_transposes(s + (-1))
                    cb_products(s + (-1))
                if has_lin:
                    lin_chunk(c + 1, k + 1, T)
                if has_stat:
                    group_stat(s + (-2))
                if has_lin:
                    lin_chunk(c + 2, k + 2, T)
                if has_scan:
                    y_products(s + (-1))

            slot(At(0), has_scan=False, has_stat=False, first=True)
            slot(At(1), has_stat=False)
            with pe.Fori(0, SLOT_TURNS) as turn:
                for i in range(2):
                    slot(At(2 + i, 2, turn))
            slot(At(8), has_lin=False)
            slot(At(9), has_lin=False, has_scan=False)

            pe.wait_ge(gl_done, 16)
            with pe.Fori(0, 4) as turn:
                for i in range(2):
                    c, k = At(C_SOUT + i, 2, turn), At(K_SOUT + i, 2, turn)
                    weights(c)
                    free(k)
                    tile(lin[:, 2 * k.parity, 0:T], c, 0, P, 16, g_hi, g_lo, T).then_inc(w_used, 1)

            def mlp(m, norm, c_up, k_up, c_dn, k_dn):
                n = width(norm)
                lin_chunk(At(c_up), At(k_up), n, norm)
                lin_chunk(At(c_up + 1), At(k_up + 1), n)
                norm_stat(norm)
                with pe.Fori(1, 8) as turn:
                    for i in range(2):
                        lin_chunk(At(c_up + i, 2, turn), At(k_up + i, 2, turn), n)
                with pe.Fori(0, 4) as turn:
                    for i in range(2):
                        k = At(k_dn + i, 2, turn)
                        free(k)
                        for half in range(2):
                            c = At(c_dn + 2 * i + half, 4, turn)
                            weights(c)
                            pe.wait_ge(hl_done, 16 * m + 8 * (half + 1))
                            tile(lin[:, 2 * k.parity, 0:n], c, 0, P, 16, hid_hi, hid_lo, n, first=half == 0,
                                 last=half == 1, kt0=16 * half).then_inc(w_used, 1)

            mlp(0, 1, C_UP0, K_UP0, C_DN0, K_DN0)

            lin_chunk(At(C_MIN), At(K_MIN), T, 2)
            lin_chunk(At(C_MIN + 1), At(K_MIN + 1), T)
            norm_stat(2)
            lin_chunk(At(C_MIN + 2), At(K_MIN + 2), T)
            pe.wait_ge(latsq_done, 3)
            for i in range(3):
                ins = nc.tensor.matmul(ps4[:, 0:T], ones, lat_sq[:, i, :], start=i == 0, stop=i == 2)
            ins.then_inc(lstat_done, 1)
            for i in range(2):
                ins = nc.tensor.matmul(ps5[:, 0:T], ones, lat_sq[:, 3 + i, :], start=i == 0, stop=i == 1)
            ins.then_inc(lstat_done, 1)

            def unit(s, n):
                c, k = At(C_HEAD + 2 * s + n // 2), At(K_HEAD + 4 * s + n)
                kts, kt0, first_t = (3, 0, META) if n < 2 else (2, 3, 0)
                if s == 0:
                    pe.wait_ge(ll_done, 3 if n < 2 else 5)
                if n % 2 == 0:
                    weights(c)
                free(k)
                for j in range(2):
                    head = 2 * (n % 2) + j
                    o = lin[:, 2 * k.parity + j, 0:T - first_t]
                    for i in range(kts):
                        at = i * 512 + head * P
                        wh, wl = w_hi[c.parity][:, at:at + P], w_lo[c.parity][:, at:at + P]
                        xh, xl = l_hi[:, kt0 + i, first_t:T], l_lo[:, kt0 + i, first_t:T]
                        mm3(o, wh, xh, start=i == 0, stop=False)
                        mm3(o, wh, xl, start=False, stop=False)
                        ins = mm3(o, wl, xh, start=False, stop=i == kts - 1)
                ins.then_inc(half_done if n % 2 == 0 else w_used, 1)

            def unit_norm(s, n):
                k = At(K_HEAD + 4 * s + n)
                pe.wait_ge(raw_read, 4 * s + n + 1)
                if n < 2:
                    pe.wait_ge(rot_sum, 2 * s + n + 1)
                elif s == 0:
                    pe.wait_ge(krope, 4)
                for j in range(2):
                    head = 2 * (n % 2) + j
                    bank = lin[:, 2 * k.parity + j, :]
                    if n < 2:
                        ins = nc.tensor.matmul(bank[:, 0:T2], ones[0:QK, :], q_sq[:, j, :], start=True, stop=True)
                    else:
                        nc.tensor.matmul(bank[:, 0:T], ones[0:QK, :], k_sq[:, head, :], start=True, stop=True)
                        idv = ident[HD:P, HD:P]
                        nc.tensor.transpose(bank[:, 272:336], v_t[HD:P, head, META:144], idv)
                        nc.tensor.transpose(bank[:, 336:400], v_t[HD:P, head, 144:T], idv)
                        ins = nc.tensor.transpose(bank[0:META, 400:464], v_t[HD:P, head, 0:META], idv)
                ins.then_inc(nsum_done, 1)

            def scores(s, j):
                n, p = 4 * s + j, s % 2
                if j == 0:
                    pe.wait_ge(fin_done, 4 * s + 4)
                if n >= 2:
                    pe.wait_ge(sm_done, n - 1)
                elif n == 0:
                    pe.wait_ge(l_act, 2)
                o = (ps5, ps6)[n % 2]
                nc.tensor.matmul(o[:, 0:144], q_fin[p][:, j, 0:128], k_fin[p][:, j, 0:144], start=True, stop=True)
                nc.tensor.matmul(o[:, 144:416], q_fin[p][:, j, 128:256], k_fin[p][:, j, :],
                                 start=True, stop=True).then_inc(s_done, 1)

            def p_transposes(s, j):
                n = 4 * s + j
                pe.wait_ge(p_done, n + 1)
                if n >= 1:
                    pe.wait_ge(pt_done, n)
                else:
                    pe.wait_ge(rln_done, 3)
                if n % 2 == 0 and n >= 2:
                    pe.wait_ge(ol_done, n // 2)
                prn = pr[n % 2]
                nc.tensor.transpose(ps4[0:META, 256:384], prn[:, 0:16], ident)
                nc.tensor.transpose(ps4[0:META, 384:512], prn[:, 144:160], ident)
                nc.tensor.transpose(ps7[:, 0:128], prn[:, 16:144], ident)
                nc.tensor.transpose(ps7[:, 128:256], prn[:, 160:288], ident)
                nc.tensor.transpose(ps7[:, 256:384], prn[:, 288:416], ident).then_inc(pT_done, 1)

            def values(s, j):
                n, p = 4 * s + j, s % 2
                pe.wait_ge(pt_done, n + 1)
                pe.wait_ge(pt0_done, n + 1)
                o = ps4[(n % 2) * HD:(n % 2 + 1) * HD, 0:T2]
                nc.tensor.matmul(o, v_tok[p][0:META, j, 0, :], p_t0[:, :], start=True, stop=False)
                nc.tensor.matmul(o, v_tok[p][:, j, 1, :], p_t[:, 0:256], start=False, stop=False)
                nc.tensor.matmul(o[:, 128:256], v_tok[p][:, j, 2, :], p_t[:, 256:384],
                                 start=False, stop=True).then_inc(pv_done, 1)

            for s in range(5):
                proj, att = s < 4, s > 0
                if att:
                    scores(s - 1, 0)
                for n in range(4):
                    if proj:
                        unit(s, n)
                    if att:
                        if n < 3:
                            scores(s - 1, n + 1)
                        p_transposes(s - 1, n)
                        values(s - 1, n)
                    if proj:
                        unit_norm(s, n)

            pe.wait_ge(ol_done, 8)
            for i in range(4):
                c, k = At(C_MOUT + i), At(K_MOUT + i)
                weights(c)
                free(k)
                for j in range(2):
                    ins = tile(lin[:, 2 * k.parity + j, 0:T2], c, j * P, 256, KD, o_hi, o_lo, T2)
                ins.then_inc(w_used, 1)

            mlp(1, 3, C_UP1, K_UP1, C_DN1, K_DN1)

            def qk_stat(i):
                pe.wait_ge(qksq_done, i + 1)
                if i >= 2:
                    pe.wait_ge(qkln_done, i - 1)
                nc.tensor.matmul((ps5, ps6)[i % 2][:, :], blk, qk_sq[i % 2][:, :, :].rearrange("p a t -> p (a t)"),
                                 start=True, stop=True).then_inc(qkstat_done, 1)

            def v_transposes():
                for i in (4, 5):
                    k = At(K_IN2 + i)
                    pe.wait_ge(drained[k.parity], k.half + 1)
                pe.wait_ge(rln_done, 5)
                for tt, o in ((0, ps7), (1, ps4)):
                    for j in range(4):
                        ins = nc.tensor.transpose(o[:, j * P:(j + 1) * P], v_r[:, j, tt * P:(tt + 1) * P], ident)
                ins.then_inc(vT_done, 1)

            def scores2(n):
                if n == 0:
                    pe.wait_ge(qkln_done, 3)
                    pe.wait_ge(qkf_done, 4)
                elif n == 1:
                    pe.wait_ge(qkln_done, 4)
                else:
                    pe.wait_ge(sm2_done, n - 1)
                rows, j = slice((n % 2) * HD, (n % 2 + 1) * HD), n // 2
                for qt in range(2):
                    ins = nc.tensor.matmul((ps5, ps6)[n % 2][:, qt * 256:(qt + 1) * 256],
                                           qk_f[rows, j, qt * P:(qt + 1) * P], qk_f[rows, 4 + j, :],
                                           start=True, stop=True)
                ins.then_inc(s2_done, 1)

            def attend2(n):
                pe.wait_ge(p2_done, n + 1)
                if n == 0:
                    pe.wait_ge(v2_done, 2)
                else:
                    pe.wait_ge(pt2_done, n)
                for kt in range(2):
                    for qt in range(2):
                        ins = nc.tensor.transpose(ps7[:, kt * 256 + qt * P:kt * 256 + (qt + 1) * P],
                                                  pr2[n % 2][:, qt * 256 + kt * P:qt * 256 + (kt + 1) * P], ident)
                ins.then_inc(pT2_done, 1)
                if n % 2 == 0 and n >= 2:
                    pe.wait_ge(yal_done, n // 2)
                pe.wait_ge(pt2_done, n + 1)
                o = ps4[(n % 2) * HD:(n % 2 + 1) * HD, 0:T2]
                for kt in range(2):
                    ins = nc.tensor.matmul(o, v2[:, kt, n * HD:(n + 1) * HD], p_t2[:, kt * 256:(kt + 1) * 256],
                                           start=kt == 0, stop=kt == 1)
                ins.then_inc(pv2_done, 1)

            for i in range(20):
                lin_chunk(At(C_IN2 + i), At(K_IN2 + i), T2, 4 if i == 0 else None)
                if i == 0:
                    norm_stat(4)
                if 1 <= i <= 4:
                    qk_stat(i - 1)
                if i == 6:
                    v_transposes()
                if 6 <= i < 14:
                    scores2(i - 6)
                if 7 <= i < 15:
                    attend2(i - 7)

            pe.wait_ge(yal_done, 4)
            pe.wait_ge(ybl_done, 2)
            for b in range(4):
                c = At(C_BR + b)
                weights(c)
                for n, (hi, lo) in enumerate(((ya_hi, ya_lo), (yb_hi, yb_lo))):
                    k = At(K_BR + 2 * b + n)
                    free(k)
                    for j in range(2):
                        ins = tile(lin[:, 2 * k.parity + j, 0:T2], c, 1024 * n + j * P, 256, 4, hi, lo, T2)
                    ins.then_inc((half_done, w_used)[n], 1)

            for i in range(4):
                c, k = At(C_WO + i), At(K_WO + i)
                weights(c)
                free(k)
                for j in range(2):
                    before = (lambda kt: pe.wait_ge(ml_done, kt // 2 + 1)) if i == 0 and j == 0 else None
                    ins = tile(lin[:, 2 * k.parity + j, 0:T2], c, j * P, 256, KD, x_hi, x_lo, T2, before=before)
                ins.then_inc(w_used, 1)

            mlp(2, 5, C_UP2, K_UP2, C_DN2, K_DN2)

        @block.scalar
        def _(act):
            a = nc.scalar.activation

            def hi(c):
                act.wait_ge(w_arrived[c.parity], (c.half + 1) * 16)
                if c.base >= 2:
                    act.wait_ge(w_used, (c + (-1)).value)
                a(w_hi[c.parity][:, :], w_raw[c.parity][:, :], ACT.Copy).then_inc(w_hi_done, 1)

            def norm_hi(norm):
                n, tk = width(norm), tokens(norm)
                for kt in range(KD):
                    act.wait_ge(*h_ready(norm, kt))
                    a(x_hi[:, kt, 0:n], h[:, kt, tk], ACT.Copy, scale=gain(norm, kt)).then_inc(xh_done, 1)
                a(h_sq[:, :, 0:n], h[:, :, tk], ACT.Square).then_inc(hsq_done, 1)

            def norm_inv(norm, squared=False):
                n = width(norm)
                act.wait_ge(stat_done, norm + 1)
                a(r_ln[:, 0:n], ps7[:, 0:n], ACT.Ln, bias=eps_t[:, 0:1], scale=1.0 / D).then_inc(rln_done, 1)
                act.wait_ge(rln_done, norm + 1)
                a(r_inv[:, 0:n], r_ln[:, 0:n], ACT.Exp, scale=-1.0 if squared else -0.5).then_inc(r_done, 1)

            act.preload_act_table_set("natural_log_exp_and_others")
            act.wait_ge(small_in, 32)
            act.wait_ge(memset_done, 4)
            norm_hi(0)
            hi(At(0))
            hi(At(1))
            a(a_exp[:, :], v(V_ALOG, rows=slice(0, 32)), ACT.Exp).then_inc(dt_act, 1)
            norm_inv(0)
            hi(At(2))
            act.wait_ge(dt_dve, 3)
            a(dta[:, :], dta[:, :], ACT.Exp, scale=-1.0).then_inc(dt_act, 1)
            act.wait_ge(dt_act, 2)
            a(dta[:, :], dta[:, :], ACT.Ln, bias=1.0).then_inc(dt_act, 1)

            def sigmoid(buf, step_sem, n):
                a(buf, buf, ACT.Exp, scale=-1.0).then_inc(step_sem, 1)
                act.wait_ge(step_sem, (n + 1).value)
                a(buf, buf, ACT.Ln, bias=1.0).then_inc(step_sem, 1)
                act.wait_ge(step_sem, (n + 2).value)
                a(buf, buf, ACT.Exp, scale=-1.0).then_inc(step_sem, 1)

            def conv0(s, pair):
                k = s.times(3, K_GRP + pair)
                act.wait_ge(drained[k.parity], (k.half + 1))
                for q in (2 * pair, 2 * pair + 1):
                    at = s.times(20, V_CONV + 5 * q)
                    a(cv[:, q, :], u[:, q, 0:T], ACT.Identity, scale=v(at.value), bias=v((at + 4).value))\
                        .then_inc(cv0_done, 1)

            def slot(s, has_lin=True, has_scan=True, has_stat=True):
                c = s.times(3, C_GRP)
                g, gs = s + (-1), s + (-2)
                if has_lin:
                    hi(c + 2)
                if has_stat:
                    act.wait_ge(y2_done, (gs + 1).value)
                    a(h_sq[:, 0:2, :], y2[:, :, :], ACT.Square).then_inc(ysq_done, 1)
                if has_lin:
                    conv0(s, 0)
                if has_scan:
                    act.wait_ge(xT_done, (g + 1).value)
                    a(x_tok[:, 0, :], ps4[:, 0:256], ACT.Copy)
                    a(x_tok[0:META, 2, :], ps4[0:META, 256:512], ACT.Copy)
                    a(x_tok[:, 1, :], ps6[:, 0:256], ACT.Copy).then_inc(xtok_done, 1)
                    for j in range(HPG):
                        act.wait_ge(dd_done, g.times(4, j + 1).value)
                        a(dd[:, j, 0:416], dd[:, j, 0:416], ACT.Exp)
                        a(dd[0:META, j, 416:432], dd[0:META, j, 416:432], ACT.Exp).then_inc(ee_done, 1)
                if has_lin:
                    hi(c + 3)
                    act.wait_ge(clamped, s.times(3, 1).value)
                    sigmoid(sg[:, 0:2, :], sg_step, s.times(9))
                    conv0(s, 1)
                if has_stat:
                    act.wait_ge(gstat_done, (gs + 1).value)
                    a(g_ln[:, :], ps5[:, 0:T], ACT.Ln, bias=eps_t[:, 0:1], scale=1.0 / 256).then_inc(gln_done, 1)
                    act.wait_ge(gln_done, (gs + 1).value)
                    a(g_inv[:, :], g_ln[:, :], ACT.Exp, scale=-0.5).then_inc(ginv_done, 1)
                    act.wait_ge(y3_done, (gs + 1).value)
                    for q in range(2):
                        t = gs.times(2, q)
                        a(g_hi[:, t.value, :], y1[:, q, :], ACT.Copy, scale=v((t + V_SNORM).value))\
                            .then_inc(gh_done, 1)
                if has_lin:
                    hi(c + 4)
                    act.wait_ge(clamped, s.times(3, 2).value)
                    sigmoid(sg[:, 2:4, :], sg_step, s.times(9, 3))
                    act.wait_ge(clamped, s.times(3, 3).value)
                    sigmoid(z_sg[:, :, :], sg_step, s.times(9, 6))

            slot(At(0), has_scan=False, has_stat=False)
            slot(At(1), has_stat=False)
            with act.Fori(0, SLOT_TURNS) as turn:
                for i in range(2):
                    slot(At(2 + i, 2, turn))
            slot(At(8), has_lin=False)
            slot(At(9), has_lin=False, has_scan=False)

            with act.Fori(0, 4) as turn:
                for i in range(2):
                    hi(At(C_SOUT + 2 + i, 2, turn))

            def mlp(m, norm, c_up, k_up, c_dn, last):
                n = width(norm)
                norm_hi(norm)

                def up(i, t):
                    k = t + k_up
                    hi(t + (c_up + 2))
                    a(relu[i][:, :, 0:n], linp(k, slice(0, n)), ACT.Relu).then_inc(drained[k.parity], 1)
                    act.wait_ge(drained[k.parity], k.half + 1)
                    at = t.times(2)
                    a(hid_hi[:, bass.ds(at.value, 2), 0:n], relu[i][:, :, 0:n], ACT.Square).then_inc(hh_done, 1)

                for i in range(2):
                    up(i, At(i))
                norm_inv(norm, squared=True)
                with act.Fori(1, 8) as turn:
                    for i in range(2):
                        t = At(i, 2, turn)
                        act.wait_ge(hl_done, (t + (16 * m - 1)).value)
                        up(i, t)
                with act.Fori(0, 3 if last else 4) as turn:
                    for i in range(4):
                        hi(At(c_dn + 2 + i, 4, turn))
                if last:
                    for i in range(2):
                        hi(At(LAST + i))

            mlp(0, 1, C_UP0, K_UP0, C_DN0, False)

            norm_hi(2)
            hi(At(C_MIN + 2))
            hi(At(C_MIN + 3))
            norm_inv(2)
            hi(At(C_MIN + 4))
            for i in range(3):
                k = At(K_MIN + i)
                act.wait_ge(drained[k.parity], k.half + 1)
                a(lat_sq[:, 2 * i:2 * i + 2, :], lat[:, 2 * i:2 * i + 2, :], ACT.Square).then_inc(latsq_done, 1)
            for i, (ps, n) in enumerate(((ps4, 384), (ps5, 256))):
                act.wait_ge(lstat_done, i + 1)
                a(l_ln[:, i, :], ps[:, 0:T], ACT.Ln, bias=eps_t[:, 0:1], scale=1.0 / n).then_inc(l_act, 1)
            for i in range(2):
                act.wait_ge(l_act, i + 1)
                a(l_inv[:, i, :], l_ln[:, i, :], ACT.Exp, scale=-0.5).then_inc(l_act, 1)
            for i in range(5):
                act.wait_ge(latn_done, 1 if i < 3 else 2)
                a(l_hi[:, i, :], lat_n[:, i, :], ACT.Copy, scale=v(V_QA + i)).then_inc(lh_done, 1)

            def unit_raw(s, n):
                c, k = At(C_HEAD + 2 * s + n // 2), At(K_HEAD + 4 * s + n)
                if n % 2 == 0:
                    act.wait_ge(half_done, 2 * s + n // 2 + 1)
                else:
                    act.wait_ge(w_used, (c + 1).value)
                hs = slice(2 * (n % 2), 2 * (n % 2) + 2)
                if n < 2:
                    a(q_sq[:, :, :], linp(k, slice(0, T2), slice(0, QK)), ACT.Square)
                    a(q_pre[0:HD, hs, :], linp(k, slice(0, T2), slice(0, HD)), ACT.Copy,
                      scale=v(V_QG, rows=slice(0, HD))).then_inc(raw_read, 1)
                else:
                    a(k_sq[0:HD, hs, :], linp(k, slice(0, T), slice(0, HD)), ACT.Square)
                    a(k_pre[0:HD, hs, :], linp(k, slice(0, T), slice(0, HD)), ACT.Copy,
                      scale=v(V_KG, rows=slice(0, HD)))
                    a(v_t[HD:P, hs, :], linp(k, slice(0, T), slice(HD, P)), ACT.Copy).then_inc(raw_read, 1)

            def unit_inv(s, n):
                k, un = At(K_HEAD + 4 * s + n), 4 * s + n
                w_ = T2 if n < 2 else T
                act.wait_ge(nsum_done, un + 1)
                if n < 2:
                    a(n_ln[:, :, 0:w_], linp(k, slice(0, w_), slice(0, QK)), ACT.Ln, bias=eps_t[0:QK, 0:1],
                      scale=1.0 / QK).then_inc(drained[k.parity], 1)
                else:
                    hs = slice(2 * (n % 2), 2 * (n % 2) + 2)
                    a(n_ln[:, :, 0:w_], linp(k, slice(0, w_), slice(0, QK)), ACT.Ln, bias=eps_t[0:QK, 0:1],
                      scale=1.0 / QK)
                    a(v_tok[s % 2][:, hs, 1:3, :], linp(k, slice(272, 400)).rearrange("p h (t d) -> p h t d", d=HD),
                      ACT.Copy)
                    a(v_tok[s % 2][0:META, hs, 0, :], linp(k, slice(400, 464), slice(0, META)), ACT.Copy)\
                        .then_inc(drained[k.parity], 1)
                act.wait_ge(drained[k.parity], k.half + 1)
                if un >= 1:
                    act.wait_ge(fin_done, un)
                if n < 2:
                    a(n_inv[:, :, 0:w_], n_ln[:, :, 0:w_], ACT.Exp, scale=-0.5, bias=eps_t[0:QK, 1:2])\
                        .then_inc(ninv_done, 1)
                else:
                    a(n_inv[:, :, 0:w_], n_ln[:, :, 0:w_], ACT.Exp, scale=-0.5).then_inc(ninv_done, 1)

            def exps(s, j):
                n = 4 * s + j
                p = n % 2
                act.wait_ge(nm_done, n + 1)
                a(pr[p][:, 0:144], s_m[p][:, 0:144], ACT.Exp, bias=nmx[p][:, 0:1], accum_out=rsum[p][:, 0:1])
                a(pr[p][:, 144:416], s_m[p][:, 144:416], ACT.Exp, bias=nmx[p][:, 1:2], accum_out=rsum[p][:, 1:2])\
                    .then_inc(ex_done, 1)

            def p_t0_copy(s, j):
                n = 4 * s + j
                act.wait_ge(pT_done, n + 1)
                a(p_t0[:, :], ps4[0:META, 256:512], ACT.Copy).then_inc(pt0_done, 1)

            def o_high(s, q):
                n = 2 * s + q
                act.wait_ge(pv_done, 2 * n + 2)
                a(o_hi[:, n, :], ps4[:, 0:T2], ACT.Copy).then_inc(oh_done, 1)

            for s in range(5):
                proj, att = s < 4, s > 0
                if att:
                    exps(s - 1, 0)
                for n in range(4):
                    if proj:
                        unit_raw(s, n)
                        if n % 2 == 1:
                            hi(At(C_HEAD + 2 * s + n // 2 + 2))
                    if att:
                        if n < 3:
                            exps(s - 1, n + 1)
                        p_t0_copy(s - 1, n)
                        if n % 2 == 1:
                            o_high(s - 1, n // 2)
                    if proj:
                        unit_inv(s, n)

            for i in range(4):
                hi(At(C_MOUT + 2 + i))
            mlp(1, 3, C_UP1, K_UP1, C_DN1, False)

            def exps2(n):
                p = n % 2
                act.wait_ge(nm2_done, n + 1)
                for qt in range(2):
                    ins = a(pr2[p][:, qt * 256:(qt + 1) * 256], s_m2[p][:, qt * 256:(qt + 1) * 256], ACT.Exp,
                            bias=nmx2[p][:, qt:qt + 1], accum_out=rsum2[p][:, qt:qt + 1])
                ins.then_inc(ex2_done, 1)

            def ya_high(q):
                act.wait_ge(pv2_done, 2 * q + 2)
                a(ya_hi[:, q, :], ps4[:, 0:T2], ACT.Copy).then_inc(yah_done, 1)

            norm_hi(4)
            for i in range(20):
                k = At(K_IN2 + i)
                hi(At(C_IN2 + i + 2))
                if i == 0:
                    norm_inv(4)
                if i < 4:
                    act.wait_ge(drained[k.parity], k.half + 1)
                    a(qk_sq[i % 2][:, :, :], qk_r[:, 2 * i:2 * i + 2, :], ACT.Square).then_inc(qksq_done, 1)
                if 1 <= i <= 4:
                    j = i - 1
                    act.wait_ge(qkstat_done, j + 1)
                    if j:
                        act.wait_ge(qkinv_done, j)
                    a(qk_ln[:, :, :].rearrange("p a t -> p (a t)"), (ps5, ps6)[j % 2][:, :], ACT.Ln,
                      bias=eps_t[:, 0:1], scale=1.0 / HD).then_inc(qkln_done, 1)
                    act.wait_ge(qkln_done, j + 1)
                    a(qk_inv[j % 2][:, :, :], qk_ln[:, :, :], ACT.Exp, scale=-0.5,
                      bias=eps_t[:, 2:3] if j < 2 else 0.0).then_inc(qkinv_done, 1)
                if i == 6:
                    act.wait_ge(vT_done, 1)
                    a(v2[:, 0, :], ps7[:, :], ACT.Copy).then_inc(v2_done, 1)
                    a(v2[:, 1, :], ps4[:, :], ACT.Copy).then_inc(v2_done, 1)
                if 6 <= i < 10:
                    j = i - 6
                    act.wait_ge(z_done, j + 1)
                    a(cv2[:, j, :], zc[:, j, 0:T2], ACT.Copy, scale=v(V_CONV2 + 3 * j)).then_inc(cv2_0, 1)
                if 6 <= i < 14:
                    exps2(i - 6)
                if i in (10, 11):
                    j = i - 10
                    act.wait_ge(yb_done, j + 1)
                    a(yb_hi[:, 2 * j:2 * j + 2, :], yb[:, 2 * j:2 * j + 2, :], ACT.Copy).then_inc(ybh_done, 1)
                if i >= 12:
                    j = i - 12
                    act.wait_ge(gclamp, j + 1)
                    sigmoid(gate[:, 2 * j:2 * j + 2, :], gate_step, At(3 * j))
                if 8 <= i < 15 and i % 2 == 0:
                    ya_high((i - 8) // 2)

            for b in range(4):
                hi(At(C_BR + b + 2))
                act.wait_ge(m_done, b + 1)
                a(x_hi[:, 2 * b:2 * b + 2, 0:T2], m_a[:, :, :], ACT.Copy).then_inc(mh_done, 1)
            for i in range(4):
                hi(At(C_WO + 2 + i))
            mlp(2, 5, C_UP2, K_UP2, C_DN2, True)

        @block.vector
        def _(dve):
            tt, ts, stt = nc.vector.tensor_tensor, nc.vector.tensor_scalar, nc.vector.scalar_tensor_tensor

            def lo(c):
                dve.wait_ge(w_hi_done, (c + 1).value)
                tt(w_lo[c.parity][:, :], w_raw[c.parity][:, :], w_hi[c.parity][:, :].bitcast(F32), ALU.subtract)\
                    .then_inc(w_lo_done, 1)

            def norm_lo(norm):
                n, tk = width(norm), tokens(norm)
                for kt in range(KD):
                    dve.wait_ge(xh_done, KD * norm + kt + 1)
                    stt(x_lo[:, kt, 0:n], h[:, kt, tk], gain(norm, kt), x_hi[:, kt, 0:n].bitcast(F32),
                        ALU.mult, ALU.subtract).then_inc(xl_done, 1)

            dve.memset(eps_t[:, 0:1], EPS).then_inc(memset_done, 1)
            dve.memset(eps_t[:, 1:2], float(np.log(QK ** -0.5))).then_inc(memset_done, 1)
            dve.memset(eps_t[:, 2:3], float(np.log(HD ** -0.5))).then_inc(memset_done, 1)
            dve.memset(u[:, :, 0:3], 0.0).then_inc(memset_done, 1)
            dve.wait_ge(small_in, 32)
            norm_lo(0)
            lo(At(0))
            lo(At(1))
            k = At(K_DT)
            r32 = slice(0, 32)
            dve.wait_ge(w_used, 1)
            dve.wait_ge(r_done, 1)
            tt(dtx[:, :], lin[r32, 0, 0:T], r_inv[r32, :], ALU.mult).then_inc(drained[0], 1)
            dve.wait_ge(drained[0], 1)
            ts(dtb[:, :], dtx[:, :], v(V_DTB, rows=r32), None, ALU.add).then_inc(dt_dve, 1)
            dve.wait_ge(dt_dve, 1)
            ts(dtx[:, :], dtb[:, :], -1.0, None, ALU.mult).then_inc(dt_dve, 1)
            dve.wait_ge(dt_dve, 2)
            tt(dta[:, :], dtb[:, :], dtx[:, :], ALU.max).then_inc(dt_dve, 1)
            lo(At(2))
            dve.wait_ge(dt_act, 3)
            stt(dt_t[:, :], dtb[:, :], 0.0, dta[:, :], ALU.max, ALU.add).then_inc(dt_dve, 1)
            dve.wait_ge(dt_dve, 4)
            ts(dtx[:, :], dt_t[:, :], a_exp[:, 0:1], -1.0, ALU.mult, ALU.mult).then_inc(dt_dve, 1)
            dve.wait_ge(dt_dve, 5)
            nc.vector.tensor_tensor_scan(acs[:, :], cst[r32, N_ONES:N_ONES + 1].broadcast_to([32, T]), dtx[:, :],
                                         0.0, ALU.mult, ALU.add).then_inc(dt_dve, 1)

            def dt_columns():
                dve.wait_ge(dtT_done, 1)
                src = ps4[:, 0:192].rearrange("p (i s h) -> p i s h", i=2, s=3)
                dst = cols[:, :, :].rearrange("p (i s) h -> p i s h", i=2)
                nc.vector.tensor_copy(dst[:, :, 0:2, :], src[:, :, 0:2, :]).then_inc(cols_done, 1)
                nc.vector.tensor_copy(dst[0:META, :, 2, :], src[0:META, :, 2, :]).then_inc(cols_done, 1)

            def evac_u(s, pair):
                c, k = s.times(3, C_GRP + pair), s.times(3, K_GRP + pair)
                dve.wait_ge(w_used, (c + 1).value)
                tt(u[:, 2 * pair:2 * pair + 2, 3:3 + T], linp(k, slice(0, T)), over(r_inv[:, :], 2), ALU.mult)\
                    .then_inc(drained[k.parity], 1)

            def conv(s, pair):
                for tap in (1, 2, 3):
                    for i in range(2):
                        q = 2 * pair + i
                        if tap == 1:
                            dve.wait_ge(cv0_done, s.times(4, q + 1).value)
                        else:
                            dve.wait_ge(cv_step, s.times(12, 6 * pair + 2 * (tap - 2) + i + 1).value)
                        stt(cv[:, q, :], u[:, q, tap:tap + T], v(s.times(20, V_CONV + 5 * q + tap).value), cv[:, q, :],
                            ALU.mult, ALU.add).then_inc(cv_step, 1)

            def clamp(dst, x):
                ts(dst, x, CLAMP, None, ALU.max).then_inc(clamped, 1)

            def silu(s, n, dst, x, sgm):
                dve.wait_ge(sg_step, s.times(9, 3 * (n + 1)).value)
                tt(dst, x, sgm, ALU.mult).then_inc(silu_done, 1)

            def head_diff(g, j):
                h_at = g.times(4, j)
                for s, (rows, at, l0) in enumerate(((P, 0, 0), (P, T, 128), (META, 416, 256))):
                    n = T - l0
                    ins = ts(dd[0:rows, j, at:at + n], acs_bc[g.parity][0:rows, j, l0:T],
                             cols[0:rows, 3 + s, bass.ds(h_at.value, 1)], 0.0, ALU.subtract, ALU.min)
                ins.then_inc(dd_done, 1)

            def head_mix(g, j):
                h_at = g.times(4, j)
                dve.wait_ge(ee_done, (h_at + 1).value)
                for s, (rows, at, n) in enumerate(((P, 0, T), (P, T, 144), (META, 416, 16))):
                    ins = stt(mm[0:rows, j, at:at + n], dd[0:rows, j, at:at + n],
                              cols[0:rows, s, bass.ds(h_at.value, 1)], cbm[0:rows, at:at + n], ALU.mult, ALU.mult)
                ins.then_inc(mm_done, 1)

            def slot(s, has_lin=True, has_scan=True, has_stat=True, first=False):
                c = s.times(3, C_GRP)
                g, gs = s + (-1), s + (-2)
                if has_stat:
                    if gs.base:
                        dve.wait_ge(gl_done, gs.times(2).value)
                    for q in range(2):
                        dve.wait_ge(y_done, gs.times(2, q + 1).value)
                        stt(y1[:, q, :], xs_s[gs.parity][:, q, :], v(gs.times(2, V_DSKIP + q).value),
                            (ps6, ps7)[q][:, 0:T], ALU.mult, ALU.add).then_inc(y_read, 1)
                    dve.wait_ge(y_read, gs.times(2, 2).value)
                    dve.wait_ge(silu_done, gs.times(3, 3).value)
                    tt(y2[:, :, :], y1[:, :, :], z_s[gs.parity][:, :, :], ALU.mult).then_inc(y2_done, 1)
                if has_lin:
                    lo(c + 2)
                    evac_u(s, 0)
                    conv(s, 0)
                    dve.wait_ge(cv_step, s.times(12, 6).value)
                    clamp(sg[:, 0:2, :], cv[:, 0:2, :])
                if first:
                    dt_columns()
                if has_scan:
                    dve.wait_ge(cb_done, (g + 1).value)
                    tt(cbm[:, 0:416], ps5[:, 0:416], cst[:, N_SSD:N_SSD + 416], ALU.mult)
                    tt(cbm[0:META, 416:432], ps5[0:META, 416:432], cst[0:META, N_SSD + 416:N_SSD + 432], ALU.mult)\
                        .then_inc(cbm_done, 1)
                    dve.wait_ge(acs_in[g.parity], (g.half + 1) * 16)
                    if g.base == 0:
                        dve.wait_ge(cols_done, 2)
                    for j in range(HPG):
                        head_diff(g, j)
                    dve.wait_ge(cbm_done, (g + 1).value)
                    for j in range(2):
                        head_mix(g, j)
                if has_lin:
                    lo(c + 3)
                    evac_u(s, 1)
                    conv(s, 1)
                    dve.wait_ge(cv_step, s.times(12, 12).value)
                    clamp(sg[:, 2:4, :], cv[:, 2:4, :])
                if has_stat:
                    dve.wait_ge(ginv_done, (gs + 1).value)
                    tt(y1[:, :, :], y2[:, :, :], over(g_inv[:, :], 2), ALU.mult).then_inc(y3_done, 1)
                if has_lin:
                    silu(s, 0, xs_s[s.parity][:, :, :], cv[:, 0:2, :], sg[:, 0:2, :])
                if has_scan:
                    for j in range(2, HPG):
                        head_mix(g, j)
                if has_stat:
                    for q in range(2):
                        t = gs.times(2, q)
                        dve.wait_ge(gh_done, (t + 1).value)
                        stt(g_lo[:, t.value, :], y1[:, q, :], v((t + V_SNORM).value),
                            g_hi[:, t.value, :].bitcast(F32), ALU.mult, ALU.subtract).then_inc(gl_done, 1)
                if has_lin:
                    k = s.times(3, K_GRP + 2)
                    lo(c + 4)
                    dve.wait_ge(w_used, (c + 3).value)
                    tt(z_raw[:, :, :], linp(k, slice(0, T)), over(r_inv[:, :], 2), ALU.mult)\
                        .then_inc(drained[k.parity], 1)
                    dve.wait_ge(drained[k.parity], k.half + 1)
                    clamp(z_sg[:, :, :], z_raw[:, :, :])
                    silu(s, 1, bc_s[:, :, :], cv[:, 2:4, :], sg[:, 2:4, :])
                    silu(s, 2, z_s[s.parity][:, :, :], z_raw[:, :, :], z_sg[:, :, :])

            slot(At(0), has_scan=False, has_stat=False, first=True)
            slot(At(1), has_stat=False)
            with dve.Fori(0, SLOT_TURNS) as turn:
                for i in range(2):
                    slot(At(2 + i, 2, turn))
            slot(At(8), has_lin=False)
            slot(At(9), has_lin=False, has_scan=False)

            with dve.Fori(0, 4) as turn:
                for i in range(2):
                    t = At(i, 2, turn)
                    c, k = t + C_SOUT, t + K_SOUT
                    lo(c + 2)
                    dve.wait_ge(w_used, (c + 1).value)
                    tt(h[:, t.value, :], h[:, t.value, :], lin[:, 2 * k.parity, 0:T], ALU.add)\
                        .then_inc(drained[k.parity], 1)

            def mlp(m, norm, c_up, c_dn, k_dn, last):
                n, tk = width(norm), tokens(norm)
                norm_lo(norm)

                def up(i, t):
                    lo(t + (c_up + 2))
                    k = t + (K_UP0, K_UP1, K_UP2)[m]
                    dve.wait_ge(drained[k.parity], k.half + 1)
                    tt(relu_sq[i][:, :, 0:n], relu[i][:, :, 0:n], relu[i][:, :, 0:n], ALU.mult).then_inc(rsq_done, 1)
                    dve.wait_ge(hh_done, (t + (16 * m + 1)).value)
                    dve.wait_ge(rsq_done, (t + (16 * m + 1)).value)
                    at = t.times(2)
                    tt(hid_lo[:, bass.ds(at.value, 2), 0:n], relu_sq[i][:, :, 0:n],
                       hid_hi[:, bass.ds(at.value, 2), 0:n].bitcast(F32), ALU.subtract).then_inc(hl_done, 1)

                with dve.Fori(0, 8) as turn:
                    for i in range(2):
                        up(i, At(i, 2, turn))

                def down(i, t, lows):
                    for half in range(2):
                        c = t.times(2, c_dn + half)
                        if lows:
                            lo(c + 2)
                    k = t + k_dn
                    dve.wait_ge(w_used, (c + 1).value)
                    tt(down_r[i][:, 0:n], lin[:, 2 * k.parity, 0:n], r_inv[:, 0:n], ALU.mult)\
                        .then_inc(drained[k.parity], 1)
                    dve.wait_ge(drained[k.parity], k.half + 1)
                    tt(h[:, t.value, tk], h[:, t.value, tk], down_r[i][:, 0:n], ALU.add).then_inc(h_mlp, 1)

                dve.wait_ge(r_done, norm + 1)
                with dve.Fori(0, 3 if last else 4) as turn:
                    for i in range(2):
                        down(i, At(i, 2, turn), True)
                if last:
                    down(0, At(6), True)
                    down(1, At(7), False)

            mlp(0, 1, C_UP0, C_DN0, K_DN0, False)

            norm_lo(2)
            for i in range(3):
                k = At(K_MIN + i)
                lo(At(C_MIN + i + 2))
                dve.wait_ge(w_used, C_MIN + i + 1)
                dve.wait_ge(r_done, 3)
                tt(lat[:, 2 * i:2 * i + 2, :], linp(k, slice(0, T)), over(r_inv[:, :], 2), ALU.mult)\
                    .then_inc(drained[k.parity], 1)
            k = At(K_MIN + 2)
            dve.wait_ge(drained[k.parity], k.half + 1)
            dve.wait_ge(rope_done, 2)
            rr, rs_ = slice(HD, QK), slice(QK, P)
            tt(rot_a[rr, 0, :], lat[rr, 5, :], rope_k[rr, :], ALU.mult).then_inc(krope, 1)
            tt(rot_b[rr, 0, :], lat[rs_, 5, :], rope_k[rs_, :], ALU.mult).then_inc(krope, 1)
            dve.wait_ge(krope, 2)
            tt(k_pre[rr, :, :], over(rot_a[rr, 0, :], 4), over(rot_b[rr, 0, :], 4), ALU.add).then_inc(krope, 1)
            tt(k_sq[rr, :, :], over(lat[rr, 5, :], 4), over(lat[rr, 5, :], 4), ALU.mult).then_inc(krope, 1)
            dve.wait_ge(l_act, 3)
            tt(lat_n[:, 0:3, :], lat[:, 0:3, :], over(l_inv[:, 0, :], 3), ALU.mult).then_inc(latn_done, 1)
            dve.wait_ge(l_act, 4)
            tt(lat_n[:, 3:5, :], lat[:, 3:5, :], over(l_inv[:, 1, :], 2), ALU.mult).then_inc(latn_done, 1)
            for i in range(5):
                dve.wait_ge(lh_done, i + 1)
                if i == 0:
                    dve.wait_ge(latn_done, 2)
                stt(l_lo[:, i, :], lat_n[:, i, :], v(V_QA + i), l_hi[:, i, :].bitcast(F32), ALU.mult, ALU.subtract)\
                    .then_inc(ll_done, 1)

            def rotate(s, n):
                k = At(K_HEAD + 4 * s + n)
                un = 2 * s + n
                dve.wait_ge(raw_read, 4 * s + n + 1)
                tq = slice(META, T)
                tt(rot_a[rr, :, 0:T2], linp(k, slice(0, T2), rr), over(rope_q[rr, tq], 2), ALU.mult)\
                    .then_inc(rot_done, 1)
                tt(rot_b[rr, :, 0:T2], linp(k, slice(0, T2), rs_), over(rope_q[rs_, tq], 2), ALU.mult)\
                    .then_inc(rot_done, 1)
                dve.wait_ge(rot_done, 2 * un + 2)
                tt(q_pre[rr, 2 * n:2 * n + 2, :], rot_a[rr, :, 0:T2], rot_b[rr, :, 0:T2], ALU.add).then_inc(rot_sum, 1)

            def finish(s, n):
                un = 4 * s + n
                dve.wait_ge(ninv_done, un + 1)
                hs = slice(2 * (n % 2), 2 * (n % 2) + 2)
                if n < 2:
                    dve.wait_ge(rot_sum, 2 * s + n + 1)
                    ins = tt(q_fin[s % 2][:, hs, :], q_pre[:, hs, :], n_inv[:, :, 0:T2], ALU.mult)
                else:
                    if s == 0:
                        dve.wait_ge(krope, 3)
                    ins = tt(k_fin[s % 2][:, hs, :], k_pre[:, hs, :], n_inv[:, :, :], ALU.mult)
                ins.then_inc(fin_done, 1)

            def maxima(s, j):
                n = 4 * s + j
                p, o = n % 2, (ps5, ps6)[n % 2]
                dve.wait_ge(s_done, n + 1)
                for i, sl in enumerate((slice(0, 144), slice(144, 416))):
                    ins = nc.vector.tensor_tensor_reduce(
                        out=s_m[p][:, sl], in0=o[:, sl], in1=cst[:, N_MLA + sl.start:N_MLA + sl.stop], scale=1.0,
                        scalar=-3e38, op0=ALU.add, op1=ALU.max, accum_out=mx[p][:, i:i + 1])
                ins.then_inc(sm_done, 1)
                dve.wait_ge(sm_done, n + 1)
                ts(nmx[p][:, :], mx[p][:, :], -1.0, None, ALU.mult).then_inc(nm_done, 1)

            def weigh(s, j):
                n = 4 * s + j
                p = n % 2
                dve.wait_ge(ex_done, n + 1)
                nc.vector.reciprocal(rinv[p][:, :], rsum[p][:, :]).then_inc(ri_done, 1)
                dve.wait_ge(ri_done, n + 1)
                ts(pr[p][:, 0:144], pr[p][:, 0:144], rinv[p][:, 0:1], None, ALU.mult)
                ts(pr[p][:, 144:416], pr[p][:, 144:416], rinv[p][:, 1:2], None, ALU.mult).then_inc(p_done, 1)

            def p_t_copy(s, j):
                n = 4 * s + j
                dve.wait_ge(pT_done, n + 1)
                nc.vector.tensor_copy(p_t[:, :], ps7[:, 0:384]).then_inc(pt_done, 1)

            def o_low(s, q):
                n = 2 * s + q
                dve.wait_ge(oh_done, n + 1)
                tt(o_lo[:, n, :], ps4[:, 0:T2], o_hi[:, n, :].bitcast(F32), ALU.subtract).then_inc(ol_done, 1)

            for s in range(5):
                proj, att = s < 4, s > 0
                if att:
                    maxima(s - 1, 0)
                for n in range(4):
                    if proj:
                        if n < 2:
                            rotate(s, n)
                        if n % 2 == 1:
                            lo(At(C_HEAD + 2 * s + n // 2 + 2))
                    if att:
                        if n < 3:
                            maxima(s - 1, n + 1)
                        weigh(s - 1, n)
                        p_t_copy(s - 1, n)
                        if n % 2 == 1:
                            o_low(s - 1, n // 2)
                    if proj:
                        finish(s, n)

            def add_pair(c, k, i):
                lo(c + 2)
                dve.wait_ge(w_used, (c + 1).value)
                tt(h[:, 2 * i:2 * i + 2, META:T], h[:, 2 * i:2 * i + 2, META:T], linp(k, slice(0, T2)), ALU.add)\
                    .then_inc(drained[k.parity], 1)

            for i in range(4):
                add_pair(At(C_MOUT + i), At(K_MOUT + i), i)
            mlp(1, 3, C_UP1, C_DN1, K_DN1, False)

            def maxima2(n):
                p, o = n % 2, (ps5, ps6)[n % 2]
                dve.wait_ge(s2_done, n + 1)
                if n == 0:
                    dve.wait_ge(bias_done, 16)
                for qt in range(2):
                    sl = slice(qt * 256, (qt + 1) * 256)
                    ins = nc.vector.tensor_tensor_reduce(
                        out=s_m2[p][:, sl], in0=o[:, sl], in1=bias_mask[:, n, qt, :], scale=1.0,
                        scalar=-3e38, op0=ALU.add, op1=ALU.max, accum_out=mx2[p][:, qt:qt + 1])
                ins.then_inc(sm2_done, 1)
                dve.wait_ge(sm2_done, n + 1)
                ts(nmx2[p][:, :], mx2[p][:, :], -1.0, None, ALU.mult).then_inc(nm2_done, 1)

            def weigh2(n):
                p = n % 2
                dve.wait_ge(ex2_done, n + 1)
                nc.vector.reciprocal(rinv2[p][:, :], rsum2[p][:, :]).then_inc(ri2_done, 1)
                dve.wait_ge(ri2_done, n + 1)
                for qt in range(2):
                    sl = slice(qt * 256, (qt + 1) * 256)
                    ins = ts(pr2[p][:, sl], pr2[p][:, sl], rinv2[p][:, qt:qt + 1], None, ALU.mult)
                ins.then_inc(p2_done, 1)

            norm_lo(4)
            for i in range(20):
                c, k = At(C_IN2 + i), At(K_IN2 + i)
                lo(c + 2)
                dve.wait_ge(w_used, (c + 1).value)
                if i == 0:
                    dve.wait_ge(r_done, 5)
                if i < 4:
                    dst = qk_r[:, 2 * i:2 * i + 2, :]
                elif i < 6:
                    dst = v_r[:, 2 * (i - 4):2 * (i - 4) + 2, :]
                elif i < 10:
                    dst = cc_ch[:, :, :]
                elif i < 12:
                    dst = cb_r[:, 2 * (i - 10):2 * (i - 10) + 2, :]
                else:
                    dst = gate[:, 2 * (i - 12):2 * (i - 12) + 2, :]
                tt(dst, linp(k, slice(0, T2)), over(r_inv[:, 0:T2], 2), ALU.mult).then_inc(drained[k.parity], 1)
                if i == 0:
                    dve.memset(zc[:, :, 0:1], 0.0)
                    dve.memset(zc[:, :, T2 + 1:T2 + 2], 0.0)
                if 1 <= i <= 4:
                    j = i - 1
                    dve.wait_ge(qkinv_done, j + 1)
                    for q in range(2):
                        ins = stt(qk_f[:, 2 * j + q, :], qk_r[:, 2 * j + q, :], v(V_QN2 if j < 2 else V_KN2),
                                  qk_inv[j % 2][:, q, :], ALU.mult, ALU.mult)
                    ins.then_inc(qkf_done, 1)
                if 6 <= i < 10:
                    j = i - 6
                    dve.wait_ge(drained[k.parity], k.half + 1)
                    tt(zc[:, j, 1:T2 + 1], cc_ch[:, 0, :], cc_ch[:, 1, :], ALU.mult).then_inc(z_done, 1)
                    for tap in (1, 2):
                        if tap == 1:
                            dve.wait_ge(cv2_0, j + 1)
                            dve.wait_ge(z_done, j + 1)
                        else:
                            dve.wait_ge(cv2_step, 2 * j + 1)
                        stt(cv2[:, j, :], zc[:, j, tap:tap + T2], v(V_CONV2 + 3 * j + tap), cv2[:, j, :],
                            ALU.mult, ALU.add).then_inc(cv2_step, 1)
                if 6 <= i < 14:
                    maxima2(i - 6)
                if 7 <= i < 15:
                    n = i - 7
                    dve.wait_ge(pT2_done, n + 1)
                    nc.vector.tensor_copy(p_t2[:, :], ps7[:, :]).then_inc(pt2_done, 1)
                if 6 <= i < 14:
                    weigh2(i - 6)
                if i in (10, 11):
                    j = i - 10
                    dve.wait_ge(drained[k.parity], k.half + 1)
                    dve.wait_ge(cv2_step, 8)
                    tt(yb[:, 2 * j:2 * j + 2, :], cv2[:, 2 * j:2 * j + 2, :], cb_r[:, 2 * j:2 * j + 2, :], ALU.mult)\
                        .then_inc(yb_done, 1)
                    dve.wait_ge(ybh_done, j + 1)
                    dve.wait_ge(yb_done, j + 1)
                    tt(yb_lo[:, 2 * j:2 * j + 2, :], yb[:, 2 * j:2 * j + 2, :],
                       yb_hi[:, 2 * j:2 * j + 2, :].bitcast(F32), ALU.subtract).then_inc(ybl_done, 1)
                if 8 <= i < 15 and i % 2 == 0:
                    q = (i - 8) // 2
                    dve.wait_ge(yah_done, q + 1)
                    tt(ya_lo[:, q, :], ps4[:, 0:T2], ya_hi[:, q, :].bitcast(F32), ALU.subtract).then_inc(yal_done, 1)

            for b in range(4):
                c = At(C_BR + b)
                lo(c + 2)
                for n, dst in enumerate((m_a, m_b)):
                    k = At(K_BR + 2 * b + n)
                    dve.wait_ge(*((half_done, 8 + b + 1) if n == 0 else (w_used, (c + 1).value)))
                    dve.wait_ge(gate_step, min(24, 3 * (2 * b + 2)))
                    if n == 0 and b:
                        dve.wait_ge(ml_done, b)
                    tt(dst[:, :, :], linp(k, slice(0, T2)), gate[:, 4 * b + n:4 * b + n + 3:2, :], ALU.mult)\
                        .then_inc(drained[k.parity], 1)
                for n in range(2):
                    k = At(K_BR + 2 * b + n)
                    dve.wait_ge(drained[k.parity], k.half + 1)
                tt(m_a[:, :, :], m_a[:, :, :], m_b[:, :, :], ALU.add).then_inc(m_done, 1)
                dve.wait_ge(m_done, b + 1)
                dve.wait_ge(mh_done, b + 1)
                tt(x_lo[:, 2 * b:2 * b + 2, 0:T2], m_a[:, :, :], x_hi[:, 2 * b:2 * b + 2, 0:T2].bitcast(F32),
                   ALU.subtract).then_inc(ml_done, 1)
            for i in range(4):
                add_pair(At(C_WO + i), At(K_WO + i), i)
            mlp(2, 5, C_UP2, C_DN2, K_DN2, True)

        @block.gpsimd
        def _(pool):
            tt, ts = nc.gpsimd.tensor_tensor, nc.gpsimd.tensor_scalar

            def norm_sum(norm):
                n = width(norm)
                pool.wait_ge(hsq_done, norm + 1)
                for i, m in enumerate((4, 2, 1)):
                    if i:
                        pool.wait_ge(pool_memset, 2 * norm + i)
                    tt(h_sq[:, 0:m, 0:n], h_sq[:, 0:m, 0:n], h_sq[:, m:2 * m, 0:n], ALU.add)\
                        .then_inc(pool_memset if m > 1 else hsum_done, 1)

            for rq in range(4):
                pool.dma_start(bias_mask[(rq % 2) * 64:(rq % 2 + 1) * 64, :, rq // 2, :], rpb[:, :, 3 - rq:7 - rq, :]
                               .rearrange("q h r c -> q h (r c)")).then_inc(rpb_in, 16)
            norm_sum(0)
            pool.wait_ge(dt_dve, 6)
            pool.dma_start(acs_dram, acs[:, :]).then_inc(acs_out, 16)
            pool.wait_ge(acs_out, 16)

            def acs_rows(g):
                src = acs_dram[bass.ds(g.times(4).value, 4), :].partition_broadcast(P)
                pool.dma_start(acs_bc[g.parity][:, :, :], src).then_inc(acs_in[g.parity], 16)

            acs_rows(At(0))
            acs_rows(At(1))

            def slot(s, has_lin=True, has_scan=True, has_stat=True, load=True):
                g, gs = s + (-1), s + (-2)
                if has_stat:
                    pool.wait_ge(ysq_done, (gs + 1).value)
                    tt(y_sum[:, :], h_sq[:, 0, :], h_sq[:, 1, :], ALU.add).then_inc(ysum_done, 1)
                if has_scan and load:
                    pool.wait_ge(dd_done, g.times(4, 4).value)
                    acs_rows(g + 2)

            slot(At(1), has_stat=False)
            with pool.Fori(0, 2) as turn:
                for i in range(2):
                    slot(At(2 + i, 2, turn))
            slot(At(6))
            slot(At(7), load=False)
            slot(At(8), has_lin=False, load=False)
            slot(At(9), has_lin=False, has_scan=False)

            norm_sum(1)
            pool.wait_ge(rpb_in, 16 * 4)
            pool.wait_ge(small_in, 32)
            for hd in range(NA_HEADS):
                for qt in range(2):
                    b = bias_mask[:, hd, qt, :].rearrange("p (r c) -> p r c", c=64)
                    tt(b, b, over(cst[:, N_NA:N_NA + 64], 4), ALU.add).then_inc(bias_done, 1)
            norm_sum(2)
            pool.wait_ge(stat_done, 3)
            tb = slice(HD, P)
            ts(rope_q[tb, :], cst[tb, N_ROPE:N_ROPE + T], v(V_QG, rows=tb), None, ALU.mult).then_inc(rope_done, 1)
            ts(rope_k[tb, :], cst[tb, N_ROPE:N_ROPE + T], v(V_KG, rows=tb), None, ALU.mult).then_inc(rope_done, 1)
            norm_sum(3)
            norm_sum(4)
            for j in range(8):
                k = At(K_IN2 + 12 + j)
                pool.wait_ge(drained[k.parity], k.half + 1)
                gt = gate[:, 2 * j:2 * j + 2, :]
                ts(gt, gt, CLAMP, None, ALU.max).then_inc(gclamp, 1)
            norm_sum(5)


def constants():
    c = np.zeros((P, N_CONST), np.float32)
    p = np.arange(P)
    c[:, N_IDENT:N_IDENT + P] = np.eye(P)
    c[:, N_ONES:N_ONES + P] = 1.0
    c[:, N_BLK:N_BLK + P] = (p[:, None] // HD) == (p[None, :] // HD)
    tok = np.arange(T)
    c[:, N_SSD:N_SSD + T] = tok[None, :] >= p[:, None]
    c[:, N_SSD + T:N_SSD + 416] = tok[None, 128:] >= 128 + p[:, None]
    c[:META, N_SSD + 416:N_SSD + 432] = tok[None, 256:] >= 256 + p[:META, None]
    c[:, N_MLA:N_MLA + 144] = np.where(tok[None, :144] <= META + p[:, None], 0.0, NEG)
    c[:, N_MLA + 144:N_MLA + 416] = np.where(tok[None, :] <= 144 + p[:, None], 0.0, NEG)
    inv = (1.0 / (np.float32(10000.0) ** (np.arange(0, 32, 2, dtype=np.float32) / np.float32(32)))).astype(np.float32)
    ang = (tok.astype(np.float32)[None, :] * inv[:, None]).astype(np.float32)
    cos, sin = np.cos(ang), np.sin(ang)
    c[HD:QK, N_ROPE:N_ROPE + T] = np.concatenate([cos, cos])
    c[QK:P, N_ROPE:N_ROPE + T] = np.concatenate([-sin, sin])
    qc, kc = (p % 64)[:, None], np.arange(64)[None, :]
    start = np.clip(qc - 8, 0, 48)
    c[:, N_NA:N_NA + 64] = np.where((kc >= start) & (kc < start + 16), 0.0, NEG)
    return c


def chunk(*parts):
    flat = [m.reshape(m.shape[0] // P, P, m.shape[1]).transpose(1, 0, 2).reshape(P, -1) for m in parts]
    row = np.concatenate(flat, axis=1)
    return np.pad(row, ((0, 0), (0, CHUNK - row.shape[1])))


def pad_cols(m, before, after):
    return np.pad(m, ((0, 0), (before, after)))


def weight_stream(i):
    w = []
    s = i["ssd_w_in"][0]
    z, xs, b, c, dt = s[:, 0:2048], s[:, 2048:4096], s[:, 4096:5120], s[:, 5120:6144], s[:, 6144:6176]
    w.append(chunk(pad_cols(dt, 0, 224)))
    for g in range(GROUPS):
        w.append(chunk(xs[:, 256 * g:256 * g + 256]))
        w.append(chunk(np.concatenate([b[:, P * g:P * g + P], c[:, P * g:P * g + P]], 1)))
        w.append(chunk(z[:, 256 * g:256 * g + 256]))
    for t in range(8):
        w.append(chunk(i["ssd_w_out"][0][:, P * t:P * t + P]))

    def mlp(up, down):
        for t in range(16):
            w.append(chunk(up[:, 256 * t:256 * t + 256]))
        for t in range(8):
            for half in range(2):
                w.append(chunk(down[2048 * half:2048 * half + 2048, P * t:P * t + P]))

    mlp(i["mlp_w_up"][0], i["mlp_w_down"][0])
    m = i["mla_w_in"][0]
    kpe = m[:, 640:672]
    m = np.concatenate([m[:, 0:640], pad_cols(kpe, 64, 0), kpe[:, 16:32], kpe[:, 0:16]], 1)
    for t in range(3):
        w.append(chunk(m[:, 256 * t:256 * t + 256]))
    q = i["mla_w_q_b"][0].reshape(384, MLA_HEADS, QK)
    q = np.concatenate([q, q[:, :, 80:96], q[:, :, 64:80]], 2).reshape(384, MLA_HEADS * P)
    for s4 in range(4):
        w.append(chunk(q[:, 512 * s4:512 * s4 + 512]))
        w.append(chunk(i["mla_w_kv_b"][0][:, 512 * s4:512 * s4 + 512]))
    for t in range(4):
        w.append(chunk(i["mla_w_out"][0][:, 256 * t:256 * t + 256]))
    mlp(i["mlp_w_up"][1], i["mlp_w_down"][1])
    n = i["w_in_2"][0]
    for t in range(6):
        w.append(chunk(n[:, 256 * t:256 * t + 256]))
    cb, cc, ch, ga, gb = n[:, 1536:2048], n[:, 2048:2560], n[:, 2560:3072], n[:, 3072:4096], n[:, 4096:5120]
    for t in range(4):
        w.append(chunk(np.concatenate([cc[:, P * t:P * t + P], ch[:, P * t:P * t + P]], 1)))
    for t in range(2):
        w.append(chunk(cb[:, 256 * t:256 * t + 256]))
    for t in range(8):
        w.append(chunk(np.concatenate([ga[:, P * t:P * t + P], gb[:, P * t:P * t + P]], 1)))
    for t in range(4):
        w.append(chunk(i["w_attn_branch_2"][0][:, 256 * t:256 * t + 256],
                       i["w_conv_branch_2"][0][:, 256 * t:256 * t + 256]))
    for t in range(4):
        w.append(chunk(i["w_o_2"][0][:, 256 * t:256 * t + 256]))
    mlp(i["w_mlp_in_2"][0], i["w_mlp_out_2"][0])
    assert len(w) == N_CHUNKS
    return np.stack(w)


def small_params(i):
    vec = np.zeros((P, N_VEC), np.float32)

    def tiles(x):
        return x.reshape(-1, P).T

    gains = (i["ln_mix"][0], i["ln_mlp"][0], i["ln_mix"][1], i["ln_mlp"][1], i["norm1_g_2"][0], i["norm2_g_2"][0])
    for n, g in enumerate(gains):
        vec[:, V_GAIN + n * KD:V_GAIN + (n + 1) * KD] = tiles(g)
    cw, cb = i["ssd_conv_w"][0], i["ssd_conv_b"][0]
    for g in range(GROUPS):
        for q, t in enumerate((2 * g, 2 * g + 1, 16 + g, 24 + g)):
            at = V_CONV + (g * 4 + q) * 5
            vec[:, at:at + 4] = cw[:, P * t:P * t + P].T
            vec[:, at + 4] = cb[P * t:P * t + P]
    vec[:, V_DSKIP:V_DSKIP + 16] = tiles(np.repeat(i["ssd_d"][0], HD))
    vec[:, V_SNORM:V_SNORM + 16] = tiles(i["ssd_norm"][0])
    vec[:, V_QA:V_QA + 3] = tiles(i["mla_q_a_norm"][0])
    vec[:, V_KVA:V_KVA + 2] = tiles(i["mla_kv_a_norm"][0])
    for col, g in ((V_QG, i["mla_q_norm"][0]), (V_KG, i["mla_k_norm"][0])):
        vec[:, col] = np.concatenate([g, g[80:96], g[64:80]])
    for t in range(4):
        vec[:, V_CONV2 + 3 * t:V_CONV2 + 3 * t + 3] = i["conv_w_2"][0][:, P * t:P * t + P].T
    vec[:, V_QN2] = np.tile(i["q_norm_g_2"][0], 2)
    vec[:, V_KN2] = np.tile(i["k_norm_g_2"][0], 2)
    vec[0:32, V_DTB] = i["ssd_dt_bias"][0]
    vec[0:32, V_ALOG] = i["ssd_a_log"][0]
    return vec


def kernel(**inputs):
    import concourse.bacc as bacc
    from concourse.bass_utils import run_bass_kernel_spmd

    i = {name: np.asarray(a) for name, a in inputs.items()}
    tokens = np.concatenate([i["meta_tokens"], i["x"][0]], axis=0)
    padded = np.pad(i["rpb_2"][0][:, 4:11, :], ((0, 0), (0, 0), (48, 48)))
    rpb = np.stack([padded[:, :, 63 - qc:127 - qc] for qc in range(64)])
    arrays = {
        "w": weight_stream(i),
        "h0": np.ascontiguousarray(tokens.T.reshape(KD, P, T).transpose(1, 0, 2)),
        "vec": small_params(i),
        "const": constants(),
        "rpb": np.ascontiguousarray(rpb),
    }
    nc = bacc.Bacc("TRN2", target_bir_lowering=False, num_devices=1)
    aps = {n: nc.dram_tensor(n, a.shape, mybir.dt.from_np(a.dtype), kind="ExternalInput").ap()
           for n, a in arrays.items()}
    out = nc.dram_tensor("out", (P, KD, SEQ), F32, kind="ExternalOutput").ap()
    acs_dram = nc.dram_tensor("acs_dram", (32, T), F32, kind="Internal").ap()
    build(nc, aps["w"], aps["h0"], aps["vec"], aps["const"], aps["rpb"], out, acs_dram)
    r = run_bass_kernel_spmd(nc, [arrays], core_ids=[0])
    o = r.results[0]["out"]
    return np.ascontiguousarray(o.transpose(1, 0, 2).reshape(D, SEQ).T)[None]
```

```python
import numpy as np
from contextlib import ExitStack
import concourse.bass as bass
from concourse import mybir
from concourse.alu_op_type import AluOpType as ALU

F32 = mybir.dt.float32
F32R = mybir.dt.float32r
ACT = mybir.ActivationFunctionType

P = 128
D = 1024
KD = D // P
META = 16
SEQ = 256
T = META + SEQ
T2 = SEQ
EPS = 1e-6
GROUPS = 8
HPG = 4
HD = 64
FF_TILES = 32
PAGE = 8 * P
SLOTS = 4
MLA_HEADS = 16
QK = 96
NA_HEADS = 8
MLA_STEPS = MLA_HEADS + 8
NEG = -1e30
CLAMP = -44.0

C_DT = 0
C_GRP = C_DT + 1
C_SOUT = C_GRP + 3 * GROUPS
C_UP0 = C_SOUT + 8
C_DN0 = C_UP0 + 16
C_MIN = C_DN0 + 16
C_HEAD = C_MIN + 3
C_MOUT = C_HEAD + 8
C_UP1 = C_MOUT + 4
C_DN1 = C_UP1 + 16
C_IN2 = C_DN1 + 16
C_BR = C_IN2 + 20
C_WO = C_BR + 4
C_UP2 = C_WO + 4
C_DN2 = C_UP2 + 16
N_PAGES = 2 * (C_DN2 + 16)

K_DT = 0
K_GRP = 1
K_SOUT = K_GRP + 3 * GROUPS
K_UP0 = K_SOUT + 4
K_DN0 = K_UP0 + 16
K_MIN = K_DN0 + 8
K_HEAD = K_MIN + 3
K_MOUT = K_HEAD + 16
K_UP1 = K_MOUT + 4
K_DN1 = K_UP1 + 16
K_IN2 = K_DN1 + 8
K_BR = K_IN2 + 20
K_WO = K_BR + 8
K_UP2 = K_WO + 4
K_DN2 = K_UP2 + 16

N_IDENT, N_ONES, N_BLK = 0, 128, 256
N_SSD = 384
SSD_W = T + (T - 128) + (T - 256)
N_MLA = N_SSD + SSD_W
MLA_W = 144 + T
N_ROPE = N_MLA + MLA_W
N_NA = N_ROPE + T
N_CONST = N_NA + 64

V_GAIN = 0
V_CONV = V_GAIN + 6 * KD
V_DSKIP = V_CONV + GROUPS * 4 * 5
V_SNORM = V_DSKIP + 16
V_QA = V_SNORM + 16
V_KVA = V_QA + 3
V_QG = V_KVA + 2
V_KG = V_QG + 1
V_CONV2 = V_KG + 1
V_QN2 = V_CONV2 + 12
V_KN2 = V_QN2 + 1
V_DTB = V_KN2 + 1
V_ALOG = V_DTB + 1
N_VEC = V_ALOG + 1


class At:

    def __init__(self, base, step=0, turn=0):
        assert step % 2 == 0
        self.base, self.step, self.turn = base, step, turn

    def __add__(self, n):
        return At(self.base + n, self.step, self.turn)

    def times(self, n, plus=0):
        return At(self.base * n + plus, self.step * n, self.turn)

    @property
    def value(self):
        return self.turn * self.step + self.base if self.step else self.base

    @property
    def half(self):
        return self.turn * (self.step // 2) + self.base // 2 if self.step else self.base // 2

    @property
    def parity(self):
        return self.base % 2

    def page(self, j=0):
        return Page(self.base * 2 + j, self.step * 2, self.turn)


class Page(At):

    @property
    def slot(self):
        assert self.step % SLOTS == 0
        return self.base % SLOTS

    @property
    def round(self):
        n = self.base // SLOTS + 1
        return self.turn * (self.step // SLOTS) + n if self.step else n


def build(nc, w, h0, vec, const, rpb, out, acs_dram):
    ctx = ExitStack()
    with ctx:
        def sb(name, shape, dt=F32, where=ctx):
            return where.enter_context(nc.sbuf_tensor(name, shape, dt))

        def sem(name):
            return ctx.enter_context(nc.semaphore(name))

        w_raw = [sb(f"w_raw{i}", [P, PAGE]) for i in range(SLOTS)]
        w_hi = [sb(f"w_hi{i}", [P, PAGE], F32R) for i in range(SLOTS)]
        w_lo = [sb(f"w_lo{i}", [P, PAGE], F32R) for i in range(SLOTS)]
        h = sb("h", [P, KD, T])
        x_hi = sb("x_hi", [P, KD, T], F32R)
        x_lo = sb("x_lo", [P, KD, T], F32R)
        h_sq = sb("h_sq", [P, KD, T])
        r_ln = sb("r_ln", [P, T])
        r_inv = sb("r_inv", [P, T])
        vecs = sb("vecs", [P, N_VEC])
        cst = sb("cst", [P, N_CONST])
        bias_mask = sb("bias_mask", [P, NA_HEADS, 2, 256])
        eps_t = sb("eps_t", [P, 3])

        ssd = ExitStack()
        g_hi = sb("g_hi", [P, 16, T], F32R, ssd)
        g_lo = sb("g_lo", [P, 16, T], F32R, ssd)
        a_exp = sb("a_exp", [32, 1], F32, ssd)
        cols = sb("cols", [P, 6, 32], F32, ssd)
        acs_bc = sb("acs_bc", [P, HPG, T], F32, ssd)
        u = sb("u", [P, 4, T + 3], F32, ssd)
        cv = sb("cv", [P, 4, T], F32, ssd)
        sg = sb("sg", [P, 4, T], F32, ssd)
        z_raw = sb("z_raw", [P, 2, T], F32, ssd)
        z_sg = sb("z_sg", [P, 2, T], F32, ssd)
        xs_s = [sb(f"xs_s{i}", [P, 2, T], F32, ssd) for i in range(2)]
        bc_s = sb("bc_s", [P, 2, T], F32, ssd)
        z_s = [sb(f"z_s{i}", [P, 2, T], F32, ssd) for i in range(2)]
        x_tok = sb("x_tok", [P, 3, 256], F32, ssd)
        cbm = sb("cbm", [P, SSD_W], F32, ssd)
        dd = [sb(f"dd{i}", [P, HPG, SSD_W], F32, ssd) for i in range(2)]
        mm = sb("mm", [P, HPG, SSD_W], F32, ssd)
        y1 = sb("y1", [P, 2, T], F32, ssd)
        y2 = sb("y2", [P, 2, T], F32, ssd)
        dtx, dtb, dta, dt_t = [mm[0:32, i, 0:T] for i in range(4)]
        acs = y1[0:32, 0, :]
        y_sum = sb("y_sum", [P, T], F32, ssd)
        g_ln = sb("g_ln", [P, T], F32, ssd)
        g_inv = sb("g_inv", [P, T], F32, ssd)
        ssd.close()

        mlp_mem = ExitStack()
        hid_hi = sb("hid_hi", [P, FF_TILES, T], F32R, mlp_mem)
        hid_lo = sb("hid_lo", [P, FF_TILES, T], F32R, mlp_mem)
        relu = [sb(f"relu{i}", [P, 2, T], F32, mlp_mem) for i in range(2)]
        relu_sq = [sb(f"relu_sq{i}", [P, 2, T], F32, mlp_mem) for i in range(2)]
        down_r = [sb(f"down_r{i}", [P, T], F32, mlp_mem) for i in range(2)]
        mlp_mem.close()

        mla = ExitStack()
        lat = sb("lat", [P, 6, T], F32, mla)
        lat_sq = h_sq[:, 0:6, :]
        lat_n = lat[:, 0:5, :]
        l_hi = sb("l_hi", [P, 5, T], F32R, mla)
        l_lo = sb("l_lo", [P, 5, T], F32R, mla)
        l_ln = sb("l_ln", [P, 2, T], F32, mla)
        l_inv = sb("l_inv", [P, 2, T], F32, mla)
        rope_q = sb("rope_q", [P, T], F32, mla)
        rope_k = sb("rope_k", [P, T], F32, mla)
        rot_a = sb("rot_a", [P, 2, T], F32, mla)
        rot_b = sb("rot_b", [P, 2, T], F32, mla)
        q_pre = sb("q_pre", [QK, 4, T2], F32, mla)
        k_pre = sb("k_pre", [QK, 4, T], F32, mla)
        q_sq = sb("q_sq", [QK, 4, T2], F32, mla)
        k_sq = sb("k_sq", [QK, 4, T], F32, mla)
        v_t = sb("v_t", [P, 4, T], F32, mla)
        n_ln = sb("n_ln", [QK, 2, T], F32, mla)
        n_inv = sb("n_inv", [QK, 2, T], F32, mla)
        q_fin = [sb(f"q_fin{i}", [QK, 4, T2], F32, mla) for i in range(2)]
        k_fin = [sb(f"k_fin{i}", [QK, 4, T], F32, mla) for i in range(2)]
        v_tok = [sb(f"v_tok{i}", [P, 4, 3, HD], F32, mla) for i in range(2)]
        o_hi = sb("o_hi", [P, 8, T2], F32R, mla)
        o_lo = sb("o_lo", [P, 8, T2], F32R, mla)
        s_m = [sb(f"s_m{i}", [P, MLA_W], F32, mla) for i in range(2)]
        pr = [sb(f"pr{i}", [P, MLA_W], F32, mla) for i in range(2)]
        p_t = sb("p_t", [P, 384], F32, mla)
        p_t0 = sb("p_t0", [META, T2], F32, mla)
        mx = [sb(f"mx{i}", [P, 2], F32, mla) for i in range(2)]
        nmx = [sb(f"nmx{i}", [P, 2], F32, mla) for i in range(2)]
        rsum = [sb(f"rsum{i}", [P, 2], F32, mla) for i in range(2)]
        rinv = [sb(f"rinv{i}", [P, 2], F32, mla) for i in range(2)]
        mla.close()

        na = ExitStack()
        with ExitStack() as attention:
            qk_r = sb("qk_r", [P, 8, T2], F32, attention)
            qk_f = sb("qk_f", [P, 8, T2], F32, attention)
        m_hi = sb("m_hi", [P, 8, T2], F32R, na)
        m_lo = sb("m_lo", [P, 8, T2], F32R, na)
        qk_sq = [sb(f"qk_sq{i}", [P, 2, T2], F32, na) for i in range(2)]
        qk_ln = sb("qk_ln", [P, 2, T2], F32, na)
        qk_inv = [sb(f"qk_inv{i}", [P, 2, T2], F32, na) for i in range(2)]
        v_r = sb("v_r", [P, 4, T2], F32, na)
        v2 = sb("v2", [P, 2, 512], F32, na)
        cc_ch = h_sq[:, 0:2, 0:T2]
        zc = sb("zc", [P, 4, T2 + 2], F32, na)
        cv2 = sb("cv2", [P, 4, T2], F32, na)
        cb_r = sb("cb_r", [P, 4, T2], F32, na)
        yb = cv2
        yb_hi = sb("yb_hi", [P, 4, T2], F32R, na)
        yb_lo = sb("yb_lo", [P, 4, T2], F32R, na)
        ya_hi = sb("ya_hi", [P, 4, T2], F32R, na)
        ya_lo = sb("ya_lo", [P, 4, T2], F32R, na)
        gate = sb("gate", [P, 16, T2], F32, na)
        s_m2 = [sb(f"s_m2{i}", [P, 512], F32, na) for i in range(2)]
        pr2 = [sb(f"pr2{i}", [P, 512], F32, na) for i in range(2)]
        p_t2 = sb("p_t2", [P, 512], F32, na)
        mx2 = [sb(f"mx2{i}", [P, 2], F32, na) for i in range(2)]
        nmx2 = [sb(f"nmx2{i}", [P, 2], F32, na) for i in range(2)]
        rsum2 = [sb(f"rsum2{i}", [P, 2], F32, na) for i in range(2)]
        rinv2 = [sb(f"rinv2{i}", [P, 2], F32, na) for i in range(2)]
        m_a, m_b = h_sq[:, 2:4, 0:T2], h_sq[:, 4:6, 0:T2]
        na.close()

        lin = ctx.enter_context(nc.psum_tensor("lin", [P, 4, 512], F32))
        ps4, ps5, ps6, ps7 = [ctx.enter_context(nc.psum_tensor(f"ps{i}", [P, 512], F32)) for i in range(4, 8)]

        def linp(k, n, rows=slice(0, P)):
            return lin[rows, 2 * k.parity:2 * k.parity + 2, n]

        ident = cst[:, N_IDENT:N_IDENT + P]
        ones = cst[:, N_ONES:N_ONES + P]
        blk = cst[:, N_BLK:N_BLK + P]

        def v(col, n=1, rows=slice(0, P)):
            return vecs[rows, bass.ds(col, n)]

        def gain(norm, kt):
            return v(V_GAIN + norm * KD + kt)

        def over(ap, n):
            return ap.unsqueeze(1).broadcast_to([ap.shape[0], n, ap.shape[1]])

        w_arrived = [sem(f"w_arrived{i}") for i in range(SLOTS)]
        w_hi_done, w_used = sem("w_hi_done"), sem("w_used")
        w_lo_done = [sem(f"w_lo_done{i}") for i in range(SLOTS)]
        drained = [sem(f"drained{i}") for i in range(2)]
        small_in, h_in, rpb_in, out_done = sem("small_in"), sem("h_in"), sem("rpb_in"), sem("out_done")
        xh_done, xl_done = sem("xh_done"), sem("xl_done")
        hsq_done, hsum_done, stat_done = sem("hsq_done"), sem("hsum_done"), sem("stat_done")
        rln_done, r_done = sem("rln_done"), sem("r_done")
        h_mlp = sem("h_mlp")
        memset_done, bias_done = sem("memset_done"), sem("bias_done")
        dt_dve, dt_act, dtT_done, cols_done = sem("dt_dve"), sem("dt_act"), sem("dtT_done"), sem("cols_done")
        acs_out = sem("acs_out")
        acs_in = sem("acs_in")
        cv0_done, cv_step, clamped, sg_step, silu_done = (sem("cv0_done"), sem("cv_step"), sem("clamped"),
                                                          sem("sg_step"), sem("silu_done"))
        xT_done, xtok_done, cb_done, cbm_done = sem("xT_done"), sem("xtok_done"), sem("cb_done"), sem("cbm_done")
        dd_done, ee_done, mm_done, y_done, y_read = (sem("dd_done"), sem("ee_done"), sem("mm_done"),
                                                     sem("y_done"), sem("y_read"))
        y2_done, ysq_done, ysum_done, gstat_done = sem("y2_done"), sem("ysq_done"), sem("ysum_done"), sem("gstat_done")
        gln_done, ginv_done, y3_done, gh_done, gl_done = (sem("gln_done"), sem("ginv_done"), sem("y3_done"),
                                                          sem("gh_done"), sem("gl_done"))
        relu_done, rsq_done, hh_done, hl_done = sem("relu_done"), sem("rsq_done"), sem("hh_done"), sem("hl_done")
        latsq_done, lstat_done, l_act, latn_done = sem("latsq_done"), sem("lstat_done"), sem("l_act"), sem("latn_done")
        lh_done, ll_done, rope_done, krope = sem("lh_done"), sem("ll_done"), sem("rope_done"), sem("krope")
        raw_read, rot_done, rot_sum, nsum_done = sem("raw_read"), sem("rot_done"), sem("rot_sum"), sem("nsum_done")
        nln_done, ninv_done, fin_done = sem("nln_done"), sem("ninv_done"), sem("fin_done")
        s_done, sm_done, nm_done, ex_done = sem("s_done"), sem("sm_done"), sem("nm_done"), sem("ex_done")
        ri_done, p_done, pT_done, pt_done, pt0_done = (sem("ri_done"), sem("p_done"), sem("pT_done"),
                                                       sem("pt_done"), sem("pt0_done"))
        pv_done, oh_done, ol_done = sem("pv_done"), sem("oh_done"), sem("ol_done")
        qksq_done, qkstat_done, qkln_done, qkinv_done, qkf_done = (sem("qksq_done"), sem("qkstat_done"),
                                                                   sem("qkln_done"), sem("qkinv_done"), sem("qkf_done"))
        vT_done, v2_done = sem("vT_done"), sem("v2_done")
        z_done, cv2_0, cv2_step, yb_done, ybh_done, ybl_done = (sem("z_done"), sem("cv2_0"), sem("cv2_step"),
                                                                sem("yb_done"), sem("ybh_done"), sem("ybl_done"))
        gclamp, gate_step = sem("gclamp"), sem("gate_step")
        s2_done, sm2_done, nm2_done, ex2_done = sem("s2_done"), sem("sm2_done"), sem("nm2_done"), sem("ex2_done")
        ri2_done, p2_done, pT2_done, pt2_done = sem("ri2_done"), sem("p2_done"), sem("pT2_done"), sem("pt2_done")
        pv2_done, yah_done, yal_done = sem("pv2_done"), sem("yah_done"), sem("yal_done")
        m_done, mh_done, ml_done = sem("m_done"), sem("mh_done"), sem("ml_done")

        block = ctx.enter_context(nc.Block())

        SLOT_TURNS = 3

        def h_ready(norm, kt):
            if norm == 0:
                return (h_in, 16)
            if norm in (2, 4):
                return (h_mlp, (kt + (8 * (norm // 2 - 1) + 1)).value)
            k = At({1: K_SOUT, 3: K_MOUT, 5: K_WO}[norm] + kt.base // 2)
            return (drained[k.parity], k.half + 1)

        def tokens(norm):
            return slice(0, T) if norm < 3 else slice(META, T)

        def width(norm):
            return T if norm < 3 else T2

        @block.sync
        def _(sp):
            sp.dma_start(cst[:, :], const).then_inc(small_in, 16)
            sp.dma_start(vecs[:, :], vec).then_inc(small_in, 16)
            sp.dma_start(h[:, :, :], h0).then_inc(h_in, 16)
            for i in range(SLOTS):
                sp.dma_start(w_raw[i][:, :], w[i]).then_inc(w_arrived[i], 16)
            with sp.Fori(1, N_PAGES // SLOTS) as turn:
                for i in range(SLOTS):
                    sp.wait_ge(w_lo_done[i], turn)
                    sp.dma_start(w_raw[i][:, :], w[turn * SLOTS + i]).then_inc(w_arrived[i], 16)
            for kt in range(KD):
                sp.wait_ge(h_mlp, 16 + kt + 1)
                sp.dma_start(out[:, kt, :], h[:, kt, META:T]).then_inc(out_done, 16)
            sp.wait_ge(out_done, 16 * KD)

        @block.tensor
        def _(pe):
            mm3 = nc.tensor.matmul

            def free(k):
                if k.base >= 2:
                    pe.wait_ge(drained[k.parity], k.half)

            def tile(o, pg, hi, lo, n, kts=KD, kt0=0, at=0, t0=0, first=True, last=True, before=None):
                pe.wait_ge(w_lo_done[pg.slot], pg.round)
                for i in range(kts):
                    if before:
                        before(i)
                    wh = w_hi[pg.slot][:, (at + i) * P:(at + i + 1) * P]
                    wl = w_lo[pg.slot][:, (at + i) * P:(at + i + 1) * P]
                    xh, xl = hi[:, kt0 + i, t0:t0 + n], lo[:, kt0 + i, t0:t0 + n]
                    mm3(o, wh, xh, start=first and i == 0, stop=False)
                    mm3(o, wh, xl, start=False, stop=False)
                    ins = mm3(o, wl, xh, start=False, stop=last and i == kts - 1)
                return ins

            def lin_chunk(c, k, n, norm=None, hi=x_hi, lo=x_lo, before=None):
                free(k)
                if norm is not None:
                    before = lambda i: pe.wait_ge(xl_done, KD * norm + i + 1)
                for j in range(2):
                    tile(lin[:, 2 * k.parity + j, 0:n], c.page(j), hi, lo, n, before=before if j == 0 else None)\
                        .then_inc(w_used, 1)

            def norm_stat(norm):
                n = width(norm)
                pe.wait_ge(hsum_done, (KD - 1) * (norm + 1))
                nc.tensor.matmul(ps7[:, 0:n], ones, h_sq[:, 0, 0:n], start=True, stop=True).then_inc(stat_done, 1)

            pe.wait_ge(small_in, 32)
            tile(lin[:, 0, 0:T], At(C_DT).page(0), x_hi, x_lo, T,
                 before=lambda i: pe.wait_ge(xl_done, i + 1)).then_inc(w_used, 1)
            pe.wait_ge(w_lo_done[1], 1)
            norm_stat(0)
            pe.sem_inc(w_used, 1)

            def dt_transposes():
                pe.wait_ge(dt_dve, 6)
                for i, src in enumerate((dt_t, acs)):
                    for s in range(3):
                        n = min(P, T - s * P)
                        ins = nc.tensor.transpose(ps4[0:n, (3 * i + s) * 32:(3 * i + s + 1) * 32],
                                                  src[:, s * P:s * P + n], ident[0:32, 0:32])
                ins.then_inc(dtT_done, 1)

            def x_transposes(g):
                pe.wait_ge(silu_done, g.times(3, 1).value)
                if g.base >= 1:
                    pe.wait_ge(y_read, g.times(2, -1).value)
                else:
                    pe.wait_ge(cols_done, 4)
                for q in range(2):
                    nc.tensor.transpose(ps4[:, q * P:(q + 1) * P], xs_s[g.parity][:, q, 0:128], ident)
                    nc.tensor.transpose(ps6[:, q * P:(q + 1) * P], xs_s[g.parity][:, q, 128:256], ident)
                    ins = nc.tensor.transpose(ps4[0:META, 256 + q * P:256 + (q + 1) * P],
                                              xs_s[g.parity][:, q, 256:T], ident)
                ins.then_inc(xT_done, 1)

            def cb_products(g):
                pe.wait_ge(silu_done, g.times(3, 2).value)
                if g.base >= 2:
                    pe.wait_ge(gln_done, (g + (-1)).value)
                b, cc = bc_s[:, 0, :], bc_s[:, 1, :]
                nc.tensor.matmul(ps5[:, 0:T], b[:, 0:128], cc, start=True, stop=True)
                nc.tensor.matmul(ps5[:, T:T + 144], b[:, 128:256], cc[:, 128:T], start=True, stop=True)
                nc.tensor.matmul(ps5[0:META, 416:432], b[:, 256:T], cc[:, 256:T],
                                 start=True, stop=True).then_inc(cb_done, 1)

            def group_stat(g):
                pe.wait_ge(ysum_done, (g + 1).value)
                pe.wait_ge(cbm_done, (g + 2).value) if g.base < 7 else None
                nc.tensor.matmul(ps5[:, 0:T], ones, y_sum[:, :], start=True, stop=True).then_inc(gstat_done, 1)

            def y_products(g):
                pe.wait_ge(xtok_done, (g + 1).value)
                for q in range(2):
                    o = (ps6, ps7)[q]
                    if q == 1 and g.base >= 1:
                        pe.wait_ge(y_read, g.times(2).value)
                    if q == 1 and g.base == 0:
                        pe.wait_ge(rln_done, 1)
                    for e in range(2):
                        j = 2 * q + e
                        pe.wait_ge(mm_done, g.times(4, j + 1).value)
                        rows = slice(e * HD, (e + 1) * HD)
                        cs = slice(j * HD, (j + 1) * HD)
                        nc.tensor.matmul(o[rows, 0:T], x_tok[:, 0, cs], mm[:, j, 0:T], start=True, stop=False)
                        nc.tensor.matmul(o[rows, 128:T], x_tok[:, 1, cs], mm[:, j, T:416], start=False, stop=False)
                        ins = nc.tensor.matmul(o[rows, 256:T], x_tok[0:META, 2, cs], mm[0:META, j, 416:432],
                                               start=False, stop=True)
                    ins.then_inc(y_done, 1)

            def slot(s, has_lin=True, has_scan=True, has_stat=True, first=False):
                c, k = s.times(3, C_GRP), s.times(3, K_GRP)
                if has_lin:
                    lin_chunk(c, k, T)
                if first:
                    dt_transposes()
                if has_scan:
                    x_transposes(s + (-1))
                    cb_products(s + (-1))
                if has_lin:
                    lin_chunk(c + 1, k + 1, T)
                if has_stat:
                    group_stat(s + (-2))
                if has_lin:
                    lin_chunk(c + 2, k + 2, T)
                if has_scan:
                    y_products(s + (-1))

            slot(At(0), has_scan=False, has_stat=False, first=True)
            slot(At(1), has_stat=False)
            with pe.Fori(0, SLOT_TURNS) as turn:
                for i in range(2):
                    slot(At(2 + i, 2, turn))
            def sout(r, j, half, before=None):
                k = At(K_SOUT + 2 * r + j // 2)
                if j % 2 == 0 and half == 0:
                    free(k)
                tile(lin[:, 2 * k.parity + j % 2, 0:T], At(C_SOUT + 4 * r).page(4 * half + j), g_hi, g_lo, T,
                     kt0=8 * half, first=half == 0, last=half == 1, before=before).then_inc(w_used, 1)

            x_transposes(At(7))
            cb_products(At(7))
            pe.wait_ge(gl_done, 8)
            sout(0, 0, 0)
            sout(0, 1, 0)
            group_stat(At(6))
            sout(0, 2, 0)
            y_products(At(7))
            sout(0, 3, 0)
            group_stat(At(7))
            sout(0, 0, 1, lambda i: pe.wait_ge(gl_done, 9 + i))
            for j in range(1, 4):
                sout(0, j, 1)
            for half in range(2):
                for j in range(4):
                    sout(1, j, half)

            def mlp(m, norm, c_up, k_up, c_dn, k_dn):
                n = width(norm)
                lin_chunk(At(c_up), At(k_up), n, norm)
                lin_chunk(At(c_up + 1), At(k_up + 1), n)
                norm_stat(norm)
                with pe.Fori(1, 8) as turn:
                    for i in range(2):
                        lin_chunk(At(c_up + i, 2, turn), At(k_up + i, 2, turn), n)
                with pe.Fori(0, 4) as turn:
                    for i in range(2):
                        k = At(k_dn + i, 2, turn)
                        free(k)
                        for q in range(4):
                            pe.wait_ge(hl_done, 16 * m + 4 * (q + 1))
                            tile(lin[:, 2 * k.parity, 0:n], At(c_dn + 2 * i, 4, turn).page(q), hid_hi, hid_lo, n,
                                 kt0=8 * q, first=q == 0, last=q == 3).then_inc(w_used, 1)

            mlp(0, 1, C_UP0, K_UP0, C_DN0, K_DN0)

            lin_chunk(At(C_MIN), At(K_MIN), T, 2)
            lin_chunk(At(C_MIN + 1), At(K_MIN + 1), T)
            norm_stat(2)
            lin_chunk(At(C_MIN + 2), At(K_MIN + 2), T)
            pe.wait_ge(latsq_done, 3)
            for i in range(3):
                ins = nc.tensor.matmul(ps4[:, 0:T], ones, lat_sq[:, i, :], start=i == 0, stop=i == 2)
            ins.then_inc(lstat_done, 1)
            for i in range(2):
                ins = nc.tensor.matmul(ps5[:, 0:T], ones, lat_sq[:, 3 + i, :], start=i == 0, stop=i == 1)
            ins.then_inc(lstat_done, 1)

            def unit(un):
                s, n = un // 4, un % 4
                k = At(K_HEAD + un)
                kts, kt0, t0 = (3, 0, META) if n < 2 else (2, 3, 0)
                if un < 4:
                    pe.wait_ge(ll_done, 3 if n < 2 else 5)
                free(k)
                for j in range(2):
                    ins = tile(lin[:, 2 * k.parity + j, 0:T - t0], At(C_HEAD + 2 * s).page(n), l_hi, l_lo, T - t0,
                               kts=kts, kt0=kt0, at=j * kts, t0=t0)
                ins.then_inc(w_used, 1)

            def unit_norm(un):
                s, n = un // 4, un % 4
                k = At(K_HEAD + un)
                pe.wait_ge(raw_read, 4 * s + n + 1)
                if n < 2:
                    pe.wait_ge(rot_sum, 2 * s + n + 1)
                elif s == 0:
                    pe.wait_ge(krope, 4)
                for j in range(2):
                    head = 2 * (n % 2) + j
                    bank = lin[:, 2 * k.parity + j, :]
                    if n < 2:
                        ins = nc.tensor.matmul(bank[:, 0:T2], ones[0:QK, :], q_sq[:, head, :], start=True, stop=True)
                    else:
                        nc.tensor.matmul(bank[:, 0:T], ones[0:QK, :], k_sq[:, head, :], start=True, stop=True)
                        idv = ident[HD:P, HD:P]
                        nc.tensor.transpose(bank[:, 272:336], v_t[HD:P, head, META:144], idv)
                        nc.tensor.transpose(bank[:, 336:400], v_t[HD:P, head, 144:T], idv)
                        ins = nc.tensor.transpose(bank[0:META, 400:464], v_t[HD:P, head, 0:META], idv)
                ins.then_inc(nsum_done, 1)

            def scores(n):
                s, j = n // 4, n % 4
                p = s % 2
                if j == 0:
                    pe.wait_ge(fin_done, 4 * s + 4)
                if n >= 2:
                    pe.wait_ge(sm_done, n - 1)
                elif n == 0:
                    pe.wait_ge(l_act, 2)
                o = (ps5, ps6)[n % 2]
                nc.tensor.matmul(o[:, 0:144], q_fin[p][:, j, 0:128], k_fin[p][:, j, 0:144], start=True, stop=True)
                nc.tensor.matmul(o[:, 144:416], q_fin[p][:, j, 128:256], k_fin[p][:, j, :],
                                 start=True, stop=True).then_inc(s_done, 1)

            def p_transposes(n):
                pe.wait_ge(p_done, n + 1)
                if n >= 1:
                    pe.wait_ge(pt_done, n)
                else:
                    pe.wait_ge(rln_done, 3)
                if n % 2 == 0 and n >= 2:
                    pe.wait_ge(ol_done, n // 2)
                prn = pr[n % 2]
                nc.tensor.transpose(ps4[0:META, 256:384], prn[:, 0:16], ident)
                nc.tensor.transpose(ps4[0:META, 384:512], prn[:, 144:160], ident)
                nc.tensor.transpose(ps7[:, 0:128], prn[:, 16:144], ident)
                nc.tensor.transpose(ps7[:, 128:256], prn[:, 160:288], ident)
                nc.tensor.transpose(ps7[:, 256:384], prn[:, 288:416], ident).then_inc(pT_done, 1)

            def values(n):
                j, p = n % 4, n // 4 % 2
                pe.wait_ge(pt_done, n + 1)
                pe.wait_ge(pt0_done, n + 1)
                o = ps4[(n % 2) * HD:(n % 2 + 1) * HD, 0:T2]
                nc.tensor.matmul(o, v_tok[p][0:META, j, 0, :], p_t0[:, :], start=True, stop=False)
                nc.tensor.matmul(o, v_tok[p][:, j, 1, :], p_t[:, 0:256], start=False, stop=False)
                nc.tensor.matmul(o[:, 128:256], v_tok[p][:, j, 2, :], p_t[:, 256:384],
                                 start=False, stop=True).then_inc(pv_done, 1)

            def mout_part(j, kts, kt0):
                k = At(K_MOUT + j // 2)
                if j % 2 == 0 and kt0 == 0:
                    free(k)
                pe.wait_ge(ol_done, kt0 + kts)
                ins = tile(lin[:, 2 * k.parity + j % 2, 0:T2], At(C_MOUT).page(j), o_hi, o_lo, T2, kts=kts, kt0=kt0,
                           at=kt0, first=kt0 == 0, last=kt0 + kts == KD)
                if kt0 + kts == KD:
                    ins.then_inc(w_used, 1)

            for t in range(MLA_STEPS):
                if t >= 8:
                    p_transposes(t - 8)
                if t < 16:
                    unit(t)
                if 18 <= t < 22:
                    mout_part(t - 18, 5, 0)
                if t >= 22:
                    mout_part(2 * (t - 22), 2, 5)
                    mout_part(2 * (t - 22) + 1, 2, 5)
                if t >= 8:
                    values(t - 8)
                if 0 <= t - 1 < 16:
                    unit_norm(t - 1)
                if 0 <= t - 5 < 16:
                    scores(t - 5)
            for j in range(4):
                mout_part(j, 1, 7)
            for i in (2, 3):
                lin_chunk(At(C_MOUT + i), At(K_MOUT + i), T2, hi=o_hi, lo=o_lo)

            mlp(1, 3, C_UP1, K_UP1, C_DN1, K_DN1)

            def qk_stat(i):
                pe.wait_ge(qksq_done, i + 1)
                if i >= 2:
                    pe.wait_ge(qkln_done, i - 1)
                nc.tensor.matmul((ps5, ps6)[i % 2][:, :], blk, qk_sq[i % 2][:, :, :].rearrange("p a t -> p (a t)"),
                                 start=True, stop=True).then_inc(qkstat_done, 1)

            def v_transposes():
                for i in (4, 5):
                    k = At(K_IN2 + i)
                    pe.wait_ge(drained[k.parity], k.half + 1)
                pe.wait_ge(rln_done, 5)
                for tt, o in ((0, ps7), (1, ps4)):
                    for j in range(4):
                        ins = nc.tensor.transpose(o[:, j * P:(j + 1) * P], v_r[:, j, tt * P:(tt + 1) * P], ident)
                ins.then_inc(vT_done, 1)

            def scores2(n):
                if n == 0:
                    pe.wait_ge(qkln_done, 3)
                    pe.wait_ge(qkf_done, 4)
                elif n == 1:
                    pe.wait_ge(qkln_done, 4)
                else:
                    pe.wait_ge(sm2_done, n - 1)
                rows, j = slice((n % 2) * HD, (n % 2 + 1) * HD), n // 2
                for qt in range(2):
                    ins = nc.tensor.matmul((ps5, ps6)[n % 2][:, qt * 256:(qt + 1) * 256],
                                           qk_f[rows, j, qt * P:(qt + 1) * P], qk_f[rows, 4 + j, :],
                                           start=True, stop=True)
                ins.then_inc(s2_done, 1)

            def p_transposes2(n):
                pe.wait_ge(p2_done, n + 1)
                if n == 0:
                    pe.wait_ge(v2_done, 2)
                else:
                    pe.wait_ge(pt2_done, n)
                for kt in range(2):
                    for qt in range(2):
                        ins = nc.tensor.transpose(ps7[:, kt * 256 + qt * P:kt * 256 + (qt + 1) * P],
                                                  pr2[n % 2][:, qt * 256 + kt * P:qt * 256 + (kt + 1) * P], ident)
                ins.then_inc(pT2_done, 1)

            def values2(n):
                if n % 2 == 0 and n >= 2:
                    pe.wait_ge(yal_done, n // 2)
                pe.wait_ge(pt2_done, n + 1)
                o = ps4[(n % 2) * HD:(n % 2 + 1) * HD, 0:T2]
                for kt in range(2):
                    ins = nc.tensor.matmul(o, v2[:, kt, n * HD:(n + 1) * HD], p_t2[:, kt * 256:(kt + 1) * 256],
                                           start=kt == 0, stop=kt == 1)
                ins.then_inc(pv2_done, 1)

            for i in range(20):
                if 8 <= i < 16:
                    p_transposes2(i - 8)
                lin_chunk(At(C_IN2 + i), At(K_IN2 + i), T2, 4 if i == 0 else None)
                if i == 0:
                    norm_stat(4)
                if 1 <= i <= 4:
                    qk_stat(i - 1)
                if i == 6:
                    v_transposes()
                if 8 <= i < 16:
                    values2(i - 8)
                if 6 <= i < 14:
                    scores2(i - 6)

            pe.wait_ge(yal_done, 4)
            pe.wait_ge(ybl_done, 2)
            for b in range(4):
                for n, (hi, lo) in enumerate(((ya_hi, ya_lo), (yb_hi, yb_lo))):
                    k = At(K_BR + 2 * b + n)
                    free(k)
                    for j in range(2):
                        ins = tile(lin[:, 2 * k.parity + j, 0:T2], At(C_BR + b).page(n), hi, lo, T2, kts=4, at=4 * j)
                    ins.then_inc(w_used, 1)

            for i in range(4):
                lin_chunk(At(C_WO + i), At(K_WO + i), T2, hi=m_hi, lo=m_lo,
                          before=(lambda kt: pe.wait_ge(ml_done, kt // 2 + 1)) if i == 0 else None)

            mlp(2, 5, C_UP2, K_UP2, C_DN2, K_DN2)

        @block.scalar
        def _(act):
            a = nc.scalar.activation

            def hi(pg, n=PAGE):
                act.wait_ge(w_arrived[pg.slot], pg.round * 16)
                if pg.base >= SLOTS:
                    act.wait_ge(w_used, (pg + (1 - SLOTS)).value)
                a(w_hi[pg.slot][:, 0:n], w_raw[pg.slot][:, 0:n], ACT.Copy).then_inc(w_hi_done, 1)

            def hi2(c):
                hi(c.page(0))
                hi(c.page(1))

            def norm_hi(norm, kt):
                n, tk = width(norm), tokens(norm)
                act.wait_ge(*h_ready(norm, kt))
                a(x_hi[:, kt.value, 0:n], h[:, kt.value, tk], ACT.Copy, scale=gain(norm, kt.value))\
                    .then_inc(xh_done, 1)
                a(h_sq[:, kt.value, 0:n], h[:, kt.value, tk], ACT.Square).then_inc(hsq_done, 1)

            def norm_inv(norm, squared=False):
                n = width(norm)
                act.wait_ge(stat_done, norm + 1)
                a(r_ln[:, 0:n], ps7[:, 0:n], ACT.Ln, bias=eps_t[:, 0:1], scale=1.0 / D).then_inc(rln_done, 1)
                act.wait_ge(rln_done, norm + 1)
                a(r_inv[:, 0:n], r_ln[:, 0:n], ACT.Exp, scale=-1.0 if squared else -0.5).then_inc(r_done, 1)

            act.preload_act_table_set("natural_log_exp_and_others")
            act.wait_ge(small_in, 32)
            act.wait_ge(memset_done, 4)
            for kt in range(KD):
                norm_hi(0, At(kt))
                if kt % 2:
                    hi(Page(kt // 2))
            a(a_exp[:, :], v(V_ALOG, rows=slice(0, 32)), ACT.Exp).then_inc(dt_act, 1)
            norm_inv(0)
            hi2(At(2))
            act.wait_ge(dt_dve, 3)
            a(dta[:, :], dta[:, :], ACT.Exp, scale=-1.0).then_inc(dt_act, 1)
            act.wait_ge(dt_act, 2)
            a(dta[:, :], dta[:, :], ACT.Ln, bias=1.0).then_inc(dt_act, 1)

            def sigmoid(buf, step_sem, n):
                a(buf, buf, ACT.Exp, scale=-1.0).then_inc(step_sem, 1)
                act.wait_ge(step_sem, (n + 1).value)
                a(buf, buf, ACT.Ln, bias=1.0).then_inc(step_sem, 1)
                act.wait_ge(step_sem, (n + 2).value)
                a(buf, buf, ACT.Exp, scale=-1.0).then_inc(step_sem, 1)

            def conv0(s, pair):
                k = s.times(3, K_GRP + pair)
                act.wait_ge(drained[k.parity], (k.half + 1))
                for q in (2 * pair, 2 * pair + 1):
                    at = s.times(20, V_CONV + 5 * q)
                    a(cv[:, q, :], u[:, q, 0:T], ACT.Identity, scale=v(at.value), bias=v((at + 4).value))\
                        .then_inc(cv0_done, 1)

            def decay(g, j):
                h_at = g.times(4, j)
                d = dd[g.parity]
                act.wait_ge(dd_done, g.times(2, j // 2 + 1).value)
                for s, (rows, at, n) in enumerate(((P, 0, T), (P, T, 144), (META, 416, 16))):
                    ins = a(d[0:rows, j, at:at + n], d[0:rows, j, at:at + n], ACT.Exp,
                            bias=cols[0:rows, 3 + s, bass.ds(h_at.value, 1)])
                ins.then_inc(ee_done, 1)

            def slot(s, has_lin=True, has_scan=True, has_stat=True):
                c = s.times(3, C_GRP)
                g, gs = s + (-1), s + (-2)
                if has_scan and g.base == 0:
                    act.wait_ge(cols_done, 4)
                if has_lin:
                    hi((c + 2).page(0))
                if has_scan:
                    act.wait_ge(clamped, g.times(3, 3).value)
                    sigmoid(z_sg[:, :, :], sg_step, g.times(9, 6))
                    decay(g, 0)
                if has_lin:
                    hi((c + 2).page(1))
                if has_scan:
                    act.wait_ge(cb_done, (g + 1).value)
                    if g.base:
                        act.wait_ge(mm_done, g.times(4).value)
                    a(cbm[:, 0:416], ps5[:, 0:416], ACT.Copy)
                    a(cbm[0:META, 416:432], ps5[0:META, 416:432], ACT.Copy).then_inc(cbm_done, 1)
                    act.wait_ge(xT_done, (g + 1).value)
                    a(x_tok[:, 0, :], ps4[:, 0:256], ACT.Copy)
                    a(x_tok[0:META, 2, :], ps4[0:META, 256:512], ACT.Copy)
                    a(x_tok[:, 1, :], ps6[:, 0:256], ACT.Copy).then_inc(xtok_done, 1)
                if has_stat:
                    act.wait_ge(y2_done, (gs + 1).value)
                    a(h_sq[:, 0:2, :], y2[:, :, :], ACT.Square).then_inc(ysq_done, 1)
                if has_lin:
                    conv0(s, 0)
                if has_scan:
                    decay(g, 1)
                    decay(g, 2)
                    decay(g, 3)
                if has_lin:
                    hi((c + 3).page(0))
                    act.wait_ge(clamped, s.times(3, 1).value)
                    sigmoid(sg[:, 0:2, :], sg_step, s.times(9))
                    conv0(s, 1)
                    hi((c + 3).page(1))
                if has_stat:
                    act.wait_ge(gstat_done, (gs + 1).value)
                    a(g_ln[:, :], ps5[:, 0:T], ACT.Ln, bias=eps_t[:, 0:1], scale=1.0 / 256).then_inc(gln_done, 1)
                    act.wait_ge(gln_done, (gs + 1).value)
                    a(g_inv[:, :], g_ln[:, :], ACT.Exp, scale=-0.5).then_inc(ginv_done, 1)
                if has_lin:
                    hi((c + 4).page(0))
                if has_stat:
                    act.wait_ge(y3_done, (gs + 1).value)
                    for q in range(2):
                        t = gs.times(2, q)
                        a(g_hi[:, t.value, :], y1[:, q, :], ACT.Copy, scale=v((t + V_SNORM).value))\
                            .then_inc(gh_done, 1)
                if has_lin:
                    act.wait_ge(clamped, s.times(3, 2).value)
                    sigmoid(sg[:, 2:4, :], sg_step, s.times(9, 3))
                    hi((c + 4).page(1))

            slot(At(0), has_scan=False, has_stat=False)
            slot(At(1), has_stat=False)
            with act.Fori(0, SLOT_TURNS) as turn:
                for i in range(2):
                    slot(At(2 + i, 2, turn))
            slot(At(8), has_lin=False)
            slot(At(9), has_lin=False, has_scan=False)

            for i in range(8):
                hi2(At(C_SOUT + 2 + i))
                if i in (3, 7):
                    for kt in range(i - 3, i + 1):
                        norm_hi(1, At(kt))

            def mlp(m, norm, c_up, k_up, c_dn, last):
                n = width(norm)

                def up(i, t):
                    k = t + k_up
                    hi((t + (c_up + 2)).page(0))
                    act.wait_ge(w_used, (t + (c_up + 1)).page().value)
                    a(relu[i][:, :, 0:n], linp(k, slice(0, n)), ACT.Relu).then_inc(drained[k.parity], 1)
                    hi((t + (c_up + 2)).page(1))
                    act.wait_ge(drained[k.parity], k.half + 1)
                    at = t.times(2)
                    a(hid_hi[:, bass.ds(at.value, 2), 0:n], relu[i][:, :, 0:n], ACT.Square).then_inc(hh_done, 1)

                for i in range(2):
                    up(i, At(i))
                norm_inv(norm, squared=True)
                with act.Fori(1, 8) as turn:
                    for i in range(2):
                        t = At(i, 2, turn)
                        act.wait_ge(hl_done, (t + (16 * m - 1)).value)
                        up(i, t)

                def down(t, next_hi=True):
                    if next_hi:
                        hi2(t.times(2, c_dn + 2))
                        hi2(t.times(2, c_dn + 3))
                    if not last:
                        norm_hi(norm + 1, t)

                with act.Fori(0, 3) as turn:
                    for i in range(2):
                        down(At(i, 2, turn))
                down(At(6))
                down(At(7), not last)

            mlp(0, 1, C_UP0, K_UP0, C_DN0, False)

            hi2(At(C_MIN + 2))
            hi(At(C_HEAD).page(0), 6 * P)
            hi(At(C_HEAD).page(1), 6 * P)
            norm_inv(2)
            hi(At(C_HEAD).page(2), 4 * P)
            hi(At(C_HEAD).page(3), 4 * P)
            for i in range(3):
                k = At(K_MIN + i)
                act.wait_ge(drained[k.parity], k.half + 1)
                a(lat_sq[:, 2 * i:2 * i + 2, :], lat[:, 2 * i:2 * i + 2, :], ACT.Square).then_inc(latsq_done, 1)
            for i, (ps, n) in enumerate(((ps4, 384), (ps5, 256))):
                act.wait_ge(lstat_done, i + 1)
                a(l_ln[:, i, :], ps[:, 0:T], ACT.Ln, bias=eps_t[:, 0:1], scale=1.0 / n).then_inc(l_act, 1)
            for i in range(2):
                act.wait_ge(l_act, i + 1)
                a(l_inv[:, i, :], l_ln[:, i, :], ACT.Exp, scale=-0.5).then_inc(l_act, 1)
            for i in range(5):
                act.wait_ge(latn_done, 1 if i < 3 else 2)
                a(l_hi[:, i, :], lat_n[:, i, :], ACT.Copy, scale=v(V_QA + i)).then_inc(lh_done, 1)

            def unit_raw(un):
                k, n = At(K_HEAD + un), un % 4
                act.wait_ge(w_used, 2 * C_HEAD + un + 1)
                hs = slice(2 * (n % 2), 2 * (n % 2) + 2)
                if n < 2:
                    a(q_sq[:, hs, :], linp(k, slice(0, T2), slice(0, QK)), ACT.Square)
                    a(q_pre[0:HD, hs, :], linp(k, slice(0, T2), slice(0, HD)), ACT.Copy,
                      scale=v(V_QG, rows=slice(0, HD))).then_inc(raw_read, 1)
                else:
                    a(k_sq[0:HD, hs, :], linp(k, slice(0, T), slice(0, HD)), ACT.Square)
                    a(k_pre[0:HD, hs, :], linp(k, slice(0, T), slice(0, HD)), ACT.Copy,
                      scale=v(V_KG, rows=slice(0, HD)))
                    a(v_t[HD:P, hs, :], linp(k, slice(0, T), slice(HD, P)), ACT.Copy).then_inc(raw_read, 1)

            def unit_inv(un):
                s, n = un // 4, un % 4
                k = At(K_HEAD + un)
                w_ = T2 if n < 2 else T
                if un >= 1:
                    act.wait_ge(ninv_done, un)
                act.wait_ge(nsum_done, un + 1)
                if n < 2:
                    a(n_ln[:, :, 0:w_], linp(k, slice(0, w_), slice(0, QK)), ACT.Ln, bias=eps_t[0:QK, 0:1],
                      scale=1.0 / QK).then_inc(drained[k.parity], 1)
                else:
                    hs = slice(2 * (n % 2), 2 * (n % 2) + 2)
                    a(n_ln[:, :, 0:w_], linp(k, slice(0, w_), slice(0, QK)), ACT.Ln, bias=eps_t[0:QK, 0:1],
                      scale=1.0 / QK)
                    a(v_tok[s % 2][:, hs, 1:3, :], linp(k, slice(272, 400)).rearrange("p h (t d) -> p h t d", d=HD),
                      ACT.Copy)
                    a(v_tok[s % 2][0:META, hs, 0, :], linp(k, slice(400, 464), slice(0, META)), ACT.Copy)\
                        .then_inc(drained[k.parity], 1)
                act.wait_ge(drained[k.parity], k.half + 1)
                if un >= 1:
                    act.wait_ge(fin_done, un)
                if n < 2:
                    a(n_inv[:, :, 0:w_], n_ln[:, :, 0:w_], ACT.Exp, scale=-0.5, bias=eps_t[0:QK, 1:2])\
                        .then_inc(ninv_done, 1)
                else:
                    a(n_inv[:, :, 0:w_], n_ln[:, :, 0:w_], ACT.Exp, scale=-0.5).then_inc(ninv_done, 1)

            def exps(n):
                p = n % 2
                act.wait_ge(nm_done, n + 1)
                a(pr[p][:, 0:144], s_m[p][:, 0:144], ACT.Exp, bias=nmx[p][:, 0:1], accum_out=rsum[p][:, 0:1])
                a(pr[p][:, 144:416], s_m[p][:, 144:416], ACT.Exp, bias=nmx[p][:, 1:2], accum_out=rsum[p][:, 1:2])\
                    .then_inc(ex_done, 1)

            def p_t0_copy(n):
                act.wait_ge(pT_done, n + 1)
                a(p_t0[:, :], ps4[0:META, 256:512], ACT.Copy).then_inc(pt0_done, 1)

            def o_high(n):
                act.wait_ge(pv_done, 2 * n + 2)
                a(o_hi[:, n, :], ps4[:, 0:T2], ACT.Copy).then_inc(oh_done, 1)

            for t in range(MLA_STEPS):
                if 0 <= t - 2 < 16:
                    unit_inv(t - 2)
                if t >= 8:
                    p_t0_copy(t - 8)
                if 0 <= t - 6 < 16:
                    exps(t - 6)
                if t < 16:
                    unit_raw(t)
                    nxt = t + 4
                    hi(At(C_HEAD).page(nxt), PAGE if nxt >= 16 else (6 if nxt % 4 < 2 else 4) * P)
                if t >= 9 and t % 2:
                    o_high((t - 9) // 2)
            for i in range(4):
                hi2(At(C_MOUT + 2 + i))
                if i in (1, 3):
                    for kt in range(2 * i - 2, 2 * i + 2):
                        norm_hi(3, At(kt))
            mlp(1, 3, C_UP1, K_UP1, C_DN1, False)

            def exps2(n):
                p = n % 2
                act.wait_ge(nm2_done, n + 1)
                for qt in range(2):
                    ins = a(pr2[p][:, qt * 256:(qt + 1) * 256], s_m2[p][:, qt * 256:(qt + 1) * 256], ACT.Exp,
                            bias=nmx2[p][:, qt:qt + 1], accum_out=rsum2[p][:, qt:qt + 1])
                ins.then_inc(ex2_done, 1)

            def ya_high(q):
                act.wait_ge(pv2_done, 2 * q + 2)
                a(ya_hi[:, q, :], ps4[:, 0:T2], ACT.Copy).then_inc(yah_done, 1)

            for i in range(20):
                k = At(K_IN2 + i)
                hi2(At(C_IN2 + i + 2))
                if i == 0:
                    norm_inv(4)
                if i < 4:
                    act.wait_ge(drained[k.parity], k.half + 1)
                    a(qk_sq[i % 2][:, :, :], qk_r[:, 2 * i:2 * i + 2, :], ACT.Square).then_inc(qksq_done, 1)
                if 1 <= i <= 4:
                    j = i - 1
                    act.wait_ge(qkstat_done, j + 1)
                    if j:
                        act.wait_ge(qkinv_done, j)
                    a(qk_ln[:, :, :].rearrange("p a t -> p (a t)"), (ps5, ps6)[j % 2][:, :], ACT.Ln,
                      bias=eps_t[:, 0:1], scale=1.0 / HD).then_inc(qkln_done, 1)
                    act.wait_ge(qkln_done, j + 1)
                    a(qk_inv[j % 2][:, :, :], qk_ln[:, :, :], ACT.Exp, scale=-0.5,
                      bias=eps_t[:, 2:3] if j < 2 else 0.0).then_inc(qkinv_done, 1)
                if i == 6:
                    act.wait_ge(vT_done, 1)
                    a(v2[:, 0, :], ps7[:, :], ACT.Copy).then_inc(v2_done, 1)
                    a(v2[:, 1, :], ps4[:, :], ACT.Copy).then_inc(v2_done, 1)
                if 6 <= i < 10:
                    j = i - 6
                    act.wait_ge(z_done, j + 1)
                    a(cv2[:, j, :], zc[:, j, 0:T2], ACT.Copy, scale=v(V_CONV2 + 3 * j)).then_inc(cv2_0, 1)
                if 6 <= i < 14:
                    exps2(i - 6)
                if i in (10, 11):
                    j = i - 10
                    act.wait_ge(yb_done, j + 1)
                    a(yb_hi[:, 2 * j:2 * j + 2, :], yb[:, 2 * j:2 * j + 2, :], ACT.Copy).then_inc(ybh_done, 1)
                if i >= 12:
                    j = i - 12
                    act.wait_ge(gclamp, j + 1)
                    sigmoid(gate[:, 2 * j:2 * j + 2, :], gate_step, At(3 * j))
                if 9 <= i < 16 and i % 2:
                    ya_high((i - 9) // 2)

            for b in range(4):
                hi2(At(C_BR + b + 2))
                act.wait_ge(m_done, b + 1)
                a(m_hi[:, 2 * b:2 * b + 2, :], m_a[:, :, :], ACT.Copy).then_inc(mh_done, 1)
            for i in range(4):
                hi2(At(C_WO + 2 + i))
                for kt in (2 * i, 2 * i + 1):
                    norm_hi(5, At(kt))
            mlp(2, 5, C_UP2, K_UP2, C_DN2, True)

        @block.vector
        def _(dve):
            tt, ts, stt = nc.vector.tensor_tensor, nc.vector.tensor_scalar, nc.vector.scalar_tensor_tensor

            def lo(pg, n=PAGE):
                dve.wait_ge(w_hi_done, (pg + 1).value)
                tt(w_lo[pg.slot][:, 0:n], w_raw[pg.slot][:, 0:n], w_hi[pg.slot][:, 0:n].bitcast(F32), ALU.subtract)\
                    .then_inc(w_lo_done[pg.slot], 1)

            def lo2(c):
                lo(c.page(0))
                lo(c.page(1))

            def norm_lo(norm, kt):
                n, tk = width(norm), tokens(norm)
                dve.wait_ge(xh_done, (kt + (KD * norm + 1)).value)
                stt(x_lo[:, kt.value, 0:n], h[:, kt.value, tk], gain(norm, kt.value),
                    x_hi[:, kt.value, 0:n].bitcast(F32), ALU.mult, ALU.subtract).then_inc(xl_done, 1)

            dve.memset(eps_t[:, 0:1], EPS).then_inc(memset_done, 1)
            dve.memset(eps_t[:, 1:2], float(np.log(QK ** -0.5))).then_inc(memset_done, 1)
            dve.memset(eps_t[:, 2:3], float(np.log(HD ** -0.5))).then_inc(memset_done, 1)
            dve.memset(u[:, :, 0:3], 0.0).then_inc(memset_done, 1)
            dve.wait_ge(small_in, 32)
            for kt in range(KD):
                norm_lo(0, At(kt))
                if kt % 2:
                    lo(Page(kt // 2))
            k = At(K_DT)
            r32 = slice(0, 32)
            dve.wait_ge(w_used, 1)
            dve.wait_ge(r_done, 1)
            tt(dtx[:, :], lin[r32, 0, 0:T], r_inv[r32, :], ALU.mult).then_inc(drained[0], 1)
            dve.wait_ge(drained[0], 1)
            ts(dtb[:, :], dtx[:, :], v(V_DTB, rows=r32), None, ALU.add).then_inc(dt_dve, 1)
            dve.wait_ge(dt_dve, 1)
            ts(dtx[:, :], dtb[:, :], -1.0, None, ALU.mult).then_inc(dt_dve, 1)
            dve.wait_ge(dt_dve, 2)
            tt(dta[:, :], dtb[:, :], dtx[:, :], ALU.max).then_inc(dt_dve, 1)
            lo2(At(2))
            dve.wait_ge(dt_act, 3)
            stt(dt_t[:, :], dtb[:, :], 0.0, dta[:, :], ALU.max, ALU.add).then_inc(dt_dve, 1)
            dve.wait_ge(dt_dve, 4)
            ts(dtx[:, :], dt_t[:, :], a_exp[:, 0:1], -1.0, ALU.mult, ALU.mult).then_inc(dt_dve, 1)
            dve.wait_ge(dt_dve, 5)
            nc.vector.tensor_tensor_scan(acs[:, :], cst[r32, N_ONES:N_ONES + 1].broadcast_to([32, T]), dtx[:, :],
                                         0.0, ALU.mult, ALU.add).then_inc(dt_dve, 1)

            def dt_columns():
                dve.wait_ge(dtT_done, 1)
                src = ps4[:, 0:192].rearrange("p (i h) -> p i h", h=32)
                for i, sign in ((0, 1.0), (3, -1.0)):
                    ts(cols[:, i:i + 2, :], src[:, i:i + 2, :], sign, None, ALU.mult).then_inc(cols_done, 1)
                    ts(cols[0:META, i + 2, :], src[0:META, i + 2, :], sign, None, ALU.mult).then_inc(cols_done, 1)

            def evac_u(s, pair):
                c, k = s.times(3, C_GRP + pair), s.times(3, K_GRP + pair)
                dve.wait_ge(w_used, (c + 1).page().value)
                tt(u[:, 2 * pair:2 * pair + 2, 3:3 + T], linp(k, slice(0, T)), over(r_inv[:, :], 2), ALU.mult)\
                    .then_inc(drained[k.parity], 1)

            def conv(s, pair):
                for tap in (1, 2, 3):
                    for i in range(2):
                        q = 2 * pair + i
                        if tap == 1:
                            dve.wait_ge(cv0_done, s.times(4, q + 1).value)
                        else:
                            dve.wait_ge(cv_step, s.times(12, 6 * pair + 2 * (tap - 2) + i + 1).value)
                        stt(cv[:, q, :], u[:, q, tap:tap + T], v(s.times(20, V_CONV + 5 * q + tap).value), cv[:, q, :],
                            ALU.mult, ALU.add).then_inc(cv_step, 1)

            def clamp(dst, x):
                ts(dst, x, CLAMP, None, ALU.max).then_inc(clamped, 1)

            def silu(s, n, dst, x, sgm):
                dve.wait_ge(sg_step, s.times(9, 3 * (n + 1)).value)
                tt(dst, x, sgm, ALU.mult).then_inc(silu_done, 1)

            def head_mix(g, j):
                h_at = g.times(4, j)
                dve.wait_ge(ee_done, (h_at + 1).value)
                for s, (rows, at, n) in enumerate(((P, 0, T), (P, T, 144), (META, 416, 16))):
                    ins = stt(mm[0:rows, j, at:at + n], dd[g.parity][0:rows, j, at:at + n],
                              cols[0:rows, s, bass.ds(h_at.value, 1)], cbm[0:rows, at:at + n], ALU.mult, ALU.mult)
                ins.then_inc(mm_done, 1)

            def slot(s, has_lin=True, has_scan=True, has_stat=True, first=False):
                c = s.times(3, C_GRP)
                g, gs = s + (-1), s + (-2)
                if has_stat:
                    if gs.base:
                        dve.wait_ge(gl_done, gs.times(2).value)
                    for q in range(2):
                        dve.wait_ge(y_done, gs.times(2, q + 1).value)
                        stt(y1[:, q, :], xs_s[gs.parity][:, q, :], v(gs.times(2, V_DSKIP + q).value),
                            (ps6, ps7)[q][:, 0:T], ALU.mult, ALU.add).then_inc(y_read, 1)
                if has_scan:
                    silu(g, 1, bc_s[:, :, :], cv[:, 2:4, :], sg[:, 2:4, :])
                    silu(g, 2, z_s[g.parity][:, :, :], z_raw[:, :, :], z_sg[:, :, :])
                if has_lin:
                    lo((c + 2).page(0))
                    evac_u(s, 0)
                    conv(s, 0)
                    dve.wait_ge(cv_step, s.times(12, 6).value)
                    clamp(sg[:, 0:2, :], cv[:, 0:2, :])
                if first:
                    dt_columns()
                if has_scan:
                    if g.base == 0:
                        dve.wait_ge(cols_done, 4)
                    dve.wait_ge(cbm_done, (g + 1).value)
                    for j in range(HPG):
                        head_mix(g, j)
                if has_lin:
                    evac_u(s, 1)
                    lo((c + 3).page(0))
                    silu(s, 0, xs_s[s.parity][:, :, :], cv[:, 0:2, :], sg[:, 0:2, :])
                    conv(s, 1)
                    dve.wait_ge(cv_step, s.times(12, 12).value)
                    clamp(sg[:, 2:4, :], cv[:, 2:4, :])
                if has_stat:
                    dve.wait_ge(ginv_done, (gs + 1).value)
                    tt(y1[:, :, :], y2[:, :, :], over(g_inv[:, :], 2), ALU.mult).then_inc(y3_done, 1)
                if has_lin:
                    lo((c + 4).page(0))
                if has_stat:
                    for q in range(2):
                        t = gs.times(2, q)
                        dve.wait_ge(gh_done, (t + 1).value)
                        stt(g_lo[:, t.value, :], y1[:, q, :], v((t + V_SNORM).value),
                            g_hi[:, t.value, :].bitcast(F32), ALU.mult, ALU.subtract).then_inc(gl_done, 1)
                if has_lin:
                    k = s.times(3, K_GRP + 2)
                    dve.wait_ge(w_used, (c + 3).page().value)
                    tt(z_raw[:, :, :], linp(k, slice(0, T)), over(r_inv[:, :], 2), ALU.mult)\
                        .then_inc(drained[k.parity], 1)
                    dve.wait_ge(drained[k.parity], k.half + 1)
                    clamp(z_sg[:, :, :], z_raw[:, :, :])

            slot(At(0), has_scan=False, has_stat=False, first=True)
            slot(At(1), has_stat=False)
            with dve.Fori(0, SLOT_TURNS) as turn:
                for i in range(2):
                    slot(At(2 + i, 2, turn))
            slot(At(8), has_lin=False)
            slot(At(9), has_lin=False, has_scan=False)

            def add_pair(k, used, i, tk):
                dve.wait_ge(w_used, used)
                n = T - tk.start
                tt(h[:, 2 * i:2 * i + 2, tk], h[:, 2 * i:2 * i + 2, tk], linp(k, slice(0, n)), ALU.add)\
                    .then_inc(drained[k.parity], 1)

            for i in range(8):
                lo2(At(C_SOUT + 2 + i))
                if i in (3, 7):
                    for j in (i // 4 * 2, i // 4 * 2 + 1):
                        add_pair(At(K_SOUT + j), 2 * C_SOUT + 8 * (i // 4) + 6 + 2 * (j % 2), j, slice(0, T))
                    for kt in range(i - 3, i + 1):
                        norm_lo(1, At(kt))

            def mlp(m, norm, c_up, c_dn, k_dn, last):
                n, tk = width(norm), tokens(norm)

                def up(i, t):
                    lo2(t + (c_up + 2))
                    k = t + (K_UP0, K_UP1, K_UP2)[m]
                    dve.wait_ge(drained[k.parity], k.half + 1)
                    tt(relu_sq[i][:, :, 0:n], relu[i][:, :, 0:n], relu[i][:, :, 0:n], ALU.mult).then_inc(rsq_done, 1)
                    dve.wait_ge(hh_done, (t + (16 * m + 1)).value)
                    dve.wait_ge(rsq_done, (t + (16 * m + 1)).value)
                    at = t.times(2)
                    tt(hid_lo[:, bass.ds(at.value, 2), 0:n], relu_sq[i][:, :, 0:n],
                       hid_hi[:, bass.ds(at.value, 2), 0:n].bitcast(F32), ALU.subtract).then_inc(hl_done, 1)

                with dve.Fori(0, 8) as turn:
                    for i in range(2):
                        up(i, At(i, 2, turn))

                def down(i, t, lows=True):
                    if lows:
                        lo2(t.times(2, c_dn + 2))
                        lo2(t.times(2, c_dn + 3))
                    k = t + k_dn
                    dve.wait_ge(w_used, t.times(2, c_dn + 2).page().value)
                    tt(down_r[i][:, 0:n], lin[:, 2 * k.parity, 0:n], r_inv[:, 0:n], ALU.mult)\
                        .then_inc(drained[k.parity], 1)
                    dve.wait_ge(drained[k.parity], k.half + 1)
                    tt(h[:, t.value, tk], h[:, t.value, tk], down_r[i][:, 0:n], ALU.add).then_inc(h_mlp, 1)
                    if not last:
                        norm_lo(norm + 1, t)

                dve.wait_ge(r_done, norm + 1)
                with dve.Fori(0, 3) as turn:
                    for i in range(2):
                        down(i, At(i, 2, turn))
                down(0, At(6))
                down(1, At(7), not last)

            mlp(0, 1, C_UP0, C_DN0, K_DN0, False)

            for i in range(3):
                k = At(K_MIN + i)
                lo(At(C_MIN + 2 + i).page(0), (8, 6, 4)[i] * P)
                dve.wait_ge(w_used, 2 * (C_MIN + i + 1))
                dve.wait_ge(r_done, 3)
                tt(lat[:, 2 * i:2 * i + 2, :], linp(k, slice(0, T)), over(r_inv[:, :], 2), ALU.mult)\
                    .then_inc(drained[k.parity], 1)
                lo(At(C_MIN + 2 + i).page(1), (8, 6, 4)[i] * P)
            k = At(K_MIN + 2)
            dve.wait_ge(drained[k.parity], k.half + 1)
            dve.wait_ge(rope_done, 2)
            rr, rs_ = slice(HD, QK), slice(QK, P)
            tt(rot_a[rr, 0, :], lat[rr, 5, :], rope_k[rr, :], ALU.mult).then_inc(krope, 1)
            tt(rot_b[rr, 0, :], lat[rs_, 5, :], rope_k[rs_, :], ALU.mult).then_inc(krope, 1)
            dve.wait_ge(krope, 2)
            tt(k_pre[rr, :, :], over(rot_a[rr, 0, :], 4), over(rot_b[rr, 0, :], 4), ALU.add).then_inc(krope, 1)
            tt(k_sq[rr, :, :], over(lat[rr, 5, :], 4), over(lat[rr, 5, :], 4), ALU.mult).then_inc(krope, 1)
            dve.wait_ge(l_act, 3)
            tt(lat_n[:, 0:3, :], lat[:, 0:3, :], over(l_inv[:, 0, :], 3), ALU.mult).then_inc(latn_done, 1)
            dve.wait_ge(l_act, 4)
            tt(lat_n[:, 3:5, :], lat[:, 3:5, :], over(l_inv[:, 1, :], 2), ALU.mult).then_inc(latn_done, 1)
            for i in range(5):
                dve.wait_ge(lh_done, i + 1)
                if i == 0:
                    dve.wait_ge(latn_done, 2)
                stt(l_lo[:, i, :], lat_n[:, i, :], v(V_QA + i), l_hi[:, i, :].bitcast(F32), ALU.mult, ALU.subtract)\
                    .then_inc(ll_done, 1)

            def rotate(t):
                s, n = t // 4, t % 4
                k = At(K_HEAD + t)
                un = 2 * s + n
                dve.wait_ge(raw_read, 4 * s + n + 1)
                tq = slice(META, T)
                if un:
                    dve.wait_ge(rot_sum, un)
                else:
                    dve.wait_ge(krope, 3)
                tt(rot_a[rr, :, 0:T2], linp(k, slice(0, T2), rr), over(rope_q[rr, tq], 2), ALU.mult)\
                    .then_inc(rot_done, 1)
                tt(rot_b[rr, :, 0:T2], linp(k, slice(0, T2), rs_), over(rope_q[rs_, tq], 2), ALU.mult)\
                    .then_inc(rot_done, 1)
                dve.wait_ge(rot_done, 2 * un + 2)
                tt(q_pre[rr, 2 * n:2 * n + 2, :], rot_a[rr, :, 0:T2], rot_b[rr, :, 0:T2], ALU.add).then_inc(rot_sum, 1)

            def finish(un):
                s, n = un // 4, un % 4
                dve.wait_ge(ninv_done, un + 1)
                hs = slice(2 * (n % 2), 2 * (n % 2) + 2)
                if n < 2:
                    dve.wait_ge(rot_sum, 2 * s + n + 1)
                    ins = tt(q_fin[s % 2][:, hs, :], q_pre[:, hs, :], n_inv[:, :, 0:T2], ALU.mult)
                else:
                    if s == 0:
                        dve.wait_ge(krope, 3)
                    ins = tt(k_fin[s % 2][:, hs, :], k_pre[:, hs, :], n_inv[:, :, :], ALU.mult)
                ins.then_inc(fin_done, 1)

            def maxima(n):
                p, o = n % 2, (ps5, ps6)[n % 2]
                dve.wait_ge(s_done, n + 1)
                for i, sl in enumerate((slice(0, 144), slice(144, 416))):
                    ins = nc.vector.tensor_tensor_reduce(
                        out=s_m[p][:, sl], in0=o[:, sl], in1=cst[:, N_MLA + sl.start:N_MLA + sl.stop], scale=1.0,
                        scalar=-3e38, op0=ALU.add, op1=ALU.max, accum_out=mx[p][:, i:i + 1])
                ins.then_inc(sm_done, 1)
                dve.wait_ge(sm_done, n + 1)
                ts(nmx[p][:, :], mx[p][:, :], -1.0, None, ALU.mult).then_inc(nm_done, 1)

            def weigh(n):
                p = n % 2
                dve.wait_ge(ex_done, n + 1)
                nc.vector.reciprocal(rinv[p][:, :], rsum[p][:, :]).then_inc(ri_done, 1)
                dve.wait_ge(ri_done, n + 1)
                ts(pr[p][:, 0:144], pr[p][:, 0:144], rinv[p][:, 0:1], None, ALU.mult)
                ts(pr[p][:, 144:416], pr[p][:, 144:416], rinv[p][:, 1:2], None, ALU.mult).then_inc(p_done, 1)

            def p_t_copy(n):
                dve.wait_ge(pT_done, n + 1)
                nc.vector.tensor_copy(p_t[:, :], ps7[:, 0:384]).then_inc(pt_done, 1)

            def o_low(n):
                dve.wait_ge(oh_done, n + 1)
                tt(o_lo[:, n, :], ps4[:, 0:T2], o_hi[:, n, :].bitcast(F32), ALU.subtract).then_inc(ol_done, 1)

            for t in range(MLA_STEPS):
                if t >= 8:
                    p_t_copy(t - 8)
                if 0 <= t - 6 < 16:
                    maxima(t - 6)
                if 0 <= t - 2 < 16:
                    finish(t - 2)
                if t < 16:
                    if t % 4 < 2:
                        rotate(t)
                    nxt = t + 4
                    lo(At(C_HEAD).page(nxt), PAGE if nxt >= 16 else (6 if nxt % 4 < 2 else 4) * P)
                if 0 <= t - 6 < 16:
                    weigh(t - 6)
                if t >= 9 and t % 2:
                    o_low((t - 9) // 2)

            for i in range(4):
                lo2(At(C_MOUT + 2 + i))
                if i in (1, 3):
                    for j in (i - 1, i):
                        add_pair(At(K_MOUT + j), 2 * (C_MOUT + j + 1), j, slice(META, T))
                    for kt in range(2 * i - 2, 2 * i + 2):
                        norm_lo(3, At(kt))
            mlp(1, 3, C_UP1, C_DN1, K_DN1, False)

            def maxima2(n):
                p, o = n % 2, (ps5, ps6)[n % 2]
                dve.wait_ge(s2_done, n + 1)
                if n == 0:
                    dve.wait_ge(bias_done, 16)
                for qt in range(2):
                    sl = slice(qt * 256, (qt + 1) * 256)
                    ins = nc.vector.tensor_tensor_reduce(
                        out=s_m2[p][:, sl], in0=o[:, sl], in1=bias_mask[:, n, qt, :], scale=1.0,
                        scalar=-3e38, op0=ALU.add, op1=ALU.max, accum_out=mx2[p][:, qt:qt + 1])
                ins.then_inc(sm2_done, 1)
                dve.wait_ge(sm2_done, n + 1)
                ts(nmx2[p][:, :], mx2[p][:, :], -1.0, None, ALU.mult).then_inc(nm2_done, 1)

            def weigh2(n):
                p = n % 2
                dve.wait_ge(ex2_done, n + 1)
                nc.vector.reciprocal(rinv2[p][:, :], rsum2[p][:, :]).then_inc(ri2_done, 1)
                dve.wait_ge(ri2_done, n + 1)
                for qt in range(2):
                    sl = slice(qt * 256, (qt + 1) * 256)
                    ins = ts(pr2[p][:, sl], pr2[p][:, sl], rinv2[p][:, qt:qt + 1], None, ALU.mult)
                ins.then_inc(p2_done, 1)

            for i in range(20):
                c, k = At(C_IN2 + i), At(K_IN2 + i)
                if 8 <= i < 16:
                    dve.wait_ge(pT2_done, i - 7)
                    nc.vector.tensor_copy(p_t2[:, :], ps7[:, :]).then_inc(pt2_done, 1)
                lo((c + 2).page(0))
                dve.wait_ge(w_used, (c + 1).page().value)
                if i == 0:
                    dve.wait_ge(r_done, 5)
                if i < 4:
                    dst = qk_r[:, 2 * i:2 * i + 2, :]
                elif i < 6:
                    dst = v_r[:, 2 * (i - 4):2 * (i - 4) + 2, :]
                elif i < 10:
                    dst = cc_ch[:, :, :]
                elif i < 12:
                    dst = cb_r[:, 2 * (i - 10):2 * (i - 10) + 2, :]
                else:
                    dst = gate[:, 2 * (i - 12):2 * (i - 12) + 2, :]
                tt(dst, linp(k, slice(0, T2)), over(r_inv[:, 0:T2], 2), ALU.mult).then_inc(drained[k.parity], 1)
                lo((c + 2).page(1))
                if i == 0:
                    dve.memset(zc[:, :, 0:1], 0.0)
                    dve.memset(zc[:, :, T2 + 1:T2 + 2], 0.0)
                if 1 <= i <= 4:
                    j = i - 1
                    dve.wait_ge(qkinv_done, j + 1)
                    for q in range(2):
                        ins = stt(qk_f[:, 2 * j + q, :], qk_r[:, 2 * j + q, :], v(V_QN2 if j < 2 else V_KN2),
                                  qk_inv[j % 2][:, q, :], ALU.mult, ALU.mult)
                    ins.then_inc(qkf_done, 1)
                if 6 <= i < 10:
                    j = i - 6
                    dve.wait_ge(drained[k.parity], k.half + 1)
                    tt(zc[:, j, 1:T2 + 1], cc_ch[:, 0, :], cc_ch[:, 1, :], ALU.mult).then_inc(z_done, 1)
                    for tap in (1, 2):
                        if tap == 1:
                            dve.wait_ge(cv2_0, j + 1)
                            dve.wait_ge(z_done, j + 1)
                        else:
                            dve.wait_ge(cv2_step, 2 * j + 1)
                        stt(cv2[:, j, :], zc[:, j, tap:tap + T2], v(V_CONV2 + 3 * j + tap), cv2[:, j, :],
                            ALU.mult, ALU.add).then_inc(cv2_step, 1)
                if 6 <= i < 14:
                    maxima2(i - 6)
                if 6 <= i < 14:
                    weigh2(i - 6)
                if i in (10, 11):
                    j = i - 10
                    dve.wait_ge(drained[k.parity], k.half + 1)
                    dve.wait_ge(cv2_step, 8)
                    tt(yb[:, 2 * j:2 * j + 2, :], cv2[:, 2 * j:2 * j + 2, :], cb_r[:, 2 * j:2 * j + 2, :], ALU.mult)\
                        .then_inc(yb_done, 1)
                    dve.wait_ge(ybh_done, j + 1)
                    dve.wait_ge(yb_done, j + 1)
                    tt(yb_lo[:, 2 * j:2 * j + 2, :], yb[:, 2 * j:2 * j + 2, :],
                       yb_hi[:, 2 * j:2 * j + 2, :].bitcast(F32), ALU.subtract).then_inc(ybl_done, 1)
                if 9 <= i < 16 and i % 2:
                    q = (i - 9) // 2
                    dve.wait_ge(yah_done, q + 1)
                    tt(ya_lo[:, q, :], ps4[:, 0:T2], ya_hi[:, q, :].bitcast(F32), ALU.subtract).then_inc(yal_done, 1)

            for b in range(4):
                c = At(C_BR + b)
                for n, dst in enumerate((m_a, m_b)):
                    k = At(K_BR + 2 * b + n)
                    dve.wait_ge(w_used, c.page(n + 1).value)
                    dve.wait_ge(gate_step, min(24, 3 * (2 * b + 2)))
                    if n == 0 and b:
                        dve.wait_ge(ml_done, b)
                    tt(dst[:, :, :], linp(k, slice(0, T2)), gate[:, 4 * b + n:4 * b + n + 3:2, :], ALU.mult)\
                        .then_inc(drained[k.parity], 1)
                    lo((c + 2).page(n))
                for n in range(2):
                    k = At(K_BR + 2 * b + n)
                    dve.wait_ge(drained[k.parity], k.half + 1)
                tt(m_a[:, :, :], m_a[:, :, :], m_b[:, :, :], ALU.add).then_inc(m_done, 1)
                dve.wait_ge(m_done, b + 1)
                dve.wait_ge(mh_done, b + 1)
                tt(m_lo[:, 2 * b:2 * b + 2, :], m_a[:, :, :], m_hi[:, 2 * b:2 * b + 2, :].bitcast(F32),
                   ALU.subtract).then_inc(ml_done, 1)
            for i in range(4):
                lo(At(C_WO + 2 + i).page(0))
                add_pair(At(K_WO + i), 2 * (C_WO + i + 1), i, slice(META, T))
                lo(At(C_WO + 2 + i).page(1))
                for kt in (2 * i, 2 * i + 1):
                    norm_lo(5, At(kt))
            mlp(2, 5, C_UP2, C_DN2, K_DN2, True)

        @block.gpsimd
        def _(pool):
            tt, ts = nc.gpsimd.tensor_tensor, nc.gpsimd.tensor_scalar

            def norm_sum(norm):
                n = width(norm)
                for kt in range(1, KD):
                    pool.wait_ge(hsq_done, KD * norm + kt + 1)
                    if kt > 1:
                        pool.wait_ge(hsum_done, (KD - 1) * norm + kt - 1)
                    tt(h_sq[:, 0, 0:n], h_sq[:, 0, 0:n], h_sq[:, kt, 0:n], ALU.add).then_inc(hsum_done, 1)

            for rq in range(4):
                pool.dma_start(bias_mask[(rq % 2) * 64:(rq % 2 + 1) * 64, :, rq // 2, :], rpb[:, :, 3 - rq:7 - rq, :]
                               .rearrange("q h r c -> q h (r c)")).then_inc(rpb_in, 16)
            norm_sum(0)
            pool.wait_ge(dt_dve, 6)
            pool.dma_start(acs_dram, acs[:, :]).then_inc(acs_out, 16)
            pool.wait_ge(acs_out, 16)

            def lo(pg):
                pool.wait_ge(w_hi_done, (pg + 1).value)
                tt(w_lo[pg.slot][:, :], w_raw[pg.slot][:, :], w_hi[pg.slot][:, :].bitcast(F32), ALU.subtract)\
                    .then_inc(w_lo_done[pg.slot], 1)

            def acs_rows(g):
                if g.base:
                    pool.wait_ge(dd_done, g.times(2).value)
                src = acs_dram[bass.ds(g.times(4).value, 4), :].partition_broadcast(P)
                pool.dma_start(acs_bc[:, :, :], src).then_inc(acs_in, 16)

            def masked_rows(g, half):
                hs = slice(2 * half, 2 * half + 2)
                d = dd[g.parity]
                if half == 0:
                    pool.wait_ge(acs_in, (g + 1).times(16).value)
                    if g.base >= 2:
                        pool.wait_ge(mm_done, g.times(4, -4).value)
                for rows, at, n, l0 in ((P, 0, T, 0), (P, T, 144, 128), (META, 416, 16, 256)):
                    ins = tt(d[0:rows, hs, at:at + n], acs_bc[0:rows, hs, l0:T],
                             over(cst[0:rows, N_SSD + at:N_SSD + at + n], 2), ALU.add)
                ins.then_inc(dd_done, 1)

            def slot(s, has_lin=True, has_stat=True, load=True):
                c, gs = s.times(3, C_GRP), s + (-2)
                if has_stat:
                    pool.wait_ge(y_read, gs.times(2, 2).value)
                    pool.wait_ge(silu_done, gs.times(3, 3).value)
                    if gs.base:
                        pool.wait_ge(y3_done, gs.value)
                    tt(y2[:, :, :], y1[:, :, :], z_s[gs.parity][:, :, :], ALU.mult).then_inc(y2_done, 1)
                    pool.wait_ge(ysq_done, (gs + 1).value)
                    tt(y_sum[:, :], h_sq[:, 0, :], h_sq[:, 1, :], ALU.add).then_inc(ysum_done, 1)
                if has_lin:
                    lo((c + 2).page(1))
                    masked_rows(s, 0)
                    lo((c + 3).page(1))
                    masked_rows(s, 1)
                    if load:
                        acs_rows(s + 1)
                    lo((c + 4).page(1))

            acs_rows(At(0))
            slot(At(0), has_stat=False)
            slot(At(1), has_stat=False)
            with pool.Fori(0, 2) as turn:
                for i in range(2):
                    slot(At(2 + i, 2, turn))
            slot(At(6))
            slot(At(7), load=False)
            slot(At(8), has_lin=False)
            slot(At(9), has_lin=False)

            norm_sum(1)
            pool.wait_ge(rpb_in, 16 * 4)
            pool.wait_ge(small_in, 32)
            for hd in range(NA_HEADS):
                for qt in range(2):
                    b = bias_mask[:, hd, qt, :].rearrange("p (r c) -> p r c", c=64)
                    tt(b, b, over(cst[:, N_NA:N_NA + 64], 4), ALU.add).then_inc(bias_done, 1)
            norm_sum(2)
            pool.wait_ge(stat_done, 3)
            tb = slice(HD, P)
            ts(rope_q[tb, :], cst[tb, N_ROPE:N_ROPE + T], v(V_QG, rows=tb), None, ALU.mult).then_inc(rope_done, 1)
            ts(rope_k[tb, :], cst[tb, N_ROPE:N_ROPE + T], v(V_KG, rows=tb), None, ALU.mult).then_inc(rope_done, 1)
            norm_sum(3)
            norm_sum(4)
            for j in range(8):
                k = At(K_IN2 + 12 + j)
                pool.wait_ge(drained[k.parity], k.half + 1)
                gt = gate[:, 2 * j:2 * j + 2, :]
                ts(gt, gt, CLAMP, None, ALU.max).then_inc(gclamp, 1)
            norm_sum(5)


def constants():
    c = np.zeros((P, N_CONST), np.float32)
    p = np.arange(P)
    c[:, N_IDENT:N_IDENT + P] = np.eye(P)
    c[:, N_ONES:N_ONES + P] = 1.0
    c[:, N_BLK:N_BLK + P] = (p[:, None] // HD) == (p[None, :] // HD)
    tok = np.arange(T)
    c[:, N_SSD:N_SSD + T] = np.where(tok[None, :] >= p[:, None], 0.0, NEG)
    c[:, N_SSD + T:N_SSD + 416] = np.where(tok[None, 128:] >= 128 + p[:, None], 0.0, NEG)
    c[:META, N_SSD + 416:N_SSD + 432] = np.where(tok[None, 256:] >= 256 + p[:META, None], 0.0, NEG)
    c[:, N_MLA:N_MLA + 144] = np.where(tok[None, :144] <= META + p[:, None], 0.0, NEG)
    c[:, N_MLA + 144:N_MLA + 416] = np.where(tok[None, :] <= 144 + p[:, None], 0.0, NEG)
    inv = (1.0 / (np.float32(10000.0) ** (np.arange(0, 32, 2, dtype=np.float32) / np.float32(32)))).astype(np.float32)
    ang = (tok.astype(np.float32)[None, :] * inv[:, None]).astype(np.float32)
    cos, sin = np.cos(ang), np.sin(ang)
    c[HD:QK, N_ROPE:N_ROPE + T] = np.concatenate([cos, cos])
    c[QK:P, N_ROPE:N_ROPE + T] = np.concatenate([-sin, sin])
    qc, kc = (p % 64)[:, None], np.arange(64)[None, :]
    start = np.clip(qc - 8, 0, 48)
    c[:, N_NA:N_NA + 64] = np.where((kc >= start) & (kc < start + 16), 0.0, NEG)
    return c


def page(m):
    kt, ct = m.shape[0] // P, m.shape[1] // P
    row = m.reshape(kt, P, ct, P).transpose(1, 2, 0, 3).reshape(P, -1)
    return np.pad(row, ((0, 0), (0, PAGE - row.shape[1])))


def pad_cols(m, before, after):
    return np.pad(m, ((0, 0), (before, after)))


def weight_stream(i):
    w = []

    def wide(m):
        for t in range(0, m.shape[1], P):
            w.append(page(m[:, t:t + P]))

    s = i["ssd_w_in"][0]
    z, xs, b, c, dt = s[:, 0:2048], s[:, 2048:4096], s[:, 4096:5120], s[:, 5120:6144], s[:, 6144:6176]
    wide(pad_cols(dt, 0, 224))
    for g in range(GROUPS):
        wide(xs[:, 256 * g:256 * g + 256])
        wide(b[:, P * g:P * g + P])
        wide(c[:, P * g:P * g + P])
        wide(z[:, 256 * g:256 * g + 256])
    for r in range(2):
        for half in range(2):
            wide(i["ssd_w_out"][0][D * half:D * half + D, 512 * r:512 * r + 512])

    def mlp(up, down):
        wide(up)
        for t in range(8):
            for q in range(4):
                wide(down[D * q:D * q + D, P * t:P * t + P])

    mlp(i["mlp_w_up"][0], i["mlp_w_down"][0])
    m = i["mla_w_in"][0]
    kpe = m[:, 640:672]
    wide(np.concatenate([m[:, 0:640], pad_cols(kpe, 64, 0), kpe[:, 16:32], kpe[:, 0:16]], 1))
    q = i["mla_w_q_b"][0].reshape(384, MLA_HEADS, QK)
    q = np.concatenate([q, q[:, :, 80:96], q[:, :, 64:80]], 2).reshape(384, MLA_HEADS * P)
    for s4 in range(4):
        for m in (q, i["mla_w_kv_b"][0]):
            for half in range(2):
                w.append(page(m[:, 512 * s4 + 256 * half:512 * s4 + 256 * half + 256]))
    wide(i["mla_w_out"][0])
    mlp(i["mlp_w_up"][1], i["mlp_w_down"][1])
    n = i["w_in_2"][0]
    wide(n[:, 0:1536])
    cb, cc, ch, ga, gb = n[:, 1536:2048], n[:, 2048:2560], n[:, 2560:3072], n[:, 3072:4096], n[:, 4096:5120]
    for t in range(0, 512, P):
        wide(cc[:, t:t + P])
        wide(ch[:, t:t + P])
    wide(cb)
    for t in range(0, 1024, P):
        wide(ga[:, t:t + P])
        wide(gb[:, t:t + P])
    for t in range(0, 1024, 256):
        w.append(page(i["w_attn_branch_2"][0][:, t:t + 256]))
        w.append(page(i["w_conv_branch_2"][0][:, t:t + 256]))
    wide(i["w_o_2"][0])
    mlp(i["w_mlp_in_2"][0], i["w_mlp_out_2"][0])
    assert len(w) == N_PAGES
    return np.stack(w)


def small_params(i):
    vec = np.zeros((P, N_VEC), np.float32)

    def tiles(x):
        return x.reshape(-1, P).T

    gains = (i["ln_mix"][0], i["ln_mlp"][0], i["ln_mix"][1], i["ln_mlp"][1], i["norm1_g_2"][0], i["norm2_g_2"][0])
    for n, g in enumerate(gains):
        vec[:, V_GAIN + n * KD:V_GAIN + (n + 1) * KD] = tiles(g)
    cw, cb = i["ssd_conv_w"][0], i["ssd_conv_b"][0]
    for g in range(GROUPS):
        for q, t in enumerate((2 * g, 2 * g + 1, 16 + g, 24 + g)):
            at = V_CONV + (g * 4 + q) * 5
            vec[:, at:at + 4] = cw[:, P * t:P * t + P].T
            vec[:, at + 4] = cb[P * t:P * t + P]
    vec[:, V_DSKIP:V_DSKIP + 16] = tiles(np.repeat(i["ssd_d"][0], HD))
    vec[:, V_SNORM:V_SNORM + 16] = tiles(i["ssd_norm"][0])
    vec[:, V_QA:V_QA + 3] = tiles(i["mla_q_a_norm"][0])
    vec[:, V_KVA:V_KVA + 2] = tiles(i["mla_kv_a_norm"][0])
    for col, g in ((V_QG, i["mla_q_norm"][0]), (V_KG, i["mla_k_norm"][0])):
        vec[:, col] = np.concatenate([g, g[80:96], g[64:80]])
    for t in range(4):
        vec[:, V_CONV2 + 3 * t:V_CONV2 + 3 * t + 3] = i["conv_w_2"][0][:, P * t:P * t + P].T
    vec[:, V_QN2] = np.tile(i["q_norm_g_2"][0], 2)
    vec[:, V_KN2] = np.tile(i["k_norm_g_2"][0], 2)
    vec[0:32, V_DTB] = i["ssd_dt_bias"][0]
    vec[0:32, V_ALOG] = i["ssd_a_log"][0]
    return vec


def kernel(**inputs):
    import concourse.bacc as bacc
    from concourse.bass_utils import run_bass_kernel_spmd

    i = {name: np.asarray(a) for name, a in inputs.items()}
    tokens = np.concatenate([i["meta_tokens"], i["x"][0]], axis=0)
    padded = np.pad(i["rpb_2"][0][:, 4:11, :], ((0, 0), (0, 0), (48, 48)))
    rpb = np.stack([padded[:, :, 63 - qc:127 - qc] for qc in range(64)])
    arrays = {
        "w": weight_stream(i),
        "h0": np.ascontiguousarray(tokens.T.reshape(KD, P, T).transpose(1, 0, 2)),
        "vec": small_params(i),
        "const": constants(),
        "rpb": np.ascontiguousarray(rpb),
    }
    nc = bacc.Bacc("TRN2", target_bir_lowering=False, num_devices=1)
    aps = {n: nc.dram_tensor(n, a.shape, mybir.dt.from_np(a.dtype), kind="ExternalInput").ap()
           for n, a in arrays.items()}
    out = nc.dram_tensor("out", (P, KD, SEQ), F32, kind="ExternalOutput").ap()
    acs_dram = nc.dram_tensor("acs_dram", (32, T), F32, kind="Internal").ap()
    build(nc, aps["w"], aps["h0"], aps["vec"], aps["const"], aps["rpb"], out, acs_dram)
    r = run_bass_kernel_spmd(nc, [arrays], core_ids=[0])
    o = r.results[0]["out"]
    return np.ascontiguousarray(o.transpose(1, 0, 2).reshape(D, SEQ).T)[None]
```

```python
import numpy as np
from contextlib import ExitStack
import concourse.bass as bass
from concourse import mybir
from concourse.alu_op_type import AluOpType as ALU

F32 = mybir.dt.float32
F32R = mybir.dt.float32r
ACT = mybir.ActivationFunctionType

P = 128
D = 1024
KD = D // P
META = 16
SEQ = 256
T = META + SEQ
T2 = SEQ
EPS = 1e-6
GROUPS = 8
HPG = 4
HD = 64
FF_TILES = 32
PAGE = 8 * P
SLOTS = 4
MLA_HEADS = 16
QK = 96
NA_HEADS = 8
MLA_STEPS = MLA_HEADS + 8
NEG = -1e30
CLAMP = -44.0

C_DT = 0
C_GRP = C_DT + 1
C_SOUT = C_GRP + 3 * GROUPS
C_UP0 = C_SOUT + 8
C_DN0 = C_UP0 + 16
C_MIN = C_DN0 + 16
C_HEAD = C_MIN + 3
C_MOUT = C_HEAD + 8
C_UP1 = C_MOUT + 4
C_DN1 = C_UP1 + 16
C_IN2 = C_DN1 + 16
C_BR = C_IN2 + 20
C_WO = C_BR + 4
C_UP2 = C_WO + 4
C_DN2 = C_UP2 + 16
N_PAGES = 2 * (C_DN2 + 16)

K_DT = 0
K_GRP = 1
K_SOUT = K_GRP + 3 * GROUPS
K_UP0 = K_SOUT + 4
K_DN0 = K_UP0 + 16
K_MIN = K_DN0 + 8
K_HEAD = K_MIN + 3
K_MOUT = K_HEAD + 16
K_UP1 = K_MOUT + 4
K_DN1 = K_UP1 + 16
K_IN2 = K_DN1 + 8
K_BR = K_IN2 + 20
K_WO = K_BR + 8
K_UP2 = K_WO + 4
K_DN2 = K_UP2 + 16

N_IDENT, N_ONES, N_BLK = 0, 128, 256
N_SSD = 384
SSD_W = T + (T - 128) + (T - 256)
N_MLA = N_SSD + SSD_W
MLA_W = 144 + T
N_ROPE = N_MLA + MLA_W
N_NA = N_ROPE + T
N_CONST = N_NA + 64

V_GAIN = 0
V_CONV = V_GAIN + 6 * KD
V_DSKIP = V_CONV + GROUPS * 4 * 5
V_SNORM = V_DSKIP + 16
V_QA = V_SNORM + 16
V_KVA = V_QA + 3
V_QG = V_KVA + 2
V_KG = V_QG + 1
V_CONV2 = V_KG + 1
V_QN2 = V_CONV2 + 12
V_KN2 = V_QN2 + 1
V_DTB = V_KN2 + 1
V_ALOG = V_DTB + 1
N_VEC = V_ALOG + 1


class At:

    def __init__(self, base, step=0, turn=0):
        assert step % 2 == 0
        self.base, self.step, self.turn = base, step, turn

    def __add__(self, n):
        return At(self.base + n, self.step, self.turn)

    def times(self, n, plus=0):
        return At(self.base * n + plus, self.step * n, self.turn)

    @property
    def value(self):
        return self.turn * self.step + self.base if self.step else self.base

    @property
    def half(self):
        return self.turn * (self.step // 2) + self.base // 2 if self.step else self.base // 2

    @property
    def parity(self):
        return self.base % 2

    def page(self, j=0):
        return Page(self.base * 2 + j, self.step * 2, self.turn)


class Page(At):

    @property
    def slot(self):
        assert self.step % SLOTS == 0
        return self.base % SLOTS

    @property
    def round(self):
        n = self.base // SLOTS + 1
        return self.turn * (self.step // SLOTS) + n if self.step else n


def build(nc, w, h0, vec, const, rpb, out, acs_dram):
    ctx = ExitStack()
    with ctx:
        def sb(name, shape, dt=F32, where=ctx):
            return where.enter_context(nc.sbuf_tensor(name, shape, dt))

        def sem(name):
            return ctx.enter_context(nc.semaphore(name))

        w_raw = [sb(f"w_raw{i}", [P, PAGE]) for i in range(SLOTS)]
        w_hi = [sb(f"w_hi{i}", [P, PAGE], F32R) for i in range(SLOTS)]
        w_lo = [sb(f"w_lo{i}", [P, PAGE], F32R) for i in range(SLOTS)]
        h = sb("h", [P, KD, T])
        x_hi = sb("x_hi", [P, KD, T], F32R)
        x_lo = sb("x_lo", [P, KD, T], F32R)
        h_sq = sb("h_sq", [P, KD, T])
        r_ln = sb("r_ln", [P, T])
        r_inv = sb("r_inv", [P, T])
        vecs = sb("vecs", [P, N_VEC])
        cst = sb("cst", [P, N_CONST])
        bias_mask = sb("bias_mask", [P, NA_HEADS, 2, 256])
        eps_t = sb("eps_t", [P, 3])

        ssd = ExitStack()
        g_hi = sb("g_hi", [P, 16, T], F32R, ssd)
        g_lo = sb("g_lo", [P, 16, T], F32R, ssd)
        a_exp = sb("a_exp", [32, 1], F32, ssd)
        cols = sb("cols", [P, 6, 32], F32, ssd)
        acs_bc = sb("acs_bc", [P, HPG, T], F32, ssd)
        u = sb("u", [P, 4, T + 3], F32, ssd)
        cv = sb("cv", [P, 4, T], F32, ssd)
        sg = sb("sg", [P, 4, T], F32, ssd)
        z_raw = sb("z_raw", [P, 2, T], F32, ssd)
        z_sg = sb("z_sg", [P, 2, T], F32, ssd)
        xs_s = [sb(f"xs_s{i}", [P, 2, T], F32, ssd) for i in range(2)]
        bc_s = sb("bc_s", [P, 2, T], F32, ssd)
        z_s = [sb(f"z_s{i}", [P, 2, T], F32, ssd) for i in range(2)]
        x_tok = sb("x_tok", [P, 3, 256], F32, ssd)
        cbm = sb("cbm", [P, SSD_W], F32, ssd)
        dd = [sb(f"dd{i}", [P, HPG, SSD_W], F32, ssd) for i in range(2)]
        mm = sb("mm", [P, HPG, SSD_W], F32, ssd)
        y1 = sb("y1", [P, 2, T], F32, ssd)
        y2 = sb("y2", [P, 2, T], F32, ssd)
        dtx, dtb, dta, dt_t = [mm[0:32, i, 0:T] for i in range(4)]
        acs = y1[0:32, 0, :]
        y_sum = sb("y_sum", [P, T], F32, ssd)
        g_ln = sb("g_ln", [P, T], F32, ssd)
        g_inv = sb("g_inv", [P, T], F32, ssd)
        ssd.close()

        mlp_mem = ExitStack()
        hid_hi = sb("hid_hi", [P, FF_TILES, T], F32R, mlp_mem)
        hid_lo = sb("hid_lo", [P, FF_TILES, T], F32R, mlp_mem)
        relu = [sb(f"relu{i}", [P, 2, T], F32, mlp_mem) for i in range(2)]
        relu_sq = [sb(f"relu_sq{i}", [P, 2, T], F32, mlp_mem) for i in range(2)]
        down_r = [sb(f"down_r{i}", [P, T], F32, mlp_mem) for i in range(2)]
        mlp_mem.close()

        mla = ExitStack()
        lat = sb("lat", [P, 6, T], F32, mla)
        lat_sq = h_sq[:, 0:6, :]
        lat_n = lat[:, 0:5, :]
        l_hi = sb("l_hi", [P, 5, T], F32R, mla)
        l_lo = sb("l_lo", [P, 5, T], F32R, mla)
        l_ln = sb("l_ln", [P, 2, T], F32, mla)
        l_inv = sb("l_inv", [P, 2, T], F32, mla)
        rope_q = sb("rope_q", [P, T], F32, mla)
        rope_k = sb("rope_k", [P, T], F32, mla)
        rot_a = sb("rot_a", [P, 2, T], F32, mla)
        rot_b = sb("rot_b", [P, 2, T], F32, mla)
        q_pre = sb("q_pre", [QK, 4, T2], F32, mla)
        k_pre = sb("k_pre", [QK, 4, T], F32, mla)
        q_sq = sb("q_sq", [QK, 4, T2], F32, mla)
        k_sq = sb("k_sq", [QK, 4, T], F32, mla)
        v_t = sb("v_t", [P, 4, T], F32, mla)
        n_ln = sb("n_ln", [QK, 2, T], F32, mla)
        n_inv = sb("n_inv", [QK, 2, T], F32, mla)
        q_fin = [sb(f"q_fin{i}", [QK, 4, T2], F32, mla) for i in range(2)]
        k_fin = [sb(f"k_fin{i}", [QK, 4, T], F32, mla) for i in range(2)]
        v_tok = [sb(f"v_tok{i}", [P, 4, 3, HD], F32, mla) for i in range(2)]
        o_hi = sb("o_hi", [P, 8, T2], F32R, mla)
        o_lo = sb("o_lo", [P, 8, T2], F32R, mla)
        s_m = [sb(f"s_m{i}", [P, MLA_W], F32, mla) for i in range(2)]
        pr = [sb(f"pr{i}", [P, MLA_W], F32, mla) for i in range(2)]
        p_t = sb("p_t", [P, 384], F32, mla)
        p_t0 = sb("p_t0", [META, T2], F32, mla)
        mx = [sb(f"mx{i}", [P, 2], F32, mla) for i in range(2)]
        nmx = [sb(f"nmx{i}", [P, 2], F32, mla) for i in range(2)]
        rsum = [sb(f"rsum{i}", [P, 2], F32, mla) for i in range(2)]
        rinv = [sb(f"rinv{i}", [P, 2], F32, mla) for i in range(2)]
        mla.close()

        na = ExitStack()
        with ExitStack() as attention:
            qk_r = sb("qk_r", [P, 8, T2], F32, attention)
            qk_f = sb("qk_f", [P, 8, T2], F32, attention)
        m_hi = sb("m_hi", [P, 8, T2], F32R, na)
        m_lo = sb("m_lo", [P, 8, T2], F32R, na)
        qk_sq = [sb(f"qk_sq{i}", [P, 2, T2], F32, na) for i in range(2)]
        qk_ln = sb("qk_ln", [P, 2, T2], F32, na)
        qk_inv = [sb(f"qk_inv{i}", [P, 2, T2], F32, na) for i in range(2)]
        v_r = sb("v_r", [P, 4, T2], F32, na)
        v2 = sb("v2", [P, 2, 512], F32, na)
        cc_ch = h_sq[:, 0:2, 0:T2]
        zc = sb("zc", [P, 4, T2 + 2], F32, na)
        cv2 = sb("cv2", [P, 4, T2], F32, na)
        cb_r = sb("cb_r", [P, 4, T2], F32, na)
        yb = cv2
        yb_hi = sb("yb_hi", [P, 4, T2], F32R, na)
        yb_lo = sb("yb_lo", [P, 4, T2], F32R, na)
        ya_hi = sb("ya_hi", [P, 4, T2], F32R, na)
        ya_lo = sb("ya_lo", [P, 4, T2], F32R, na)
        gate = sb("gate", [P, 16, T2], F32, na)
        s_m2 = [sb(f"s_m2{i}", [P, 512], F32, na) for i in range(2)]
        pr2 = [sb(f"pr2{i}", [P, 512], F32, na) for i in range(2)]
        p_t2 = sb("p_t2", [P, 512], F32, na)
        mx2 = [sb(f"mx2{i}", [P, 2], F32, na) for i in range(2)]
        nmx2 = [sb(f"nmx2{i}", [P, 2], F32, na) for i in range(2)]
        rsum2 = [sb(f"rsum2{i}", [P, 2], F32, na) for i in range(2)]
        rinv2 = [sb(f"rinv2{i}", [P, 2], F32, na) for i in range(2)]
        m_a, m_b = h_sq[:, 2:4, 0:T2], h_sq[:, 4:6, 0:T2]
        na.close()

        lin = ctx.enter_context(nc.psum_tensor("lin", [P, 4, 512], F32))
        ps4, ps5, ps6, ps7 = [ctx.enter_context(nc.psum_tensor(f"ps{i}", [P, 512], F32)) for i in range(4, 8)]

        def linp(k, n, rows=slice(0, P)):
            return lin[rows, 2 * k.parity:2 * k.parity + 2, n]

        ident = cst[:, N_IDENT:N_IDENT + P]
        ones = cst[:, N_ONES:N_ONES + P]
        blk = cst[:, N_BLK:N_BLK + P]

        def v(col, n=1, rows=slice(0, P)):
            return vecs[rows, bass.ds(col, n)]

        def gain(norm, kt):
            return v(V_GAIN + norm * KD + kt)

        def over(ap, n):
            return ap.unsqueeze(1).broadcast_to([ap.shape[0], n, ap.shape[1]])

        w_arrived = [sem(f"w_arrived{i}") for i in range(SLOTS)]
        w_hi_done, w_used = sem("w_hi_done"), sem("w_used")
        w_lo_done = [sem(f"w_lo_done{i}") for i in range(SLOTS)]
        drained = [sem(f"drained{i}") for i in range(2)]
        vec_in, const_in, rpb_in, out_done = sem("vec_in"), sem("const_in"), sem("rpb_in"), sem("out_done")
        h_in = [sem(f"h_in{i}") for i in range(4)]
        xh_done, xl_done = sem("xh_done"), sem("xl_done")
        hsq_done, hsum_done, stat_done = sem("hsq_done"), sem("hsum_done"), sem("stat_done")
        rln_done, r_done = sem("rln_done"), sem("r_done")
        h_mlp = sem("h_mlp")
        memset_done, bias_done = sem("memset_done"), sem("bias_done")
        dt_dve, dt_act, dtT_done, cols_done = sem("dt_dve"), sem("dt_act"), sem("dtT_done"), sem("cols_done")
        acs_out = sem("acs_out")
        acs_in = sem("acs_in")
        cv0_done, cv_step, clamped, sg_step, silu_done = (sem("cv0_done"), sem("cv_step"), sem("clamped"),
                                                          sem("sg_step"), sem("silu_done"))
        z_clamped, zg_step, z_silu_done = sem("z_clamped"), sem("zg_step"), sem("z_silu_done")
        xT_done, xtok_done, cb_done, cbm_done = sem("xT_done"), sem("xtok_done"), sem("cb_done"), sem("cbm_done")
        dd_done, ee_done, mm_done, y_done, y_read = (sem("dd_done"), sem("ee_done"), sem("mm_done"),
                                                     sem("y_done"), sem("y_read"))
        y2_done, ysq_done, ysum_done, gstat_done = sem("y2_done"), sem("ysq_done"), sem("ysum_done"), sem("gstat_done")
        gln_done, ginv_done, y3_done, gh_done, gl_done = (sem("gln_done"), sem("ginv_done"), sem("y3_done"),
                                                          sem("gh_done"), sem("gl_done"))
        relu_done, rsq_done, hh_done, hl_done = sem("relu_done"), sem("rsq_done"), sem("hh_done"), sem("hl_done")
        latsq_done, lstat_done, l_act, latn_done = sem("latsq_done"), sem("lstat_done"), sem("l_act"), sem("latn_done")
        lh_done, ll_done, rope_done, krope = sem("lh_done"), sem("ll_done"), sem("rope_done"), sem("krope")
        raw_read, rot_done, rot_sum, nsum_done = sem("raw_read"), sem("rot_done"), sem("rot_sum"), sem("nsum_done")
        qsq_read, ksq_read, kpre_done = sem("qsq_read"), sem("ksq_read"), sem("kpre_done")
        nln_done, ninv_done, fin_done = sem("nln_done"), sem("ninv_done"), sem("fin_done")
        s_done, sm_done, nm_done, ex_done = sem("s_done"), sem("sm_done"), sem("nm_done"), sem("ex_done")
        ri_done, p_done, pT_done, pt_done, pt0_done = (sem("ri_done"), sem("p_done"), sem("pT_done"),
                                                       sem("pt_done"), sem("pt0_done"))
        pv_done, oh_done, ol_done = sem("pv_done"), sem("oh_done"), sem("ol_done")
        qksq_done, qkstat_done, qkln_done, qkinv_done, qkf_done = (sem("qksq_done"), sem("qkstat_done"),
                                                                   sem("qkln_done"), sem("qkinv_done"), sem("qkf_done"))
        vT_done, v2_done = sem("vT_done"), sem("v2_done")
        z_done, cv2_0, cv2_step, yb_done, ybh_done, ybl_done = (sem("z_done"), sem("cv2_0"), sem("cv2_step"),
                                                                sem("yb_done"), sem("ybh_done"), sem("ybl_done"))
        gclamp, gate_step = sem("gclamp"), sem("gate_step")
        s2_done, sm2_done, nm2_done, ex2_done = sem("s2_done"), sem("sm2_done"), sem("nm2_done"), sem("ex2_done")
        ri2_done, p2_done, pT2_done, pt2_done = sem("ri2_done"), sem("p2_done"), sem("pT2_done"), sem("pt2_done")
        pv2_done, yah_done, yal_done = sem("pv2_done"), sem("yah_done"), sem("yal_done")
        m_done, mh_done, ml_done = sem("m_done"), sem("mh_done"), sem("ml_done")

        block = ctx.enter_context(nc.Block())

        SLOT_TURNS = 3

        def h_ready(norm, kt):
            if norm == 0:
                return (h_in[kt.base // 2], 16)
            if norm in (2, 4):
                return (h_mlp, (kt + (8 * (norm // 2 - 1) + 1)).value)
            k = At({1: K_SOUT, 3: K_MOUT, 5: K_WO}[norm] + kt.base // 2)
            return (drained[k.parity], k.half + 1)

        def tokens(norm):
            return slice(0, T) if norm < 3 else slice(META, T)

        def width(norm):
            return T if norm < 3 else T2

        @block.sync
        def _(sp):
            sp.dma_start(vecs[:, :], vec).then_inc(vec_in, 16)
            for q in range(4):
                tiles = slice(2 * q, 2 * q + 2)
                sp.dma_start(h[:, tiles, :], h0[:, tiles, :]).then_inc(h_in[q], 16)
                if q == 0:
                    sp.dma_start(w_raw[0][:, :], w[0]).then_inc(w_arrived[0], 16)
            sp.dma_start(cst[:, :], const).then_inc(const_in, 16)
            for i in range(1, SLOTS):
                sp.dma_start(w_raw[i][:, :], w[i]).then_inc(w_arrived[i], 16)
            with sp.Fori(1, N_PAGES // SLOTS) as turn:
                for i in range(SLOTS):
                    sp.wait_ge(w_lo_done[i], turn)
                    sp.dma_start(w_raw[i][:, :], w[turn * SLOTS + i]).then_inc(w_arrived[i], 16)
            for kt in range(KD):
                sp.wait_ge(h_mlp, 16 + kt + 1)
                sp.dma_start(out[:, kt, :], h[:, kt, META:T]).then_inc(out_done, 16)
            sp.wait_ge(out_done, 16 * KD)

        @block.tensor
        def _(pe):
            mm3 = nc.tensor.matmul

            def free(k):
                if k.base >= 2:
                    pe.wait_ge(drained[k.parity], k.half)

            def tile(o, pg, hi, lo, n, kts=KD, kt0=0, at=0, t0=0, first=True, last=True, before=None):
                pe.wait_ge(w_lo_done[pg.slot], pg.round)
                for i in range(kts):
                    if before:
                        before(i)
                    wh = w_hi[pg.slot][:, (at + i) * P:(at + i + 1) * P]
                    wl = w_lo[pg.slot][:, (at + i) * P:(at + i + 1) * P]
                    xh, xl = hi[:, kt0 + i, t0:t0 + n], lo[:, kt0 + i, t0:t0 + n]
                    mm3(o, wh, xh, start=first and i == 0, stop=False)
                    mm3(o, wh, xl, start=False, stop=False)
                    ins = mm3(o, wl, xh, start=False, stop=last and i == kts - 1)
                return ins

            def lin_chunk(c, k, n, norm=None, hi=x_hi, lo=x_lo, before=None):
                free(k)
                if norm is not None:
                    before = lambda i: pe.wait_ge(xl_done, KD * norm + i + 1)
                if before is None:
                    for j in range(2):
                        tile(lin[:, 2 * k.parity + j, 0:n], c.page(j), hi, lo, n).then_inc(w_used, 1)
                    return
                for kt0, kts in ((0, KD - 2), (KD - 2, 2)):
                    for j in range(2):
                        late = (lambda i: before(kt0 + i)) if j == 0 else None
                        ins = tile(lin[:, 2 * k.parity + j, 0:n], c.page(j), hi, lo, n, kts=kts, kt0=kt0, at=kt0,
                                   first=kt0 == 0, last=kt0 > 0, before=late)
                        if kt0:
                            ins.then_inc(w_used, 1)

            def norm_stat(norm):
                n = width(norm)
                pe.wait_ge(hsum_done, (KD - 1) * (norm + 1))
                nc.tensor.matmul(ps7[:, 0:n], ones, h_sq[:, 0, 0:n], start=True, stop=True).then_inc(stat_done, 1)

            tile(lin[:, 0, 0:T], At(C_DT).page(0), x_hi, x_lo, T,
                 before=lambda i: pe.wait_ge(xl_done, i + 1)).then_inc(w_used, 1)
            pe.wait_ge(w_lo_done[1], 1)
            pe.sem_inc(w_used, 1)

            def dt_transposes():
                pe.wait_ge(dt_dve, 6)
                for i, src in enumerate((dt_t, acs)):
                    for s in range(3):
                        n = min(P, T - s * P)
                        ins = nc.tensor.transpose(ps4[0:n, (3 * i + s) * 32:(3 * i + s + 1) * 32],
                                                  src[:, s * P:s * P + n], ident[0:32, 0:32])
                ins.then_inc(dtT_done, 1)

            def x_transposes(g):
                pe.wait_ge(silu_done, g.times(2, 1).value)
                if g.base >= 1:
                    pe.wait_ge(y_read, g.times(2, -1).value)
                else:
                    pe.wait_ge(cols_done, 4)
                for q in range(2):
                    nc.tensor.transpose(ps4[:, q * P:(q + 1) * P], xs_s[g.parity][:, q, 0:128], ident)
                    nc.tensor.transpose(ps6[:, q * P:(q + 1) * P], xs_s[g.parity][:, q, 128:256], ident)
                    ins = nc.tensor.transpose(ps4[0:META, 256 + q * P:256 + (q + 1) * P],
                                              xs_s[g.parity][:, q, 256:T], ident)
                ins.then_inc(xT_done, 1)

            def cb_products(g):
                pe.wait_ge(silu_done, g.times(2, 2).value)
                if g.base >= 2:
                    pe.wait_ge(gln_done, (g + (-1)).value)
                b, cc = bc_s[:, 0, :], bc_s[:, 1, :]
                nc.tensor.matmul(ps5[:, 0:T], b[:, 0:128], cc, start=True, stop=True)
                nc.tensor.matmul(ps5[:, T:T + 144], b[:, 128:256], cc[:, 128:T], start=True, stop=True)
                nc.tensor.matmul(ps5[0:META, 416:432], b[:, 256:T], cc[:, 256:T],
                                 start=True, stop=True).then_inc(cb_done, 1)

            def group_stat(g):
                pe.wait_ge(ysum_done, (g + 1).value)
                pe.wait_ge(cbm_done, (g + 2).value) if g.base < 7 else None
                nc.tensor.matmul(ps5[:, 0:T], ones, y_sum[:, :], start=True, stop=True).then_inc(gstat_done, 1)

            def y_products(g):
                pe.wait_ge(xtok_done, (g + 1).value)
                for q in range(2):
                    o = (ps6, ps7)[q]
                    if q == 1 and g.base >= 1:
                        pe.wait_ge(y_read, g.times(2).value)
                    if q == 1 and g.base == 0:
                        pe.wait_ge(rln_done, 1)
                    for e in range(2):
                        j = 2 * q + e
                        pe.wait_ge(mm_done, g.times(4, j + 1).value)
                        rows = slice(e * HD, (e + 1) * HD)
                        cs = slice(j * HD, (j + 1) * HD)
                        nc.tensor.matmul(o[rows, 0:T], x_tok[:, 0, cs], mm[:, j, 0:T], start=True, stop=False)
                        nc.tensor.matmul(o[rows, 128:T], x_tok[:, 1, cs], mm[:, j, T:416], start=False, stop=False)
                        ins = nc.tensor.matmul(o[rows, 256:T], x_tok[0:META, 2, cs], mm[0:META, j, 416:432],
                                               start=False, stop=True)
                    ins.then_inc(y_done, 1)

            def slot(s, has_lin=True, has_scan=True, has_stat=True, first=False):
                c, k = s.times(3, C_GRP), s.times(3, K_GRP)
                if first:
                    tile(lin[:, 2 * k.parity, 0:T], c.page(0), x_hi, x_lo, T).then_inc(w_used, 1)
                    pe.wait_ge(const_in, 16)
                    norm_stat(0)
                    tile(lin[:, 2 * k.parity + 1, 0:T], c.page(1), x_hi, x_lo, T).then_inc(w_used, 1)
                elif has_lin:
                    lin_chunk(c, k, T)
                if has_scan:
                    x_transposes(s + (-1))
                    cb_products(s + (-1))
                if has_lin:
                    lin_chunk(c + 1, k + 1, T)
                if first:
                    dt_transposes()
                if has_stat:
                    group_stat(s + (-2))
                if has_lin:
                    lin_chunk(c + 2, k + 2, T)
                if has_scan:
                    y_products(s + (-1))

            slot(At(0), has_scan=False, has_stat=False, first=True)
            slot(At(1), has_stat=False)
            with pe.Fori(0, SLOT_TURNS) as turn:
                for i in range(2):
                    slot(At(2 + i, 2, turn))
            def sout(r, j, half, kt=0, kts=8):
                k = At(K_SOUT + 2 * r + j // 2)
                if j % 2 == 0 and half == 0:
                    free(k)
                end = kt + kts == 8
                ins = tile(lin[:, 2 * k.parity + j % 2, 0:T], At(C_SOUT + 4 * r).page(4 * half + j), g_hi, g_lo, T,
                           kts=kts, kt0=8 * half + kt, at=kt, first=half == 0, last=half == 1 and end)
                if end:
                    ins.then_inc(w_used, 1)

            pe.wait_ge(gl_done, 8)
            sout(0, 0, 0)
            sout(0, 1, 0)
            x_transposes(At(7))
            cb_products(At(7))
            sout(0, 2, 0)
            group_stat(At(6))
            y_products(At(7))
            sout(0, 3, 0)
            pe.wait_ge(gl_done, 14)
            for j in range(3):
                sout(0, j, 1, 0, 6)
            group_stat(At(7))
            sout(0, 3, 1, 0, 6)
            pe.wait_ge(gl_done, 16)
            for j in range(4):
                sout(0, j, 1, 6, 2)
            for half in range(2):
                for j in range(4):
                    sout(1, j, half)

            def mlp(m, norm, c_up, k_up, c_dn, k_dn):
                n = width(norm)
                lin_chunk(At(c_up), At(k_up), n, norm)
                lin_chunk(At(c_up + 1), At(k_up + 1), n)
                norm_stat(norm)
                with pe.Fori(1, 8) as turn:
                    for i in range(2):
                        lin_chunk(At(c_up + i, 2, turn), At(k_up + i, 2, turn), n)
                with pe.Fori(0, 4) as turn:
                    for i in range(2):
                        k = At(k_dn + i, 2, turn)
                        free(k)
                        for q in range(4):
                            pe.wait_ge(hl_done, 16 * m + 4 * (q + 1))
                            tile(lin[:, 2 * k.parity, 0:n], At(c_dn + 2 * i, 4, turn).page(q), hid_hi, hid_lo, n,
                                 kt0=8 * q, first=q == 0, last=q == 3).then_inc(w_used, 1)

            mlp(0, 1, C_UP0, K_UP0, C_DN0, K_DN0)

            lin_chunk(At(C_MIN), At(K_MIN), T, 2)
            norm_stat(2)
            lin_chunk(At(C_MIN + 1), At(K_MIN + 1), T)
            k = At(K_MIN + 2)
            free(k)
            tile(lin[:, 2 * k.parity, 0:T], At(C_MIN + 2).page(0), x_hi, x_lo, T).then_inc(w_used, 1)
            pe.wait_ge(latsq_done, 2)
            for i in range(3):
                ins = nc.tensor.matmul(ps4[:, 0:T], ones, lat_sq[:, i, :], start=i == 0, stop=i == 2)
            ins.then_inc(lstat_done, 1)
            tile(lin[:, 2 * k.parity + 1, 0:T], At(C_MIN + 2).page(1), x_hi, x_lo, T).then_inc(w_used, 1)

            def kv_stat():
                pe.wait_ge(latsq_done, 3)
                for i in range(2):
                    ins = nc.tensor.matmul(ps5[:, 0:T], ones, lat_sq[:, 3 + i, :], start=i == 0, stop=i == 1)
                ins.then_inc(lstat_done, 1)

            def unit(un):
                s, n = un // 4, un % 4
                k = At(K_HEAD + un)
                kts, kt0, t0 = (3, 0, META) if n < 2 else (2, 3, 0)
                if un < 4:
                    pe.wait_ge(ll_done, 3 if n < 2 else 5)
                free(k)
                for j in range(2):
                    ins = tile(lin[:, 2 * k.parity + j, 0:T - t0], At(C_HEAD + 2 * s).page(n), l_hi, l_lo, T - t0,
                               kts=kts, kt0=kt0, at=j * kts, t0=t0)
                ins.then_inc(w_used, 1)

            def unit_norm(un):
                s, n = un // 4, un % 4
                k = At(K_HEAD + un)
                pe.wait_ge(raw_read, 4 * s + n + 1)
                if n < 2:
                    pe.wait_ge(rot_done, 2 * (2 * s + n) + 1)
                else:
                    pe.wait_ge(kpre_done, 2 * s + n - 1)
                    if s == 0:
                        pe.wait_ge(krope, 4)
                for j in range(2):
                    head = 2 * (n % 2) + j
                    bank = lin[:, 2 * k.parity + j, :]
                    if n < 2:
                        ins = nc.tensor.matmul(bank[:, 0:T2], ones[0:QK, :], q_sq[:, head, :], start=True, stop=True)
                    else:
                        nc.tensor.matmul(bank[:, 0:T], ones[0:QK, :], k_sq[:, head, :], start=True, stop=True)
                        idv = ident[HD:P, HD:P]
                        nc.tensor.transpose(bank[:, 272:336], v_t[HD:P, head, META:144], idv)
                        nc.tensor.transpose(bank[:, 336:400], v_t[HD:P, head, 144:T], idv)
                        ins = nc.tensor.transpose(bank[0:META, 400:464], v_t[HD:P, head, 0:META], idv)
                ins.then_inc(nsum_done, 1)

            def scores(n):
                s, j = n // 4, n % 4
                p = s % 2
                if j == 0:
                    pe.wait_ge(fin_done, 4 * s + 4)
                if n >= 2:
                    pe.wait_ge(sm_done, n - 1)
                elif n == 0:
                    pe.wait_ge(l_act, 3)
                o = (ps5, ps6)[n % 2]
                nc.tensor.matmul(o[:, 0:144], q_fin[p][:, j, 0:128], k_fin[p][:, j, 0:144], start=True, stop=True)
                nc.tensor.matmul(o[:, 144:416], q_fin[p][:, j, 128:256], k_fin[p][:, j, :],
                                 start=True, stop=True).then_inc(s_done, 1)

            def p_transposes(n):
                pe.wait_ge(p_done, n + 1)
                if n >= 1:
                    pe.wait_ge(pt_done, n)
                else:
                    pe.wait_ge(rln_done, 3)
                if n % 2 == 0 and n >= 2:
                    pe.wait_ge(ol_done, n // 2)
                prn = pr[n % 2]
                nc.tensor.transpose(ps4[0:META, 256:384], prn[:, 0:16], ident)
                nc.tensor.transpose(ps4[0:META, 384:512], prn[:, 144:160], ident)
                nc.tensor.transpose(ps7[:, 0:128], prn[:, 16:144], ident)
                nc.tensor.transpose(ps7[:, 128:256], prn[:, 160:288], ident)
                nc.tensor.transpose(ps7[:, 256:384], prn[:, 288:416], ident).then_inc(pT_done, 1)

            def values(n):
                j, p = n % 4, n // 4 % 2
                pe.wait_ge(pt_done, n + 1)
                pe.wait_ge(pt0_done, n + 1)
                o = ps4[(n % 2) * HD:(n % 2 + 1) * HD, 0:T2]
                nc.tensor.matmul(o, v_tok[p][0:META, j, 0, :], p_t0[:, :], start=True, stop=False)
                nc.tensor.matmul(o, v_tok[p][:, j, 1, :], p_t[:, 0:256], start=False, stop=False)
                nc.tensor.matmul(o[:, 128:256], v_tok[p][:, j, 2, :], p_t[:, 256:384],
                                 start=False, stop=True).then_inc(pv_done, 1)

            def mout_part(j, kts, kt0):
                k = At(K_MOUT + j // 2)
                if j % 2 == 0 and kt0 == 0:
                    free(k)
                pe.wait_ge(ol_done, kt0 + kts)
                ins = tile(lin[:, 2 * k.parity + j % 2, 0:T2], At(C_MOUT).page(j), o_hi, o_lo, T2, kts=kts, kt0=kt0,
                           at=kt0, first=kt0 == 0, last=kt0 + kts == KD)
                if kt0 + kts == KD:
                    ins.then_inc(w_used, 1)

            for t in range(MLA_STEPS):
                if t < 16:
                    unit(t)
                if t == 0:
                    kv_stat()
                if 19 <= t < 23:
                    mout_part(t - 19, 5, 0)
                if 0 <= t - 5 < 16 and t < 16:
                    scores(t - 5)
                if t >= 8:
                    p_transposes(t - 8)
                if 0 <= t - 5 < 16 and t >= 16:
                    scores(t - 5)
                if t < 16:
                    unit_norm(t)
                if t == 23:
                    mout_part(0, 2, 5)
                    mout_part(1, 2, 5)
                if t >= 8:
                    values(t - 8)
            mout_part(2, 2, 5)
            mout_part(3, 2, 5)
            for j in range(4):
                mout_part(j, 1, 7)
            for i in (2, 3):
                lin_chunk(At(C_MOUT + i), At(K_MOUT + i), T2, hi=o_hi, lo=o_lo)

            mlp(1, 3, C_UP1, K_UP1, C_DN1, K_DN1)

            def qk_stat(i):
                pe.wait_ge(qksq_done, i + 1)
                if i >= 2:
                    pe.wait_ge(qkln_done, i - 1)
                nc.tensor.matmul((ps5, ps6)[i % 2][:, :], blk, qk_sq[i % 2][:, :, :].rearrange("p a t -> p (a t)"),
                                 start=True, stop=True).then_inc(qkstat_done, 1)

            def v_transposes():
                for i in (4, 5):
                    k = At(K_IN2 + i)
                    pe.wait_ge(drained[k.parity], k.half + 1)
                pe.wait_ge(rln_done, 5)
                for tt, o in ((0, ps7), (1, ps4)):
                    for j in range(4):
                        ins = nc.tensor.transpose(o[:, j * P:(j + 1) * P], v_r[:, j, tt * P:(tt + 1) * P], ident)
                ins.then_inc(vT_done, 1)

            def scores2(n):
                if n == 0:
                    pe.wait_ge(qkln_done, 3)
                    pe.wait_ge(qkf_done, 4)
                elif n == 1:
                    pe.wait_ge(qkln_done, 4)
                else:
                    pe.wait_ge(sm2_done, n - 1)
                rows, j = slice((n % 2) * HD, (n % 2 + 1) * HD), n // 2
                for qt in range(2):
                    ins = nc.tensor.matmul((ps5, ps6)[n % 2][:, qt * 256:(qt + 1) * 256],
                                           qk_f[rows, j, qt * P:(qt + 1) * P], qk_f[rows, 4 + j, :],
                                           start=True, stop=True)
                ins.then_inc(s2_done, 1)

            def p_transposes2(n):
                pe.wait_ge(p2_done, n + 1)
                if n == 0:
                    pe.wait_ge(v2_done, 2)
                else:
                    pe.wait_ge(pt2_done, n)
                for kt in range(2):
                    for qt in range(2):
                        ins = nc.tensor.transpose(ps7[:, kt * 256 + qt * P:kt * 256 + (qt + 1) * P],
                                                  pr2[n % 2][:, qt * 256 + kt * P:qt * 256 + (kt + 1) * P], ident)
                ins.then_inc(pT2_done, 1)

            def values2(n):
                if n % 2 == 0 and n >= 2:
                    pe.wait_ge(yal_done, n // 2)
                pe.wait_ge(pt2_done, n + 1)
                o = ps4[(n % 2) * HD:(n % 2 + 1) * HD, 0:T2]
                for kt in range(2):
                    ins = nc.tensor.matmul(o, v2[:, kt, n * HD:(n + 1) * HD], p_t2[:, kt * 256:(kt + 1) * 256],
                                           start=kt == 0, stop=kt == 1)
                ins.then_inc(pv2_done, 1)

            for i in range(20):
                if 8 <= i < 16:
                    p_transposes2(i - 8)
                lin_chunk(At(C_IN2 + i), At(K_IN2 + i), T2, 4 if i == 0 else None)
                if i == 0:
                    norm_stat(4)
                if 1 <= i <= 4:
                    qk_stat(i - 1)
                if i == 6:
                    v_transposes()
                if 8 <= i < 16:
                    values2(i - 8)
                if 6 <= i < 14:
                    scores2(i - 6)

            pe.wait_ge(yal_done, 4)
            pe.wait_ge(ybl_done, 2)
            for b in range(4):
                for n, (hi, lo) in enumerate(((ya_hi, ya_lo), (yb_hi, yb_lo))):
                    k = At(K_BR + 2 * b + n)
                    free(k)
                    for j in range(2):
                        ins = tile(lin[:, 2 * k.parity + j, 0:T2], At(C_BR + b).page(n), hi, lo, T2, kts=4, at=4 * j)
                    ins.then_inc(w_used, 1)

            for i in range(4):
                lin_chunk(At(C_WO + i), At(K_WO + i), T2, hi=m_hi, lo=m_lo,
                          before=(lambda kt: pe.wait_ge(ml_done, kt // 2 + 1)) if i == 0 else None)

            mlp(2, 5, C_UP2, K_UP2, C_DN2, K_DN2)

        @block.scalar
        def _(act):
            a = nc.scalar.activation

            def hi(pg, n=PAGE):
                act.wait_ge(w_arrived[pg.slot], pg.round * 16)
                if pg.base >= SLOTS:
                    act.wait_ge(w_used, (pg + (1 - SLOTS)).value)
                a(w_hi[pg.slot][:, 0:n], w_raw[pg.slot][:, 0:n], ACT.Copy).then_inc(w_hi_done, 1)

            def hi2(c):
                hi(c.page(0))
                hi(c.page(1))

            def round_h(norm, kt):
                act.wait_ge(*h_ready(norm, kt))
                a(x_hi[:, kt.value, 0:width(norm)], h[:, kt.value, tokens(norm)], ACT.Copy,
                  scale=gain(norm, kt.value)).then_inc(xh_done, 1)

            def square_h(norm, kt):
                a(h_sq[:, kt.value, 0:width(norm)], h[:, kt.value, tokens(norm)], ACT.Square).then_inc(hsq_done, 1)

            def norm_hi(norm, kt):
                round_h(norm, kt)
                square_h(norm, kt)

            def norm_inv(norm, squared=False):
                n = width(norm)
                act.wait_ge(stat_done, norm + 1)
                a(r_ln[:, 0:n], ps7[:, 0:n], ACT.Ln, bias=eps_t[:, 0:1], scale=1.0 / D).then_inc(rln_done, 1)
                act.wait_ge(rln_done, norm + 1)
                a(r_inv[:, 0:n], r_ln[:, 0:n], ACT.Exp, scale=-1.0 if squared else -0.5).then_inc(r_done, 1)

            act.preload_act_table_set("natural_log_exp_and_others")
            act.wait_ge(vec_in, 16)
            act.wait_ge(memset_done, 4)
            for kt in range(KD):
                round_h(0, At(kt))
                if kt == 1:
                    hi(Page(0))
            for kt in range(KD):
                square_h(0, At(kt))
                if kt in (1, 3, 5):
                    hi(Page(kt // 2 + 1))
            a(a_exp[:, :], v(V_ALOG, rows=slice(0, 32)), ACT.Exp).then_inc(dt_act, 1)
            norm_inv(0)
            hi2(At(2))
            act.wait_ge(dt_dve, 3)
            a(dta[:, :], dta[:, :], ACT.Exp, scale=-1.0).then_inc(dt_act, 1)
            act.wait_ge(dt_act, 2)
            a(dta[:, :], dta[:, :], ACT.Ln, bias=1.0).then_inc(dt_act, 1)

            def sigmoid(buf, step_sem, n):
                a(buf, buf, ACT.Exp, scale=-1.0).then_inc(step_sem, 1)
                act.wait_ge(step_sem, (n + 1).value)
                a(buf, buf, ACT.Ln, bias=1.0).then_inc(step_sem, 1)
                act.wait_ge(step_sem, (n + 2).value)
                a(buf, buf, ACT.Exp, scale=-1.0).then_inc(step_sem, 1)

            def conv0(s, pair):
                k = s.times(3, K_GRP + pair)
                act.wait_ge(drained[k.parity], (k.half + 1))
                for q in (2 * pair, 2 * pair + 1):
                    at = s.times(20, V_CONV + 5 * q)
                    a(cv[:, q, :], u[:, q, 0:T], ACT.Identity, scale=v(at.value), bias=v((at + 4).value))\
                        .then_inc(cv0_done, 1)

            def decay(g, j):
                h_at = g.times(4, j)
                d = dd[g.parity]
                act.wait_ge(dd_done, g.times(2, j // 2 + 1).value)
                for s, (rows, at, n) in enumerate(((P, 0, T), (P, T, 144), (META, 416, 16))):
                    ins = a(d[0:rows, j, at:at + n], d[0:rows, j, at:at + n], ACT.Exp,
                            bias=cols[0:rows, 3 + s, bass.ds(h_at.value, 1)])
                ins.then_inc(ee_done, 1)

            def slot(s, has_lin=True, has_scan=True, has_stat=True):
                c = s.times(3, C_GRP)
                g, gs = s + (-1), s + (-2)
                if has_scan and g.base == 0:
                    act.wait_ge(cols_done, 4)
                if has_lin:
                    hi((c + 2).page(0))
                if has_scan:
                    decay(g, 0)
                if has_lin:
                    hi((c + 2).page(1))
                if has_scan:
                    act.wait_ge(cb_done, (g + 1).value)
                    if g.base:
                        act.wait_ge(mm_done, g.times(4).value)
                    a(cbm[:, 0:416], ps5[:, 0:416], ACT.Copy)
                    a(cbm[0:META, 416:432], ps5[0:META, 416:432], ACT.Copy).then_inc(cbm_done, 1)
                    act.wait_ge(xT_done, (g + 1).value)
                    a(x_tok[:, 0, :], ps4[:, 0:256], ACT.Copy)
                    a(x_tok[0:META, 2, :], ps4[0:META, 256:512], ACT.Copy)
                    a(x_tok[:, 1, :], ps6[:, 0:256], ACT.Copy).then_inc(xtok_done, 1)
                if has_stat:
                    act.wait_ge(y2_done, (gs + 1).value)
                    a(h_sq[:, 0:2, :], y2[:, :, :], ACT.Square).then_inc(ysq_done, 1)
                if has_lin:
                    conv0(s, 0)
                if has_scan:
                    decay(g, 1)
                    decay(g, 2)
                    decay(g, 3)
                if has_lin:
                    hi((c + 3).page(0))
                    act.wait_ge(clamped, s.times(2, 1).value)
                    sigmoid(sg[:, 0:2, :], sg_step, s.times(6))
                if has_scan:
                    act.wait_ge(z_clamped, (g + 1).value)
                    sigmoid(z_sg[:, :, :], zg_step, g.times(3))
                if has_lin:
                    conv0(s, 1)
                    hi((c + 3).page(1))
                if not has_lin:
                    hi2(s + (C_SOUT - 6))
                if has_stat:
                    act.wait_ge(gstat_done, (gs + 1).value)
                    a(g_ln[:, :], ps5[:, 0:T], ACT.Ln, bias=eps_t[:, 0:1], scale=1.0 / 256).then_inc(gln_done, 1)
                    act.wait_ge(gln_done, (gs + 1).value)
                    a(g_inv[:, :], g_ln[:, :], ACT.Exp, scale=-0.5).then_inc(ginv_done, 1)
                if has_lin:
                    hi((c + 4).page(0))
                if has_stat:
                    act.wait_ge(y3_done, (gs + 1).value)
                    for q in range(2):
                        t = gs.times(2, q)
                        a(g_hi[:, t.value, :], z_s[gs.parity][:, q, :], ACT.Copy, scale=v((t + V_SNORM).value))\
                            .then_inc(gh_done, 1)
                if has_lin:
                    act.wait_ge(clamped, s.times(2, 2).value)
                    sigmoid(sg[:, 2:4, :], sg_step, s.times(6, 3))
                    hi((c + 4).page(1))

            slot(At(0), has_scan=False, has_stat=False)
            slot(At(1), has_stat=False)
            with act.Fori(0, SLOT_TURNS) as turn:
                for i in range(2):
                    slot(At(2 + i, 2, turn))
            slot(At(8), has_lin=False)
            slot(At(9), has_lin=False, has_scan=False)

            for i in range(2, 8):
                hi2(At(C_SOUT + 2 + i))
                if i % 4 >= 2:
                    j = i // 4 * 2 + i % 2
                    for kt in (2 * j, 2 * j + 1):
                        norm_hi(1, At(kt))

            def mlp(m, norm, c_up, k_up, c_dn, last):
                n = width(norm)

                def up(i, t):
                    k = t + k_up
                    hi((t + (c_up + 2)).page(0))
                    act.wait_ge(w_used, (t + (c_up + 1)).page().value)
                    a(relu[i][:, :, 0:n], linp(k, slice(0, n)), ACT.Relu).then_inc(drained[k.parity], 1)
                    hi((t + (c_up + 2)).page(1))
                    act.wait_ge(drained[k.parity], k.half + 1)
                    at = t.times(2)
                    a(hid_hi[:, bass.ds(at.value, 2), 0:n], relu[i][:, :, 0:n], ACT.Square).then_inc(hh_done, 1)

                for i in range(2):
                    up(i, At(i))
                norm_inv(norm, squared=True)
                with act.Fori(1, 8) as turn:
                    for i in range(2):
                        t = At(i, 2, turn)
                        act.wait_ge(hl_done, (t + (16 * m - 1)).value)
                        up(i, t)

                def down(t, next_hi=True):
                    if next_hi:
                        hi2(t.times(2, c_dn + 2))
                        hi2(t.times(2, c_dn + 3))
                    if not last:
                        norm_hi(norm + 1, t)

                with act.Fori(0, 3) as turn:
                    for i in range(2):
                        down(At(i, 2, turn))
                down(At(6))
                down(At(7), not last)

            mlp(0, 1, C_UP0, K_UP0, C_DN0, False)

            hi2(At(C_MIN + 2))
            hi(At(C_HEAD).page(0), 6 * P)
            hi(At(C_HEAD).page(1), 6 * P)
            norm_inv(2)
            def lat_square(i):
                k = At(K_MIN + i)
                act.wait_ge(drained[k.parity], k.half + 1)
                a(lat_sq[:, 2 * i:2 * i + 2, :], lat[:, 2 * i:2 * i + 2, :], ACT.Square).then_inc(latsq_done, 1)

            lat_square(0)
            lat_square(1)
            hi(At(C_HEAD).page(2), 4 * P)
            for i, (ps, n, tiles) in enumerate(((ps4, 384, range(3)), (ps5, 256, range(3, 5)))):
                if i == 1:
                    lat_square(2)
                act.wait_ge(lstat_done, i + 1)
                a(l_ln[:, i, :], ps[:, 0:T], ACT.Ln, bias=eps_t[:, 0:1], scale=1.0 / n).then_inc(l_act, 1)
                act.wait_ge(l_act, 2 * i + 1)
                a(l_inv[:, i, :], l_ln[:, i, :], ACT.Exp, scale=-0.5).then_inc(l_act, 1)
                act.wait_ge(latn_done, i + 1)
                for q in tiles:
                    a(l_hi[:, q, :], lat_n[:, q, :], ACT.Copy, scale=v(V_QA + q)).then_inc(lh_done, 1)
                if i == 0:
                    hi(At(C_HEAD).page(3), 4 * P)

            def unit_raw(un):
                k, n = At(K_HEAD + un), un % 4
                act.wait_ge(w_used, 2 * C_HEAD + un + 1)
                hs = slice(2 * (n % 2), 2 * (n % 2) + 2)
                if n < 2:
                    a(q_sq[:, hs, :], linp(k, slice(0, T2), slice(0, QK)), ACT.Square).then_inc(qsq_read, 1)
                    a(q_pre[0:HD, hs, :], linp(k, slice(0, T2), slice(0, HD)), ACT.Copy,
                      scale=v(V_QG, rows=slice(0, HD))).then_inc(raw_read, 1)
                else:
                    a(k_sq[0:HD, hs, :], linp(k, slice(0, T), slice(0, HD)), ACT.Square).then_inc(ksq_read, 1)
                    a(v_t[HD:P, hs, :], linp(k, slice(0, T), slice(HD, P)), ACT.Copy).then_inc(raw_read, 1)

            def unit_inv(un):
                s, n = un // 4, un % 4
                k = At(K_HEAD + un)
                w_ = T2 if n < 2 else T
                if un >= 1:
                    act.wait_ge(ninv_done, un)
                act.wait_ge(nsum_done, un + 1)
                if n < 2:
                    a(n_ln[:, :, 0:w_], linp(k, slice(0, w_), slice(0, QK)), ACT.Ln, bias=eps_t[0:QK, 0:1],
                      scale=1.0 / QK).then_inc(drained[k.parity], 1)
                else:
                    hs = slice(2 * (n % 2), 2 * (n % 2) + 2)
                    a(n_ln[:, :, 0:w_], linp(k, slice(0, w_), slice(0, QK)), ACT.Ln, bias=eps_t[0:QK, 0:1],
                      scale=1.0 / QK)
                    if s >= 2:
                        act.wait_ge(pv_done, 4 * (s - 2) + 2 * (n - 1))
                    a(v_tok[s % 2][:, hs, 1:3, :], linp(k, slice(272, 400)).rearrange("p h (t d) -> p h t d", d=HD),
                      ACT.Copy)
                    a(v_tok[s % 2][0:META, hs, 0, :], linp(k, slice(400, 464), slice(0, META)), ACT.Copy)\
                        .then_inc(drained[k.parity], 1)
                act.wait_ge(drained[k.parity], k.half + 1)
                if un >= 1:
                    act.wait_ge(fin_done, un)
                if n < 2:
                    a(n_inv[:, :, 0:w_], n_ln[:, :, 0:w_], ACT.Exp, scale=-0.5, bias=eps_t[0:QK, 1:2])\
                        .then_inc(ninv_done, 1)
                else:
                    a(n_inv[:, :, 0:w_], n_ln[:, :, 0:w_], ACT.Exp, scale=-0.5).then_inc(ninv_done, 1)

            def exps(n):
                p = n % 2
                act.wait_ge(nm_done, n + 1)
                a(pr[p][:, 0:144], s_m[p][:, 0:144], ACT.Exp, bias=nmx[p][:, 0:1], accum_out=rsum[p][:, 0:1])
                a(pr[p][:, 144:416], s_m[p][:, 144:416], ACT.Exp, bias=nmx[p][:, 1:2], accum_out=rsum[p][:, 1:2])\
                    .then_inc(ex_done, 1)

            def p_t0_copy(n):
                act.wait_ge(pT_done, n + 1)
                a(p_t0[:, :], ps4[0:META, 256:512], ACT.Copy).then_inc(pt0_done, 1)

            def o_high(n):
                act.wait_ge(pv_done, 2 * n + 2)
                a(o_hi[:, n, :], ps4[:, 0:T2], ACT.Copy).then_inc(oh_done, 1)

            for t in range(MLA_STEPS + 1):
                if 1 <= t <= 16:
                    unit_inv(t - 1)
                if t >= 10 and t % 2 == 0:
                    o_high((t - 10) // 2)
                if 1 <= t <= 16:
                    nxt = t + 3
                    hi(At(C_HEAD).page(nxt), PAGE if nxt >= 16 else (6 if nxt % 4 < 2 else 4) * P)
                if t < 16:
                    unit_raw(t)
                if 8 <= t < MLA_STEPS:
                    p_t0_copy(t - 8)
                if 0 <= t - 6 < 16:
                    exps(t - 6)
            for i in range(4):
                hi2(At(C_MOUT + 2 + i))
                for kt in ((), range(4), (4, 5), (6, 7))[i]:
                    norm_hi(3, At(kt))
            mlp(1, 3, C_UP1, K_UP1, C_DN1, False)

            def exps2(n):
                p = n % 2
                act.wait_ge(nm2_done, n + 1)
                for qt in range(2):
                    ins = a(pr2[p][:, qt * 256:(qt + 1) * 256], s_m2[p][:, qt * 256:(qt + 1) * 256], ACT.Exp,
                            bias=nmx2[p][:, qt:qt + 1], accum_out=rsum2[p][:, qt:qt + 1])
                ins.then_inc(ex2_done, 1)

            def gate_sigmoid(j):
                act.wait_ge(gclamp, j + 1)
                sigmoid(gate[:, 2 * j:2 * j + 2, :], gate_step, At(3 * j))

            def ya_high(q):
                act.wait_ge(pv2_done, 2 * q + 2)
                a(ya_hi[:, q, :], ps4[:, 0:T2], ACT.Copy).then_inc(yah_done, 1)

            for i in range(20):
                k = At(K_IN2 + i)
                hi2(At(C_IN2 + i + 2))
                if i == 0:
                    norm_inv(4)
                if i < 4:
                    act.wait_ge(drained[k.parity], k.half + 1)
                    a(qk_sq[i % 2][:, :, :], qk_r[:, 2 * i:2 * i + 2, :], ACT.Square).then_inc(qksq_done, 1)
                if 1 <= i <= 4:
                    j = i - 1
                    act.wait_ge(qkstat_done, j + 1)
                    if j:
                        act.wait_ge(qkinv_done, j)
                    a(qk_ln[:, :, :].rearrange("p a t -> p (a t)"), (ps5, ps6)[j % 2][:, :], ACT.Ln,
                      bias=eps_t[:, 0:1], scale=1.0 / HD).then_inc(qkln_done, 1)
                    act.wait_ge(qkln_done, j + 1)
                    a(qk_inv[j % 2][:, :, :], qk_ln[:, :, :], ACT.Exp, scale=-0.5,
                      bias=eps_t[:, 2:3] if j < 2 else 0.0).then_inc(qkinv_done, 1)
                if i == 6:
                    act.wait_ge(vT_done, 1)
                    a(v2[:, 0, :], ps7[:, :], ACT.Copy).then_inc(v2_done, 1)
                    a(v2[:, 1, :], ps4[:, :], ACT.Copy).then_inc(v2_done, 1)
                if 6 <= i < 10:
                    j = i - 6
                    act.wait_ge(z_done, j + 1)
                    a(cv2[:, j, :], zc[:, j, 0:T2], ACT.Copy, scale=v(V_CONV2 + 3 * j)).then_inc(cv2_0, 1)
                if 9 <= i < 16 and i % 2:
                    ya_high((i - 9) // 2)
                if 6 <= i < 14:
                    exps2(i - 6)
                if i in (10, 11):
                    j = i - 10
                    act.wait_ge(yb_done, j + 1)
                    a(yb_hi[:, 2 * j:2 * j + 2, :], yb[:, 2 * j:2 * j + 2, :], ACT.Copy).then_inc(ybh_done, 1)
                if i >= 13:
                    gate_sigmoid(i - 13)

            for b in range(4):
                hi(At(C_BR + b + 2).page(0))
                if b < 3:
                    hi(At(C_BR + b + 2).page(1))
                if b == 0:
                    gate_sigmoid(7)
                act.wait_ge(m_done, b + 1)
                a(m_hi[:, 2 * b:2 * b + 2, :], m_a[:, :, :], ACT.Copy).then_inc(mh_done, 1)
                if b == 3:
                    hi(At(C_BR + b + 2).page(1))
            for i in range(4):
                hi2(At(C_WO + 2 + i))
                for kt in (2 * i, 2 * i + 1):
                    norm_hi(5, At(kt))
            mlp(2, 5, C_UP2, K_UP2, C_DN2, True)

        @block.vector
        def _(dve):
            tt, ts, stt = nc.vector.tensor_tensor, nc.vector.tensor_scalar, nc.vector.scalar_tensor_tensor

            def lo(pg, n=PAGE):
                dve.wait_ge(w_hi_done, (pg + 1).value)
                tt(w_lo[pg.slot][:, 0:n], w_raw[pg.slot][:, 0:n], w_hi[pg.slot][:, 0:n].bitcast(F32), ALU.subtract)\
                    .then_inc(w_lo_done[pg.slot], 1)

            def lo2(c):
                lo(c.page(0))
                lo(c.page(1))

            def norm_lo(norm, kt):
                n, tk = width(norm), tokens(norm)
                dve.wait_ge(xh_done, (kt + (KD * norm + 1)).value)
                stt(x_lo[:, kt.value, 0:n], h[:, kt.value, tk], gain(norm, kt.value),
                    x_hi[:, kt.value, 0:n].bitcast(F32), ALU.mult, ALU.subtract).then_inc(xl_done, 1)

            dve.memset(eps_t[:, 0:1], EPS).then_inc(memset_done, 1)
            dve.memset(eps_t[:, 1:2], float(np.log(QK ** -0.5))).then_inc(memset_done, 1)
            dve.memset(eps_t[:, 2:3], float(np.log(HD ** -0.5))).then_inc(memset_done, 1)
            dve.memset(u[:, :, 0:3], 0.0).then_inc(memset_done, 1)
            dve.wait_ge(vec_in, 16)
            for kt in range(KD):
                norm_lo(0, At(kt))
                if kt == 1:
                    lo(Page(0))
            for j in (1, 2, 3):
                lo(Page(j))
            k = At(K_DT)
            r32 = slice(0, 32)
            dve.wait_ge(w_used, 1)
            dve.wait_ge(r_done, 1)
            tt(dtx[:, :], lin[r32, 0, 0:T], r_inv[r32, :], ALU.mult).then_inc(drained[0], 1)
            dve.wait_ge(drained[0], 1)
            ts(dtb[:, :], dtx[:, :], v(V_DTB, rows=r32), None, ALU.add).then_inc(dt_dve, 1)
            dve.wait_ge(dt_dve, 1)
            ts(dtx[:, :], dtb[:, :], -1.0, None, ALU.mult).then_inc(dt_dve, 1)
            dve.wait_ge(dt_dve, 2)
            tt(dta[:, :], dtb[:, :], dtx[:, :], ALU.max).then_inc(dt_dve, 1)
            lo2(At(2))
            dve.wait_ge(dt_act, 3)
            stt(dt_t[:, :], dtb[:, :], 0.0, dta[:, :], ALU.max, ALU.add).then_inc(dt_dve, 1)
            dve.wait_ge(dt_dve, 4)
            ts(dtx[:, :], dt_t[:, :], a_exp[:, 0:1], -1.0, ALU.mult, ALU.mult).then_inc(dt_dve, 1)
            dve.wait_ge(dt_dve, 5)
            dve.wait_ge(const_in, 16)
            nc.vector.tensor_tensor_scan(acs[:, :], cst[r32, N_ONES:N_ONES + 1].broadcast_to([32, T]), dtx[:, :],
                                         0.0, ALU.mult, ALU.add).then_inc(dt_dve, 1)

            def dt_columns():
                dve.wait_ge(dtT_done, 1)
                src = ps4[:, 0:192].rearrange("p (i h) -> p i h", h=32)
                for i, sign in ((0, 1.0), (3, -1.0)):
                    ts(cols[:, i:i + 2, :], src[:, i:i + 2, :], sign, None, ALU.mult).then_inc(cols_done, 1)
                    ts(cols[0:META, i + 2, :], src[0:META, i + 2, :], sign, None, ALU.mult).then_inc(cols_done, 1)

            def evac_u(s, pair):
                c, k = s.times(3, C_GRP + pair), s.times(3, K_GRP + pair)
                dve.wait_ge(w_used, (c + 1).page().value)
                tt(u[:, 2 * pair:2 * pair + 2, 3:3 + T], linp(k, slice(0, T)), over(r_inv[:, :], 2), ALU.mult)\
                    .then_inc(drained[k.parity], 1)

            def conv(s, pair):
                for tap in (1, 2, 3):
                    for i in range(2):
                        q = 2 * pair + i
                        if tap == 1:
                            dve.wait_ge(cv0_done, s.times(4, q + 1).value)
                        else:
                            dve.wait_ge(cv_step, s.times(12, 6 * pair + 2 * (tap - 2) + i + 1).value)
                        stt(cv[:, q, :], u[:, q, tap:tap + T], v(s.times(20, V_CONV + 5 * q + tap).value), cv[:, q, :],
                            ALU.mult, ALU.add).then_inc(cv_step, 1)

            def clamp(dst, x):
                return ts(dst, x, CLAMP, None, ALU.max)

            def silu(s, n, dst, x, sgm):
                dve.wait_ge(sg_step, s.times(6, 3 * (n + 1)).value)
                tt(dst, x, sgm, ALU.mult).then_inc(silu_done, 1)

            def head_mix(g, j):
                h_at = g.times(4, j)
                dve.wait_ge(ee_done, (h_at + 1).value)
                for s, (rows, at, n) in enumerate(((P, 0, T), (P, T, 144), (META, 416, 16))):
                    ins = stt(mm[0:rows, j, at:at + n], dd[g.parity][0:rows, j, at:at + n],
                              cols[0:rows, s, bass.ds(h_at.value, 1)], cbm[0:rows, at:at + n], ALU.mult, ALU.mult)
                ins.then_inc(mm_done, 1)

            def g_low(g):
                for q in range(2):
                    t = g.times(2, q)
                    dve.wait_ge(gh_done, (t + 1).value)
                    stt(g_lo[:, t.value, :], z_s[g.parity][:, q, :], v((t + V_SNORM).value),
                        g_hi[:, t.value, :].bitcast(F32), ALU.mult, ALU.subtract).then_inc(gl_done, 1)

            def slot(s, has_lin=True, has_scan=True, has_stat=True, first=False, has_low=True):
                c = s.times(3, C_GRP)
                g, gs = s + (-1), s + (-2)
                if has_stat:
                    if gs.base:
                        dve.wait_ge(y3_done, gs.value)
                    for q in range(2):
                        dve.wait_ge(y_done, gs.times(2, q + 1).value)
                        stt(y1[:, q, :], xs_s[gs.parity][:, q, :], v(gs.times(2, V_DSKIP + q).value),
                            (ps6, ps7)[q][:, 0:T], ALU.mult, ALU.add).then_inc(y_read, 1)
                if has_scan:
                    silu(g, 1, bc_s[:, :, :], cv[:, 2:4, :], sg[:, 2:4, :])
                if has_low:
                    g_low(gs + (-1))
                    dve.wait_ge(gl_done, gs.times(2).value)
                if has_lin:
                    lo((c + 2).page(0))
                    evac_u(s, 0)
                    conv(s, 0)
                    dve.wait_ge(cv_step, s.times(12, 6).value)
                    clamp(sg[:, 0:2, :], cv[:, 0:2, :]).then_inc(clamped, 1)
                if first:
                    dt_columns()
                if has_scan:
                    if g.base == 0:
                        dve.wait_ge(cols_done, 4)
                    dve.wait_ge(cbm_done, (g + 1).value)
                    for j in range(HPG):
                        head_mix(g, j)
                if has_lin:
                    evac_u(s, 1)
                    lo((c + 3).page(0))
                    silu(s, 0, xs_s[s.parity][:, :, :], cv[:, 0:2, :], sg[:, 0:2, :])
                if has_scan:
                    dve.wait_ge(zg_step, g.times(3, 3).value)
                    tt(z_s[g.parity][:, :, :], z_raw[:, :, :], z_sg[:, :, :], ALU.mult).then_inc(z_silu_done, 1)
                if has_lin:
                    conv(s, 1)
                    dve.wait_ge(cv_step, s.times(12, 12).value)
                    clamp(sg[:, 2:4, :], cv[:, 2:4, :]).then_inc(clamped, 1)
                if not has_lin:
                    lo2(s + (C_SOUT - 6))
                if has_stat:
                    dve.wait_ge(ginv_done, (gs + 1).value)
                    tt(z_s[gs.parity][:, :, :], y2[:, :, :], over(g_inv[:, :], 2), ALU.mult).then_inc(y3_done, 1)
                if has_lin:
                    lo((c + 4).page(0))
                if has_stat and not has_lin:
                    g_low(gs)
                if has_lin:
                    k = s.times(3, K_GRP + 2)
                    dve.wait_ge(w_used, (c + 3).page().value)
                    tt(z_raw[:, :, :], linp(k, slice(0, T)), over(r_inv[:, :], 2), ALU.mult)\
                        .then_inc(drained[k.parity], 1)
                    dve.wait_ge(drained[k.parity], k.half + 1)
                    clamp(z_sg[:, :, :], z_raw[:, :, :]).then_inc(z_clamped, 1)

            slot(At(0), has_scan=False, has_stat=False, first=True, has_low=False)
            slot(At(1), has_stat=False, has_low=False)
            slot(At(2), has_low=False)
            slot(At(3))
            with dve.Fori(1, SLOT_TURNS) as turn:
                for i in range(2):
                    slot(At(2 + i, 2, turn))
            slot(At(8), has_lin=False)
            slot(At(9), has_lin=False, has_scan=False, has_low=False)

            def add_pair(k, used, i, tk):
                dve.wait_ge(w_used, used)
                n = T - tk.start
                tt(h[:, 2 * i:2 * i + 2, tk], h[:, 2 * i:2 * i + 2, tk], linp(k, slice(0, n)), ALU.add)\
                    .then_inc(drained[k.parity], 1)

            for i in range(2, 8):
                lo(At(C_SOUT + 2 + i).page(0))
                if i % 4 >= 2:
                    j = i // 4 * 2 + i % 2
                    add_pair(At(K_SOUT + j), 2 * (C_SOUT + i + 1), j, slice(0, T))
                lo(At(C_SOUT + 2 + i).page(1))
                if i % 4 >= 2:
                    for kt in (2 * j, 2 * j + 1):
                        norm_lo(1, At(kt))

            def mlp(m, norm, c_up, c_dn, k_dn, last):
                n, tk = width(norm), tokens(norm)

                def up(i, t):
                    lo2(t + (c_up + 2))
                    k = t + (K_UP0, K_UP1, K_UP2)[m]
                    dve.wait_ge(drained[k.parity], k.half + 1)
                    tt(relu_sq[i][:, :, 0:n], relu[i][:, :, 0:n], relu[i][:, :, 0:n], ALU.mult).then_inc(rsq_done, 1)
                    dve.wait_ge(hh_done, (t + (16 * m + 1)).value)
                    dve.wait_ge(rsq_done, (t + (16 * m + 1)).value)
                    at = t.times(2)
                    tt(hid_lo[:, bass.ds(at.value, 2), 0:n], relu_sq[i][:, :, 0:n],
                       hid_hi[:, bass.ds(at.value, 2), 0:n].bitcast(F32), ALU.subtract).then_inc(hl_done, 1)

                with dve.Fori(0, 8) as turn:
                    for i in range(2):
                        up(i, At(i, 2, turn))

                def down(i, t, lows=True):
                    if lows:
                        lo2(t.times(2, c_dn + 2))
                        lo2(t.times(2, c_dn + 3))
                    k = t + k_dn
                    dve.wait_ge(w_used, t.times(2, c_dn + 2).page().value)
                    tt(down_r[i][:, 0:n], lin[:, 2 * k.parity, 0:n], r_inv[:, 0:n], ALU.mult)\
                        .then_inc(drained[k.parity], 1)
                    dve.wait_ge(drained[k.parity], k.half + 1)
                    tt(h[:, t.value, tk], h[:, t.value, tk], down_r[i][:, 0:n], ALU.add).then_inc(h_mlp, 1)
                    if not last:
                        norm_lo(norm + 1, t)

                dve.wait_ge(r_done, norm + 1)
                with dve.Fori(0, 3) as turn:
                    for i in range(2):
                        down(i, At(i, 2, turn))
                down(0, At(6))
                down(1, At(7), not last)

            mlp(0, 1, C_UP0, C_DN0, K_DN0, False)

            def latents(i):
                k = At(K_MIN + i)
                lo(At(C_MIN + 2 + i).page(0), (8, 6, 4)[i] * P)
                dve.wait_ge(w_used, 2 * (C_MIN + i + 1))
                dve.wait_ge(r_done, 3)
                tt(lat[:, 2 * i:2 * i + 2, :], linp(k, slice(0, T)), over(r_inv[:, :], 2), ALU.mult)\
                    .then_inc(drained[k.parity], 1)

            def latent_norm(i, tiles):
                dve.wait_ge(l_act, 2 * i + 2)
                each = slice(tiles[0], tiles[-1] + 1)
                tt(lat_n[:, each, :], lat[:, each, :], over(l_inv[:, i, :], len(tiles)), ALU.mult)\
                    .then_inc(latn_done, 1)
                dve.wait_ge(latn_done, i + 1)
                for q in tiles:
                    dve.wait_ge(lh_done, q + 1)
                    stt(l_lo[:, q, :], lat_n[:, q, :], v(V_QA + q), l_hi[:, q, :].bitcast(F32),
                        ALU.mult, ALU.subtract).then_inc(ll_done, 1)

            latents(0)
            lo(At(C_MIN + 2).page(1))
            latents(1)
            lo(At(C_MIN + 3).page(1), 6 * P)
            latent_norm(0, range(3))
            latents(2)
            lo(At(C_MIN + 4).page(1), 4 * P)
            latent_norm(1, range(3, 5))
            k = At(K_MIN + 2)
            dve.wait_ge(drained[k.parity], k.half + 1)
            dve.wait_ge(rope_done, 2)
            rr, rs_ = slice(HD, QK), slice(QK, P)
            tt(rot_a[rr, 0, :], lat[rr, 5, :], rope_k[rr, :], ALU.mult).then_inc(krope, 1)
            tt(rot_b[rr, 0, :], lat[rs_, 5, :], rope_k[rs_, :], ALU.mult).then_inc(krope, 1)
            dve.wait_ge(krope, 2)
            tt(k_pre[rr, :, :], over(rot_a[rr, 0, :], 4), over(rot_b[rr, 0, :], 4), ALU.add).then_inc(krope, 1)
            tt(k_sq[rr, :, :], over(lat[rr, 5, :], 4), over(lat[rr, 5, :], 4), ALU.mult).then_inc(krope, 1)

            def rotate(t):
                s, n = t // 4, t % 4
                k = At(K_HEAD + t)
                un = 2 * s + n
                dve.wait_ge(qsq_read, un + 1)
                tq = slice(META, T)
                if un:
                    dve.wait_ge(rot_sum, un)
                else:
                    dve.wait_ge(krope, 3)
                both = slice(HD, P)
                tt(rot_a[both, :, 0:T2], linp(k, slice(0, T2), both), over(rope_q[both, tq], 2), ALU.mult)\
                    .then_inc(rot_done, 1)

            def rotate_sum(t):
                s, n = t // 4, t % 4
                un = 2 * s + n
                dve.wait_ge(rot_done, 2 * un + 1)
                nc.vector.tensor_copy(rot_b[rr, :, 0:T2], rot_a[rs_, :, 0:T2]).then_inc(rot_done, 1)
                dve.wait_ge(rot_done, 2 * un + 2)
                tt(q_pre[rr, 2 * n:2 * n + 2, :], rot_a[rr, :, 0:T2], rot_b[rr, :, 0:T2], ALU.add).then_inc(rot_sum, 1)

            def keys(t):
                s, n = t // 4, t % 4
                un = 2 * s + n - 2
                k = At(K_HEAD + t)
                dve.wait_ge(ksq_read, un + 1)
                if s:
                    dve.wait_ge(fin_done, t - 3)
                ts(k_pre[0:HD, 2 * (n - 2):2 * (n - 2) + 2, :], linp(k, slice(0, T), slice(0, HD)),
                   v(V_KG, rows=slice(0, HD)), None, ALU.mult).then_inc(kpre_done, 1)

            def finish(un):
                s, n = un // 4, un % 4
                dve.wait_ge(ninv_done, un + 1)
                hs = slice(2 * (n % 2), 2 * (n % 2) + 2)
                if n < 2:
                    dve.wait_ge(rot_sum, 2 * s + n + 1)
                    ins = tt(q_fin[s % 2][:, hs, :], q_pre[:, hs, :], n_inv[:, :, 0:T2], ALU.mult)
                else:
                    dve.wait_ge(kpre_done, 2 * s + n - 1)
                    if s == 0:
                        dve.wait_ge(krope, 3)
                    ins = tt(k_fin[s % 2][:, hs, :], k_pre[:, hs, :], n_inv[:, :, :], ALU.mult)
                ins.then_inc(fin_done, 1)

            def maxima(n):
                p, o = n % 2, (ps5, ps6)[n % 2]
                dve.wait_ge(s_done, n + 1)
                for i, sl in enumerate((slice(0, 144), slice(144, 416))):
                    ins = nc.vector.tensor_tensor_reduce(
                        out=s_m[p][:, sl], in0=o[:, sl], in1=cst[:, N_MLA + sl.start:N_MLA + sl.stop], scale=1.0,
                        scalar=-3e38, op0=ALU.add, op1=ALU.max, accum_out=mx[p][:, i:i + 1])
                ins.then_inc(sm_done, 1)
                dve.wait_ge(sm_done, n + 1)
                ts(nmx[p][:, :], mx[p][:, :], -1.0, None, ALU.mult).then_inc(nm_done, 1)

            def weigh(n):
                p = n % 2
                dve.wait_ge(ex_done, n + 1)
                nc.vector.reciprocal(rinv[p][:, :], rsum[p][:, :]).then_inc(ri_done, 1)
                dve.wait_ge(ri_done, n + 1)
                ts(pr[p][:, 0:144], pr[p][:, 0:144], rinv[p][:, 0:1], None, ALU.mult)
                ts(pr[p][:, 144:416], pr[p][:, 144:416], rinv[p][:, 1:2], None, ALU.mult).then_inc(p_done, 1)

            def p_t_copy(n):
                dve.wait_ge(pT_done, n + 1)
                nc.vector.tensor_copy(p_t[:, :], ps7[:, 0:384]).then_inc(pt_done, 1)

            def o_low(n):
                dve.wait_ge(oh_done, n + 1)
                tt(o_lo[:, n, :], ps4[:, 0:T2], o_hi[:, n, :].bitcast(F32), ALU.subtract).then_inc(ol_done, 1)

            for t in range(MLA_STEPS + 1):
                if 0 <= t - 6 < 16:
                    maxima(t - 6)
                if t >= 10 and t % 2 == 0:
                    o_low((t - 10) // 2)
                if 1 <= t <= 16:
                    finish(t - 1)
                if t < 16:
                    (rotate, keys)[t % 4 // 2](t)
                if 8 <= t < MLA_STEPS:
                    p_t_copy(t - 8)
                if t < 16 and t % 4 < 2:
                    rotate_sum(t)
                if 0 <= t - 6 < 16:
                    weigh(t - 6)

            for i in range(4):
                lo(At(C_MOUT + 2 + i).page(0))
                if i != 1:
                    add_pair(At(K_MOUT + i), 2 * (C_MOUT + i + 1), i, slice(META, T))
                lo(At(C_MOUT + 2 + i).page(1))
                if i == 0:
                    add_pair(At(K_MOUT + 1), 2 * (C_MOUT + 2), 1, slice(META, T))
                for kt in ((), range(4), (4, 5), (6, 7))[i]:
                    norm_lo(3, At(kt))
            mlp(1, 3, C_UP1, C_DN1, K_DN1, False)

            def maxima2(n):
                p, o = n % 2, (ps5, ps6)[n % 2]
                dve.wait_ge(s2_done, n + 1)
                if n == 0:
                    dve.wait_ge(bias_done, 16)
                for qt in range(2):
                    sl = slice(qt * 256, (qt + 1) * 256)
                    ins = nc.vector.tensor_tensor_reduce(
                        out=s_m2[p][:, sl], in0=o[:, sl], in1=bias_mask[:, n, qt, :], scale=1.0,
                        scalar=-3e38, op0=ALU.add, op1=ALU.max, accum_out=mx2[p][:, qt:qt + 1])
                ins.then_inc(sm2_done, 1)
                dve.wait_ge(sm2_done, n + 1)
                ts(nmx2[p][:, :], mx2[p][:, :], -1.0, None, ALU.mult).then_inc(nm2_done, 1)

            def weigh2(n):
                p = n % 2
                dve.wait_ge(ex2_done, n + 1)
                nc.vector.reciprocal(rinv2[p][:, :], rsum2[p][:, :]).then_inc(ri2_done, 1)
                dve.wait_ge(ri2_done, n + 1)
                for qt in range(2):
                    sl = slice(qt * 256, (qt + 1) * 256)
                    ins = ts(pr2[p][:, sl], pr2[p][:, sl], rinv2[p][:, qt:qt + 1], None, ALU.mult)
                ins.then_inc(p2_done, 1)

            for i in range(20):
                c, k = At(C_IN2 + i), At(K_IN2 + i)
                if 8 <= i < 16:
                    dve.wait_ge(pT2_done, i - 7)
                    nc.vector.tensor_copy(p_t2[:, :], ps7[:, :]).then_inc(pt2_done, 1)
                lo((c + 2).page(0))
                dve.wait_ge(w_used, (c + 1).page().value)
                if i == 0:
                    dve.wait_ge(r_done, 5)
                if i < 4:
                    dst = qk_r[:, 2 * i:2 * i + 2, :]
                elif i < 6:
                    dst = v_r[:, 2 * (i - 4):2 * (i - 4) + 2, :]
                elif i < 10:
                    dst = cc_ch[:, :, :]
                elif i < 12:
                    dst = cb_r[:, 2 * (i - 10):2 * (i - 10) + 2, :]
                else:
                    dst = gate[:, 2 * (i - 12):2 * (i - 12) + 2, :]
                tt(dst, linp(k, slice(0, T2)), over(r_inv[:, 0:T2], 2), ALU.mult).then_inc(drained[k.parity], 1)
                lo((c + 2).page(1))
                if i == 0:
                    dve.memset(zc[:, :, 0:1], 0.0)
                    dve.memset(zc[:, :, T2 + 1:T2 + 2], 0.0)
                if 1 <= i <= 4:
                    j = i - 1
                    dve.wait_ge(qkinv_done, j + 1)
                    for q in range(2):
                        ins = stt(qk_f[:, 2 * j + q, :], qk_r[:, 2 * j + q, :], v(V_QN2 if j < 2 else V_KN2),
                                  qk_inv[j % 2][:, q, :], ALU.mult, ALU.mult)
                    ins.then_inc(qkf_done, 1)
                if 6 <= i < 10:
                    j = i - 6
                    dve.wait_ge(drained[k.parity], k.half + 1)
                    tt(zc[:, j, 1:T2 + 1], cc_ch[:, 0, :], cc_ch[:, 1, :], ALU.mult).then_inc(z_done, 1)
                if 9 <= i < 16 and i % 2:
                    q = (i - 9) // 2
                    dve.wait_ge(yah_done, q + 1)
                    tt(ya_lo[:, q, :], ps4[:, 0:T2], ya_hi[:, q, :].bitcast(F32), ALU.subtract).then_inc(yal_done, 1)
                if 6 <= i < 14:
                    maxima2(i - 6)
                if 6 <= i < 10:
                    j = i - 6
                    for tap in (1, 2):
                        if tap == 1:
                            dve.wait_ge(cv2_0, j + 1)
                            dve.wait_ge(z_done, j + 1)
                        else:
                            dve.wait_ge(cv2_step, 2 * j + 1)
                        stt(cv2[:, j, :], zc[:, j, tap:tap + T2], v(V_CONV2 + 3 * j + tap), cv2[:, j, :],
                            ALU.mult, ALU.add).then_inc(cv2_step, 1)
                if 6 <= i < 14:
                    weigh2(i - 6)
                if i in (10, 11):
                    j = i - 10
                    dve.wait_ge(drained[k.parity], k.half + 1)
                    dve.wait_ge(cv2_step, 8)
                    tt(yb[:, 2 * j:2 * j + 2, :], cv2[:, 2 * j:2 * j + 2, :], cb_r[:, 2 * j:2 * j + 2, :], ALU.mult)\
                        .then_inc(yb_done, 1)
                    dve.wait_ge(ybh_done, j + 1)
                    dve.wait_ge(yb_done, j + 1)
                    tt(yb_lo[:, 2 * j:2 * j + 2, :], yb[:, 2 * j:2 * j + 2, :],
                       yb_hi[:, 2 * j:2 * j + 2, :].bitcast(F32), ALU.subtract).then_inc(ybl_done, 1)

            for b in range(4):
                c = At(C_BR + b)
                for n, dst in enumerate((m_a, m_b)):
                    k = At(K_BR + 2 * b + n)
                    dve.wait_ge(w_used, c.page(n + 1).value)
                    dve.wait_ge(gate_step, min(24, 3 * (2 * b + 2)))
                    if n == 0 and b:
                        dve.wait_ge(ml_done, b)
                    tt(dst[:, :, :], linp(k, slice(0, T2)), gate[:, 4 * b + n:4 * b + n + 3:2, :], ALU.mult)\
                        .then_inc(drained[k.parity], 1)
                    if n == 0:
                        lo((c + 2).page(0))
                for n in range(2):
                    k = At(K_BR + 2 * b + n)
                    dve.wait_ge(drained[k.parity], k.half + 1)
                tt(m_a[:, :, :], m_a[:, :, :], m_b[:, :, :], ALU.add).then_inc(m_done, 1)
                if b < 3:
                    lo((c + 2).page(1))
                dve.wait_ge(m_done, b + 1)
                dve.wait_ge(mh_done, b + 1)
                tt(m_lo[:, 2 * b:2 * b + 2, :], m_a[:, :, :], m_hi[:, 2 * b:2 * b + 2, :].bitcast(F32),
                   ALU.subtract).then_inc(ml_done, 1)
                if b == 3:
                    lo((c + 2).page(1))
            for i in range(4):
                lo(At(C_WO + 2 + i).page(0))
                add_pair(At(K_WO + i), 2 * (C_WO + i + 1), i, slice(META, T))
                lo(At(C_WO + 2 + i).page(1))
                for kt in (2 * i, 2 * i + 1):
                    norm_lo(5, At(kt))
            mlp(2, 5, C_UP2, C_DN2, K_DN2, True)

        @block.gpsimd
        def _(pool):
            tt, ts = nc.gpsimd.tensor_tensor, nc.gpsimd.tensor_scalar

            def norm_sum(norm):
                n = width(norm)
                for kt in range(1, KD):
                    pool.wait_ge(hsq_done, KD * norm + kt + 1)
                    if kt > 1:
                        pool.wait_ge(hsum_done, (KD - 1) * norm + kt - 1)
                    tt(h_sq[:, 0, 0:n], h_sq[:, 0, 0:n], h_sq[:, kt, 0:n], ALU.add).then_inc(hsum_done, 1)

            norm_sum(0)
            pool.wait_ge(dt_dve, 6)
            pool.dma_start(acs_dram, acs[:, :]).then_inc(acs_out, 16)
            pool.wait_ge(acs_out, 16)

            pool.wait_ge(const_in, 16)

            def lo(pg, n=PAGE):
                pool.wait_ge(w_hi_done, (pg + 1).value)
                tt(w_lo[pg.slot][:, 0:n], w_raw[pg.slot][:, 0:n], w_hi[pg.slot][:, 0:n].bitcast(F32), ALU.subtract)\
                    .then_inc(w_lo_done[pg.slot], 1)

            def acs_rows(g):
                if g.base:
                    pool.wait_ge(dd_done, g.times(2).value)
                src = acs_dram[bass.ds(g.times(4).value, 4), :].partition_broadcast(P)
                pool.dma_start(acs_bc[:, :, :], src).then_inc(acs_in, 16)

            def masked_rows(g, half):
                hs = slice(2 * half, 2 * half + 2)
                d = dd[g.parity]
                if half == 0:
                    pool.wait_ge(acs_in, (g + 1).times(16).value)
                    if g.base >= 2:
                        pool.wait_ge(mm_done, g.times(4, -4).value)
                for rows, at, n, l0 in ((P, 0, T, 0), (P, T, 144, 128), (META, 416, 16, 256)):
                    ins = tt(d[0:rows, hs, at:at + n], acs_bc[0:rows, hs, l0:T],
                             over(cst[0:rows, N_SSD + at:N_SSD + at + n], 2), ALU.add)
                ins.then_inc(dd_done, 1)

            def slot(s, has_lin=True, has_stat=True, load=True):
                c, gs = s.times(3, C_GRP), s + (-2)
                if has_stat:
                    pool.wait_ge(y_read, gs.times(2, 2).value)
                    pool.wait_ge(z_silu_done, (gs + 1).value)
                    if gs.base:
                        pool.wait_ge(y3_done, gs.value)
                    tt(y2[:, :, :], y1[:, :, :], z_s[gs.parity][:, :, :], ALU.mult).then_inc(y2_done, 1)
                    pool.wait_ge(ysq_done, (gs + 1).value)
                    tt(y_sum[:, :], h_sq[:, 0, :], h_sq[:, 1, :], ALU.add).then_inc(ysum_done, 1)
                if has_lin:
                    lo((c + 2).page(1))
                    masked_rows(s, 0)
                    lo((c + 3).page(1))
                    masked_rows(s, 1)
                    if load:
                        acs_rows(s + 1)
                    lo((c + 4).page(1))

            acs_rows(At(0))
            slot(At(0), has_stat=False)
            slot(At(1), has_stat=False)
            with pool.Fori(0, 2) as turn:
                for i in range(2):
                    slot(At(2 + i, 2, turn))
            slot(At(6))
            slot(At(7), load=False)
            slot(At(8), has_lin=False)
            slot(At(9), has_lin=False)

            for rq in range(4):
                pool.dma_start(bias_mask[(rq % 2) * 64:(rq % 2 + 1) * 64, :, rq // 2, :], rpb[:, :, 3 - rq:7 - rq, :]
                               .rearrange("q h r c -> q h (r c)")).then_inc(rpb_in, 16)
            norm_sum(1)
            pool.wait_ge(rpb_in, 16 * 4)
            pool.wait_ge(const_in, 16)
            for hd in range(NA_HEADS):
                for qt in range(2):
                    b = bias_mask[:, hd, qt, :].rearrange("p (r c) -> p r c", c=64)
                    tt(b, b, over(cst[:, N_NA:N_NA + 64], 4), ALU.add).then_inc(bias_done, 1)
            norm_sum(2)
            pool.wait_ge(stat_done, 3)
            tb = slice(HD, P)
            ts(rope_q[tb, :], cst[tb, N_ROPE:N_ROPE + T], v(V_QG, rows=tb), None, ALU.mult).then_inc(rope_done, 1)
            ts(rope_k[tb, :], cst[tb, N_ROPE:N_ROPE + T], v(V_KG, rows=tb), None, ALU.mult).then_inc(rope_done, 1)
            for nxt in range(4, 20):
                lo(At(C_HEAD).page(nxt), PAGE if nxt >= 16 else (6 if nxt % 4 < 2 else 4) * P)
            norm_sum(3)
            norm_sum(4)
            for j in range(8):
                k = At(K_IN2 + 12 + j)
                pool.wait_ge(drained[k.parity], k.half + 1)
                gt = gate[:, 2 * j:2 * j + 2, :]
                ts(gt, gt, CLAMP, None, ALU.max).then_inc(gclamp, 1)
            norm_sum(5)


def constants():
    c = np.zeros((P, N_CONST), np.float32)
    p = np.arange(P)
    c[:, N_IDENT:N_IDENT + P] = np.eye(P)
    c[:, N_ONES:N_ONES + P] = 1.0
    c[:, N_BLK:N_BLK + P] = (p[:, None] // HD) == (p[None, :] // HD)
    tok = np.arange(T)
    c[:, N_SSD:N_SSD + T] = np.where(tok[None, :] >= p[:, None], 0.0, NEG)
    c[:, N_SSD + T:N_SSD + 416] = np.where(tok[None, 128:] >= 128 + p[:, None], 0.0, NEG)
    c[:META, N_SSD + 416:N_SSD + 432] = np.where(tok[None, 256:] >= 256 + p[:META, None], 0.0, NEG)
    c[:, N_MLA:N_MLA + 144] = np.where(tok[None, :144] <= META + p[:, None], 0.0, NEG)
    c[:, N_MLA + 144:N_MLA + 416] = np.where(tok[None, :] <= 144 + p[:, None], 0.0, NEG)
    inv = (1.0 / (np.float32(10000.0) ** (np.arange(0, 32, 2, dtype=np.float32) / np.float32(32)))).astype(np.float32)
    ang = (tok.astype(np.float32)[None, :] * inv[:, None]).astype(np.float32)
    cos, sin = np.cos(ang), np.sin(ang)
    c[HD:QK, N_ROPE:N_ROPE + T] = np.concatenate([cos, cos])
    c[QK:P, N_ROPE:N_ROPE + T] = np.concatenate([-sin, sin])
    qc, kc = (p % 64)[:, None], np.arange(64)[None, :]
    start = np.clip(qc - 8, 0, 48)
    c[:, N_NA:N_NA + 64] = np.where((kc >= start) & (kc < start + 16), 0.0, NEG)
    return c


def page(m):
    kt, ct = m.shape[0] // P, m.shape[1] // P
    row = m.reshape(kt, P, ct, P).transpose(1, 2, 0, 3).reshape(P, -1)
    return np.pad(row, ((0, 0), (0, PAGE - row.shape[1])))


def pad_cols(m, before, after):
    return np.pad(m, ((0, 0), (before, after)))


def weight_stream(i):
    w = []

    def wide(m):
        for t in range(0, m.shape[1], P):
            w.append(page(m[:, t:t + P]))

    s = i["ssd_w_in"][0]
    z, xs, b, c, dt = s[:, 0:2048], s[:, 2048:4096], s[:, 4096:5120], s[:, 5120:6144], s[:, 6144:6176]
    wide(pad_cols(dt, 0, 224))
    for g in range(GROUPS):
        wide(xs[:, 256 * g:256 * g + 256])
        wide(b[:, P * g:P * g + P])
        wide(c[:, P * g:P * g + P])
        wide(z[:, 256 * g:256 * g + 256])
    for r in range(2):
        for half in range(2):
            wide(i["ssd_w_out"][0][D * half:D * half + D, 512 * r:512 * r + 512])

    def mlp(up, down):
        wide(up)
        for t in range(8):
            for q in range(4):
                wide(down[D * q:D * q + D, P * t:P * t + P])

    mlp(i["mlp_w_up"][0], i["mlp_w_down"][0])
    m = i["mla_w_in"][0]
    kpe = m[:, 640:672]
    wide(np.concatenate([m[:, 0:640], pad_cols(kpe, 64, 0), kpe[:, 16:32], kpe[:, 0:16]], 1))
    q = i["mla_w_q_b"][0].reshape(384, MLA_HEADS, QK)
    q = np.concatenate([q, q[:, :, 80:96], q[:, :, 64:80]], 2).reshape(384, MLA_HEADS * P)
    for s4 in range(4):
        for m in (q, i["mla_w_kv_b"][0]):
            for half in range(2):
                w.append(page(m[:, 512 * s4 + 256 * half:512 * s4 + 256 * half + 256]))
    wide(i["mla_w_out"][0])
    mlp(i["mlp_w_up"][1], i["mlp_w_down"][1])
    n = i["w_in_2"][0]
    wide(n[:, 0:1536])
    cb, cc, ch, ga, gb = n[:, 1536:2048], n[:, 2048:2560], n[:, 2560:3072], n[:, 3072:4096], n[:, 4096:5120]
    for t in range(0, 512, P):
        wide(cc[:, t:t + P])
        wide(ch[:, t:t + P])
    wide(cb)
    for t in range(0, 1024, P):
        wide(ga[:, t:t + P])
        wide(gb[:, t:t + P])
    for t in range(0, 1024, 256):
        w.append(page(i["w_attn_branch_2"][0][:, t:t + 256]))
        w.append(page(i["w_conv_branch_2"][0][:, t:t + 256]))
    wide(i["w_o_2"][0])
    mlp(i["w_mlp_in_2"][0], i["w_mlp_out_2"][0])
    assert len(w) == N_PAGES
    return np.stack(w)


def small_params(i):
    vec = np.zeros((P, N_VEC), np.float32)

    def tiles(x):
        return x.reshape(-1, P).T

    gains = (i["ln_mix"][0], i["ln_mlp"][0], i["ln_mix"][1], i["ln_mlp"][1], i["norm1_g_2"][0], i["norm2_g_2"][0])
    for n, g in enumerate(gains):
        vec[:, V_GAIN + n * KD:V_GAIN + (n + 1) * KD] = tiles(g)
    cw, cb = i["ssd_conv_w"][0], i["ssd_conv_b"][0]
    for g in range(GROUPS):
        for q, t in enumerate((2 * g, 2 * g + 1, 16 + g, 24 + g)):
            at = V_CONV + (g * 4 + q) * 5
            vec[:, at:at + 4] = cw[:, P * t:P * t + P].T
            vec[:, at + 4] = cb[P * t:P * t + P]
    vec[:, V_DSKIP:V_DSKIP + 16] = tiles(np.repeat(i["ssd_d"][0], HD))
    vec[:, V_SNORM:V_SNORM + 16] = tiles(i["ssd_norm"][0])
    vec[:, V_QA:V_QA + 3] = tiles(i["mla_q_a_norm"][0])
    vec[:, V_KVA:V_KVA + 2] = tiles(i["mla_kv_a_norm"][0])
    for col, g in ((V_QG, i["mla_q_norm"][0]), (V_KG, i["mla_k_norm"][0])):
        vec[:, col] = np.concatenate([g, g[80:96], g[64:80]])
    for t in range(4):
        vec[:, V_CONV2 + 3 * t:V_CONV2 + 3 * t + 3] = i["conv_w_2"][0][:, P * t:P * t + P].T
    vec[:, V_QN2] = np.tile(i["q_norm_g_2"][0], 2)
    vec[:, V_KN2] = np.tile(i["k_norm_g_2"][0], 2)
    vec[0:32, V_DTB] = i["ssd_dt_bias"][0]
    vec[0:32, V_ALOG] = i["ssd_a_log"][0]
    return vec


def kernel(**inputs):
    import concourse.bacc as bacc
    from concourse.bass_utils import run_bass_kernel_spmd

    i = {name: np.asarray(a) for name, a in inputs.items()}
    tokens = np.concatenate([i["meta_tokens"], i["x"][0]], axis=0)
    padded = np.pad(i["rpb_2"][0][:, 4:11, :], ((0, 0), (0, 0), (48, 48)))
    rpb = np.stack([padded[:, :, 63 - qc:127 - qc] for qc in range(64)])
    arrays = {
        "w": weight_stream(i),
        "h0": np.ascontiguousarray(tokens.T.reshape(KD, P, T).transpose(1, 0, 2)),
        "vec": small_params(i),
        "const": constants(),
        "rpb": np.ascontiguousarray(rpb),
    }
    nc = bacc.Bacc("TRN2", target_bir_lowering=False, num_devices=1)
    aps = {n: nc.dram_tensor(n, a.shape, mybir.dt.from_np(a.dtype), kind="ExternalInput").ap()
           for n, a in arrays.items()}
    out = nc.dram_tensor("out", (P, KD, SEQ), F32, kind="ExternalOutput").ap()
    acs_dram = nc.dram_tensor("acs_dram", (32, T), F32, kind="Internal").ap()
    build(nc, aps["w"], aps["h0"], aps["vec"], aps["const"], aps["rpb"], out, acs_dram)
    r = run_bass_kernel_spmd(nc, [arrays], core_ids=[0])
    o = r.results[0]["out"]
    return np.ascontiguousarray(o.transpose(1, 0, 2).reshape(D, SEQ).T)[None]
```
